# Optimizing a Trainium2 kernel written in Bass

```python
import jax, jax.numpy as jnp
from jax import lax
import numpy as np
import math

D_MODEL = 1024
BATCH = 1
SEQ = 256
DEPTH = 1

CHUNK = 64
D_CONV = 512
CONV_WIDTH = 31
N_HEADS = 8
HEAD_DIM = 64
D_ATTN = N_HEADS * HEAD_DIM
D_MIX = D_CONV + D_ATTN
Q_BLOCK = 128
D_FF = 2816
EPS = 1e-6
N_IN = 2 * D_CONV + 3 * D_ATTN + N_HEADS


def rms_norm(x, g):
    xf = x.astype(jnp.float32)
    y = xf * lax.rsqrt(jnp.mean(xf * xf, axis=-1, keepdims=True) + EPS)
    return (y * g.astype(jnp.float32)).astype(x.dtype)

def layer_norm(x, g, b):
    xf = x.astype(jnp.float32)
    mu = jnp.mean(xf, axis=-1, keepdims=True)
    xc = xf - mu
    y = xc * lax.rsqrt(jnp.mean(xc * xc, axis=-1, keepdims=True) + EPS)
    return (y * g.astype(jnp.float32) + b.astype(jnp.float32)).astype(x.dtype)

def swiglu_ffn(h, w13, w2):
    gate, up = jnp.split(h @ w13, 2, axis=-1)
    return (jax.nn.silu(gate) * up) @ w2

def conv_module(a, g, conv_w, conv_b, ln_g, ln_b):
    u = a * jax.nn.sigmoid(g)
    u_pad = jnp.pad(u, ((0, 0), (CONV_WIDTH - 1, 0), (0, 0)))
    y = lax.conv_general_dilated(
        u_pad, conv_w[:, None, :].astype(u.dtype), window_strides=(1,), padding="VALID",
        dimension_numbers=("NWC", "WIO", "NWC"), feature_group_count=D_CONV)
    y = y + conv_b.astype(y.dtype)
    y = layer_norm(y, ln_g, ln_b)
    return jax.nn.silu(y)

def forgetting_attention(q, k, v, f_logit):
    seq = q.shape[1]
    log_f = jax.nn.log_sigmoid(f_logit.astype(jnp.float32))
    cum = jnp.cumsum(log_f, axis=1).transpose(0, 2, 1)
    scale = HEAD_DIM ** -0.5
    outs = []
    for i in range(seq // Q_BLOCK):
        q0, q1 = i * Q_BLOCK, (i + 1) * Q_BLOCK
        qb, kb, vb = q[:, q0:q1], k[:, :q1], v[:, :q1]
        s = jnp.einsum("bqhd,bkhd->bhqk", qb, kb, preferred_element_type=jnp.float32) * scale
        s = s + cum[:, :, q0:q1, None] - cum[:, :, None, :q1]
        qpos = jnp.arange(q0, q1)
        kpos = jnp.arange(q1)
        s = jnp.where(kpos[None, :] <= qpos[:, None], s, -jnp.inf)
        p = jax.nn.softmax(s, axis=-1)
        outs.append(jnp.einsum("bhqk,bkhd->bqhd", p.astype(vb.dtype), vb))
    return jnp.concatenate(outs, axis=1)

def first_inputs(seed: int = 0) -> dict:
    key = jax.random.key(seed)
    ks = jax.random.split(key, 24)
    f32 = jnp.float32

    def nrm(k, shape, scale):
        return jax.random.normal(k, shape, f32) * scale

    def gain(k, shape):
        return 1.0 + 0.05 * jax.random.normal(k, shape, f32)

    L = DEPTH
    return {
        "x": jax.random.normal(ks[0], (BATCH, SEQ, D_MODEL), f32),
        "ffn1_norm": gain(ks[1], (L, D_MODEL)),
        "ffn1_w13": nrm(ks[2], (L, D_MODEL, 2 * D_FF), D_MODEL ** -0.5),
        "ffn1_w2": nrm(ks[3], (L, D_FF, D_MODEL), D_FF ** -0.5),
        "mix_norm": gain(ks[4], (L, D_MODEL)),
        "w_in": nrm(ks[5], (L, D_MODEL, N_IN), D_MODEL ** -0.5),
        "conv_w": nrm(ks[6], (L, CONV_WIDTH, D_CONV), CONV_WIDTH ** -0.5),
        "conv_b": nrm(ks[7], (L, D_CONV), 0.02),
        "conv_ln_g": gain(ks[8], (L, D_CONV)),
        "conv_ln_b": nrm(ks[9], (L, D_CONV), 0.02),
        "forget_b": jax.random.uniform(ks[10], (L, N_HEADS), f32, minval=1.0, maxval=4.0),
        "out_norm_conv": gain(ks[11], (L, D_CONV)),
        "out_norm_attn": gain(ks[12], (L, D_ATTN)),
        "w_out": nrm(ks[13], (L, D_MIX, D_MODEL), D_MIX ** -0.5),
        "ffn2_norm": gain(ks[14], (L, D_MODEL)),
        "ffn2_w13": nrm(ks[15], (L, D_MODEL, 2 * D_FF), D_MODEL ** -0.5),
        "ffn2_w2": nrm(ks[16], (L, D_FF, D_MODEL), D_FF ** -0.5),
        "final_norm": gain(ks[17], (D_MODEL,)),
    }

def first_block(x, ffn1_norm, ffn1_w13, ffn1_w2, mix_norm, w_in, conv_w, conv_b, conv_ln_g,
              conv_ln_b, forget_b, out_norm_conv, out_norm_attn, w_out, ffn2_norm, ffn2_w13,
              ffn2_w2, final_norm):
    bsz, seq, _ = x.shape
    splits = [D_CONV, 2 * D_CONV, 2 * D_CONV + D_ATTN, 2 * D_CONV + 2 * D_ATTN,
              2 * D_CONV + 3 * D_ATTN]
    for l in range(DEPTH):
        x = x + 0.5 * swiglu_ffn(rms_norm(x, ffn1_norm[l]), ffn1_w13[l], ffn1_w2[l])

        h = rms_norm(x, mix_norm[l])
        proj = h @ w_in[l]
        a, g, q, k, v, fl = jnp.split(proj, splits, axis=-1)

        y_conv = conv_module(a, g, conv_w[l], conv_b[l], conv_ln_g[l], conv_ln_b[l])

        heads = (bsz, seq, N_HEADS, HEAD_DIM)
        y_attn = forgetting_attention(q.reshape(heads), k.reshape(heads), v.reshape(heads),
                                      fl + forget_b[l].astype(fl.dtype))
        y_attn = y_attn.reshape(bsz, seq, D_ATTN)

        y = jnp.concatenate([rms_norm(y_conv, out_norm_conv[l]),
                             rms_norm(y_attn, out_norm_attn[l])], axis=-1)
        x = x + y @ w_out[l]

        x = x + 0.5 * swiglu_ffn(rms_norm(x, ffn2_norm[l]), ffn2_w13[l], ffn2_w2[l])
    return rms_norm(x, final_norm)


DEPTH_2 = 2

PLE_DIM = 256
N_A_LAYERS = DEPTH_2 // 2
N_B_LAYERS = DEPTH_2 - N_A_LAYERS
GDN_HEADS = 8
GDN_HEAD_DIM = 128
GDN_WIDTH = GDN_HEADS * GDN_HEAD_DIM
CONV_WIDTH_2 = 4
GDN_CHUNK = 64
SB_HEADS = 8
SB_HEAD_DIM = 128
SB_WIDTH = SB_HEADS * SB_HEAD_DIM
SB_BLOCK = 128
FFN_HIDDEN = -(-8 * D_MODEL // (3 * 256)) * 256


def rms_norm_2(x, g):
    xf = x.astype(jnp.float32)
    y = xf * lax.rsqrt(jnp.mean(xf * xf, axis=-1, keepdims=True) + EPS)
    return (y * g.astype(jnp.float32)).astype(x.dtype)

def l2_norm(x):
    return x * lax.rsqrt(jnp.sum(x * x, axis=-1, keepdims=True) + EPS)

def causal_conv(x, w):
    k_w, c = w.shape
    return lax.conv_general_dilated(x, w[:, None, :], window_strides=(1,), padding=[(k_w - 1, 0)],
                                    dimension_numbers=('NWC', 'WIO', 'NWC'), feature_group_count=c)

def to_chunks(t):
    b, s, h = t.shape[:3]
    t = t.reshape((b, s // GDN_CHUNK, GDN_CHUNK, h) + t.shape[3:])
    return jnp.swapaxes(t, 2, 3)

def gated_delta_rule(q, k, v, g, beta):
    b_, s_, h_, dk = q.shape
    dv = v.shape[-1]
    c = GDN_CHUNK
    q, k, v, g, beta = to_chunks(q), to_chunks(k), to_chunks(v), to_chunks(g), to_chunks(beta)
    G = jnp.cumsum(g, axis=-1)
    causal = jnp.tril(jnp.ones((c, c), dtype=bool))
    strict = jnp.tril(jnp.ones((c, c), dtype=bool), -1)
    decay_mat = jnp.exp(jnp.where(causal, G[..., :, None] - G[..., None, :], -jnp.inf))
    kk = jnp.einsum('bnhrd,bnhsd->bnhrs', k, k)
    a_low = jnp.where(strict, beta[..., None] * kk * decay_mat, 0.0)
    eye = jnp.eye(c, dtype=q.dtype)
    rhs = jnp.concatenate([v * beta[..., None], k * (beta * jnp.exp(G))[..., None]], axis=-1)
    sol = lax.linalg.triangular_solve(a_low + eye, rhs, left_side=True, lower=True, unit_diagonal=True)
    u, w = sol[..., :dv], sol[..., dv:]
    qk = jnp.einsum('bnhrd,bnhsd->bnhrs', q, k) * decay_mat
    q_dec = q * jnp.exp(G)[..., None]
    k_dec = k * jnp.exp(G[..., -1:] - G)[..., None]
    g_last = jnp.exp(G[..., -1])

    def step(state, xs):
        q_c, k_c, qk_c, u_c, w_c, gl_c = xs
        v_new = u_c - jnp.einsum('bhcd,bhde->bhce', w_c, state)
        o = jnp.einsum('bhcd,bhde->bhce', q_c, state) + jnp.einsum('bhrs,bhse->bhre', qk_c, v_new)
        state = state * gl_c[..., None, None] + jnp.einsum('bhcd,bhce->bhde', k_c, v_new)
        return state, o

    xs = tuple(jnp.moveaxis(t, 1, 0) for t in (q_dec, k_dec, qk, u, w, g_last))
    s0 = jnp.zeros((b_, h_, dk, dv), q.dtype)
    _, o = lax.scan(step, s0, xs)
    return o.transpose(1, 0, 3, 2, 4).reshape(b_, s_, h_, dv)

def gdn_mixer(hn, w_in, w_conv, a_log, dt_bias, norm_g, w_out):
    b_, s_, _ = hn.shape
    proj = hn @ w_in
    qkv = jax.nn.silu(causal_conv(proj[..., :3 * GDN_WIDTH], w_conv))
    gate = proj[..., 3 * GDN_WIDTH:4 * GDN_WIDTH].reshape(b_, s_, GDN_HEADS, GDN_HEAD_DIM)
    a_in = proj[..., 4 * GDN_WIDTH:4 * GDN_WIDTH + GDN_HEADS].astype(jnp.float32)
    b_in = proj[..., 4 * GDN_WIDTH + GDN_HEADS:].astype(jnp.float32)
    qkv = qkv.astype(jnp.float32).reshape(b_, s_, 3, GDN_HEADS, GDN_HEAD_DIM)
    q = l2_norm(qkv[:, :, 0]) * (GDN_HEAD_DIM ** -0.5)
    k = l2_norm(qkv[:, :, 1])
    v = qkv[:, :, 2]
    beta = jax.nn.sigmoid(b_in)
    g = -jnp.exp(a_log.astype(jnp.float32)) * jax.nn.softplus(a_in + dt_bias.astype(jnp.float32))
    o = gated_delta_rule(q, k, v, g, beta).astype(hn.dtype)
    o = rms_norm_2(o, norm_g) * jax.nn.silu(gate)
    return o.reshape(b_, s_, GDN_WIDTH) @ w_out

def shared_kv(h, kv_norm, w_kv, k_norm):
    b_, s_, _ = h.shape
    kv = (rms_norm_2(h, kv_norm) @ w_kv).reshape(b_, s_, 2, SB_HEADS, SB_HEAD_DIM)
    k = rms_norm_2(kv[:, :, 0], k_norm).transpose(0, 2, 1, 3)
    v = kv[:, :, 1].transpose(0, 2, 1, 3)
    return k, v

def stick_breaking(q, k, v):
    s_ = q.shape[2]
    outs = []
    for blk in range(s_ // SB_BLOCK):
        t0, t1 = blk * SB_BLOCK, (blk + 1) * SB_BLOCK
        z = jnp.einsum('bhtd,bhsd->bhts', q[:, :, t0:t1], k[:, :, :t1]).astype(jnp.float32)
        t_idx = t0 + jnp.arange(SB_BLOCK)[:, None]
        s_idx = jnp.arange(t1)[None, :]
        mask = s_idx < t_idx
        log_not = jnp.where(mask, jax.nn.log_sigmoid(-z), 0.0)
        suffix = lax.cumsum(log_not, axis=3, reverse=True) - log_not
        log_w = jnp.where(mask, jax.nn.log_sigmoid(z) + suffix, -jnp.inf)
        wgt = jnp.exp(log_w).astype(v.dtype)
        outs.append(jnp.einsum('bhts,bhsd->bhtd', wgt, v[:, :, :t1]))
    return jnp.concatenate(outs, axis=2)

def sb_mixer(hn, k_sh, v_sh, w_q, q_norm, w_out):
    b_, s_, _ = hn.shape
    q = (hn @ w_q).reshape(b_, s_, SB_HEADS, SB_HEAD_DIM)
    q = (rms_norm_2(q, q_norm) * (SB_HEAD_DIM ** -0.5)).transpose(0, 2, 1, 3)
    o = stick_breaking(q, k_sh, v_sh)
    return o.transpose(0, 2, 1, 3).reshape(b_, s_, SB_WIDTH) @ w_out

def swiglu(hn, w_in, w_out):
    gu = hn @ w_in
    return (jax.nn.silu(gu[..., :FFN_HIDDEN]) * gu[..., FFN_HIDDEN:]) @ w_out

def second_inputs(seed: int = 0) -> dict:
    key = jax.random.key(seed)
    ks = jax.random.split(key, 24)
    f32 = jnp.float32

    def nrm(k, shape, fan_in):
        return jax.random.normal(k, shape, f32) * (fan_in ** -0.5)

    def gain(k, shape):
        return 1.0 + 0.02 * jax.random.normal(k, shape, f32)

    dt = jnp.exp(jax.random.uniform(ks[8], (N_A_LAYERS, GDN_HEADS), f32, math.log(1e-3), math.log(1e-1)))
    return {
        "x": jax.random.normal(ks[0], (BATCH, SEQ, D_MODEL), f32),
        "p": jax.random.normal(ks[1], (DEPTH_2, BATCH, SEQ, PLE_DIM), f32),
        "ln_mix": gain(ks[2], (DEPTH_2, D_MODEL)),
        "ln_ffn": gain(ks[3], (DEPTH_2, D_MODEL)),
        "ln_ple": gain(ks[4], (DEPTH_2, D_MODEL)),
        "gdn_w_in": nrm(ks[5], (N_A_LAYERS, D_MODEL, 4 * GDN_WIDTH + 2 * GDN_HEADS), D_MODEL),
        "gdn_conv": nrm(ks[6], (N_A_LAYERS, CONV_WIDTH_2, 3 * GDN_WIDTH), CONV_WIDTH_2),
        "gdn_a_log": jnp.log(jax.random.uniform(ks[7], (N_A_LAYERS, GDN_HEADS), f32, 1.0, 16.0)),
        "gdn_dt_bias": dt + jnp.log(-jnp.expm1(-dt)),
        "gdn_norm": gain(ks[9], (N_A_LAYERS, GDN_HEAD_DIM)),
        "gdn_w_out": nrm(ks[10], (N_A_LAYERS, GDN_WIDTH, D_MODEL), GDN_WIDTH),
        "kv_norm": gain(ks[11], (D_MODEL,)),
        "w_kv": nrm(ks[12], (D_MODEL, 2 * SB_WIDTH), D_MODEL),
        "k_norm": gain(ks[13], (SB_HEAD_DIM,)),
        "sb_w_q": nrm(ks[14], (N_B_LAYERS, D_MODEL, SB_WIDTH), D_MODEL),
        "sb_q_norm": gain(ks[15], (N_B_LAYERS, SB_HEAD_DIM)),
        "sb_w_out": nrm(ks[16], (N_B_LAYERS, SB_WIDTH, D_MODEL), SB_WIDTH),
        "ffn_w_in": nrm(ks[17], (DEPTH_2, D_MODEL, 2 * FFN_HIDDEN), D_MODEL),
        "ffn_w_out": nrm(ks[18], (DEPTH_2, FFN_HIDDEN, D_MODEL), FFN_HIDDEN),
        "ple_w_proj": nrm(ks[19], (DEPTH_2, PLE_DIM, D_MODEL), PLE_DIM),
        "ple_w_gate": nrm(ks[20], (DEPTH_2, D_MODEL, D_MODEL), D_MODEL),
    }

def second_block(x, p, ln_mix, ln_ffn, ln_ple, gdn_w_in, gdn_conv, gdn_a_log, gdn_dt_bias, gdn_norm,
              gdn_w_out, kv_norm, w_kv, k_norm, sb_w_q, sb_q_norm, sb_w_out, ffn_w_in, ffn_w_out,
              ple_w_proj, ple_w_gate):
    h = x
    k_sh, v_sh = None, None
    for i in range(DEPTH_2):
        hn = rms_norm_2(h, ln_mix[i])
        if i < N_A_LAYERS:
            h = h + gdn_mixer(hn, gdn_w_in[i], gdn_conv[i], gdn_a_log[i], gdn_dt_bias[i],
                              gdn_norm[i], gdn_w_out[i])
        else:
            j = i - N_A_LAYERS
            h = h + sb_mixer(hn, k_sh, v_sh, sb_w_q[j], sb_q_norm[j], sb_w_out[j])
        h = h + swiglu(rms_norm_2(h, ln_ffn[i]), ffn_w_in[i], ffn_w_out[i])
        h = h + (p[i] @ ple_w_proj[i]) * jax.nn.sigmoid(rms_norm_2(h, ln_ple[i]) @ ple_w_gate[i])
        if i == N_A_LAYERS - 1:
            k_sh, v_sh = shared_kv(h, kv_norm, w_kv, k_norm)
    return h


def setup_inputs(seed=0):
    out = dict(first_inputs(seed))
    for name, value in second_inputs(seed + 1).items():
        if name != "x":
            out[name + "_2"] = value
    return out


def reference(
    x, ffn1_norm, ffn1_w13, ffn1_w2, mix_norm, w_in, conv_w, conv_b, conv_ln_g, conv_ln_b,
    forget_b, out_norm_conv, out_norm_attn, w_out, ffn2_norm, ffn2_w13, ffn2_w2, final_norm,
    p_2, ln_mix_2, ln_ffn_2, ln_ple_2, gdn_w_in_2, gdn_conv_2, gdn_a_log_2, gdn_dt_bias_2,
    gdn_norm_2, gdn_w_out_2, kv_norm_2, w_kv_2, k_norm_2, sb_w_q_2, sb_q_norm_2, sb_w_out_2,
    ffn_w_in_2, ffn_w_out_2, ple_w_proj_2, ple_w_gate_2,
):
    x = first_block(
        x, ffn1_norm, ffn1_w13, ffn1_w2, mix_norm, w_in, conv_w, conv_b, conv_ln_g, conv_ln_b,
        forget_b, out_norm_conv, out_norm_attn, w_out, ffn2_norm, ffn2_w13, ffn2_w2, final_norm,
    )
    return second_block(
        x, p_2, ln_mix_2, ln_ffn_2, ln_ple_2, gdn_w_in_2, gdn_conv_2, gdn_a_log_2,
        gdn_dt_bias_2, gdn_norm_2, gdn_w_out_2, kv_norm_2, w_kv_2, k_norm_2, sb_w_q_2,
        sb_q_norm_2, sb_w_out_2, ffn_w_in_2, ffn_w_out_2, ple_w_proj_2, ple_w_gate_2,
    )


_drawn_inputs = setup_inputs


def setup_inputs(seed=0):
    import zlib

    import numpy as np

    out = dict(_drawn_inputs(seed))
    spreads = {}
    factors = {'conv_ln_b': 4.036,
     'ffn2_norm': 3.006,
     'ln_mix_2': 3.091,
     'ln_ffn_2': 3.456,
     'ln_ple_2': 8.0,
     'gdn_norm_2': 5.851,
     'kv_norm_2': 5.529,
     'k_norm_2': 8.0,
     'sb_q_norm_2': 8.0}
    for name, (base, spread) in spreads.items():
        noise = np.random.default_rng([zlib.crc32(name.encode()), seed]).standard_normal(out[name].shape)
        drawn = base * np.exp(spread * noise) if base else spread * noise
        out[name] = __import__('jax').numpy.asarray(drawn.astype(out[name].dtype))
    for name, factor in factors.items():
        out[name] = (out[name] * factor).astype(out[name].dtype)
    return out
```

```python
from contextlib import ExitStack
import math

import concourse.bass as bass
from concourse import mybir

F32 = mybir.dt.float32
F32R = mybir.dt.float32r
ALU = mybir.AluOpType
ACT = mybir.ActivationFunctionType
AX_X = mybir.AxisListType.X

P = 128
EPS = 1e-6
BIG = 1e30


def build_program(nc, a, out):
    SEQ, D = a["x"].shape[1:]
    NT = SEQ // P
    KD = D // P
    KF = a["ffn1_w2"].shape[1] // P
    NBLK = KF // 2
    DC = a["conv_b"].shape[1]
    CT = DC // P
    TAPS = a["conv_w"].shape[1]
    PAD = TAPS - 1
    H1 = a["forget_b"].shape[1]
    D1 = DC // H1
    H2 = a["gdn_a_log_2"].shape[1]
    HG = H2 // 4
    W4 = a["gdn_conv_2"].shape[1]
    PAD4 = W4 - 1
    QKV = 3 * H2
    PLE = a["p_2"].shape[3]
    RAW, SPLIT = 4, 3
    SLOT = 4 * 512

    slots, first = [], {}

    def stream_gate_up(name, w):
        first[name] = len(slots)
        v = w.rearrange("(k p) (g n) -> p k g n", p=P, g=2)
        for j in range(NBLK):
            for h in range(2):
                slots.append([(("k", k), v[:, 4 * h + k, :, j * 256:(j + 1) * 256]) for k in range(4)])

    def stream_blocks(name, w, n):
        first[name] = len(slots)
        v = w.rearrange("(k p) n -> p k n", p=P)
        for c in range(n):
            for h in range(2):
                slots.append([(("rows", 4), v[:, 4 * h:4 * h + 4, c * 512:(c + 1) * 512])])

    def stream_wide(name, w):
        first[name] = len(slots)
        v = w.rearrange("(k p) n -> p k n", p=P)
        for s in range(w.shape[0] // (2 * P)):
            slots.append([(("rows", 2), v[:, 2 * s:2 * s + 2, :])])

    stream_gate_up("up0", a["ffn1_w13"][0])
    stream_wide("down0", a["ffn1_w2"][0])
    stream_blocks("mix", a["w_in"][0], 5)
    stream_wide("mix_out", a["w_out"][0])
    stream_gate_up("up1", a["ffn2_w13"][0])
    stream_wide("down1", a["ffn2_w2"][0])
    stream_blocks("gdn", a["gdn_w_in_2"][0], 8)
    stream_wide("gdn_out", a["gdn_w_out_2"][0])
    stream_gate_up("up2", a["ffn_w_in_2"][0])
    stream_wide("down2", a["ffn_w_out_2"][0])
    stream_wide("ple_p0", a["ple_w_proj_2"][0])
    stream_wide("ple_g0", a["ple_w_gate_2"][0])
    stream_blocks("kv", a["w_kv_2"], 4)
    stream_blocks("sbq", a["sb_w_q_2"][0], 2)
    stream_wide("sb_out", a["sb_w_out_2"][0])
    stream_gate_up("up3", a["ffn_w_in_2"][1])
    stream_wide("down3", a["ffn_w_out_2"][1])
    stream_wide("ple_p1", a["ple_w_proj_2"][1])
    stream_wide("ple_g1", a["ple_w_gate_2"][1])
    NSLOT = len(slots)

    WIDE = ["down0", "mix_out", "down1", "gdn_out", "down2", "ple_g0", "sb_out", "down3", "ple_g1"]
    wide_slots = {n: (KF if n[:4] == "down" else KD) // 2 for n in WIDE}

    NORM = [a["ffn1_norm"][0], a["mix_norm"][0], a["ffn2_norm"][0], a["final_norm"], a["ln_mix_2"][0],
            a["ln_ffn_2"][0], a["ln_ple_2"][0], a["kv_norm_2"], a["ln_mix_2"][1], a["ln_ffn_2"][1],
            a["ln_ple_2"][1]]
    FINAL = 3
    gain_before = {"up0": [0], "mix": [1], "up1": [2], "gdn": [3, 4], "up2": [5], "ple_p0": [6],
                   "kv": [7, 8], "up3": [9], "ple_p1": [10]}
    TURN = ["n0", "n1", "n2", "n4", "gdn", "n5", "n6", "n7", "n8", "sb", "n9", "n10"]
    turn_of_up = ["n0", "n2", "n5", "n9"]

    with ExitStack() as ctx:
        def sb(name, shape, dt=F32):
            return ctx.enter_context(nc.sbuf_tensor(name, shape, dt))

        made = {}

        def sem(name):
            if name not in made:
                made[name] = ctx.enter_context(nc.semaphore(name))
            return made[name]

        bank = [ctx.enter_context(nc.psum_tensor(f"bank{i}", [P, 512], F32)) for i in range(8)]
        raw = [sb(f"raw{i}", [P, SLOT]) for i in range(RAW)]
        whi = [sb(f"whi{i}", [P, SLOT], F32R) for i in range(SPLIT)]
        wlo = [sb(f"wlo{i}", [P, SLOT], F32R) for i in range(SPLIT)]
        X = sb("X", [P, NT, D])
        xs = sb("xs", [P, NT, D])
        xThi = sb("xThi", [P, KD, SEQ], F32R)
        xTlo = sb("xTlo", [P, KD, SEQ], F32R)
        gain = [sb(f"gain{i}", [P, D]) for i in range(2)]
        ident = sb("ident", [P, P])
        ones = sb("ones", [P, P])
        upto = sb("upto", [P, P])
        sumsq = sb("sumsq", [P, 2 * len(NORM)])
        meansq = sb("meansq", [P, 2 * len(NORM)])
        rstd = sb("rstd", [P, 2 * len(NORM)])
        eps_col = sb("eps_col", [P, 1])
        mean_of = sb("mean_of", [P, P])
        half = sb("half", [P, 16])
        chan = sb("chan", [P, 4, CT])
        tap = sb("tap", [P, CT, TAPS])
        tap4 = sb("tap4", [P, QKV, W4])
        attn_gain = sb("attn_gain", [P, DC])
        forget_b = sb("forget_b", [P, H1])
        narrow = sb("narrow", [P, KD, 24])
        narrow_hi = sb("narrow_hi", [P, KD, 24], F32R)
        narrow_lo = sb("narrow_lo", [P, KD, 24], F32R)
        a_log = sb("a_log", [P, H2])
        dt_bias = sb("dt_bias", [P, H2])
        head_gain = sb("head_gain", [P, 3, P])
        GDNG, KG, QG = range(3)

        def region(always, *turns):
            got = []
            with ExitStack() as phase:
                got += [phase.enter_context(nc.sbuf_tensor(n, s, d)) for n, s, d in always]
                for specs in turns:
                    with ExitStack() as turn:
                        got += [turn.enter_context(nc.sbuf_tensor(n, s, d)) for n, s, d in specs]
            return got

        hThi, hTlo, hnat, silu, p_in, pThi, pTlo, row_chan, row_tap, row_tap4 = region(
            [("hThi", [P, KF, SEQ], F32R), ("hTlo", [P, KF, SEQ], F32R),
             ("hnat", [P, 2, NT, 256], F32), ("silu", [P, 2, NT, 256], F32)],
            [("p_in", [P, NT, PLE], F32), ("pThi", [P, 2, SEQ], F32R), ("pTlo", [P, 2, SEQ], F32R)],
            [("row_chan", [4 * CT, P], F32), ("row_tap", [TAPS, DC], F32), ("row_tap4", [W4, QKV * P], F32)])
        pp, gate_s = region([("pp", [P, NT, D], F32), ("gate_s", [P, NT, D], F32)])
        (u, gs, y, ysq, cmu, crs, qz, kT, v1, mask1, zf, zfe, lf, cum, dg1, p1, p2, pT1, mx, nmx, rsum, rinv, yA,
         yst, yms, yrs, minus1, prod1) = region([
            ("u", [P, CT, PAD + SEQ], F32), ("gs", [P, CT, SEQ], F32), ("y", [P, CT, SEQ], F32),
            ("ysq", [P, CT, SEQ], F32), ("cmu", [P, SEQ], F32), ("crs", [P, SEQ], F32),
            ("qz", [P, H1, SEQ], F32), ("kT", [P, CT, SEQ], F32), ("v1", [P, NT, DC], F32),
            ("mask1", [P, SEQ], F32), ("zf", [P, NT, H1], F32), ("zfe", [P, NT, H1], F32),
            ("lf", [P, NT, H1], F32), ("cum", [P, NT, H1], F32), ("dg1", [P, 2, NT, P], F32),
            ("p1", [P, 2, 384], F32), ("p2", [P, 2, 384], F32), ("pT1", [P, 2, 384], F32),
            ("mx", [P, 2, 2], F32), ("nmx", [P, 2, 2], F32), ("rsum", [P, NT, H1], F32),
            ("rinv", [P, NT, H1], F32), ("yA", [P, NT, DC], F32), ("yst", [P, 2], F32), ("yms", [P, 2], F32),
            ("yrs", [P, 2], F32), ("minus1", [P, P], F32),
            ("prod1", [P, 3, SEQ], F32)])
        (qkT, sg, zab, eab, gl, lkq, vec, knat, bv, dg, dec, AT, QKT, lvl, maskT, S, oss, oms, ors, v_or_TU, u4, y4,
         sq4) = region(
            [("qkT", [P, 2 * H2, SEQ], F32), ("sg", [P, NT, D], F32), ("zab", [P, NT, 2 * H2], F32),
             ("eab", [P, NT, 2 * H2], F32), ("gl", [P, NT, 2 * H2], F32), ("lkq", [P, NT, 2 * H2], F32),
             ("vec", [P, 10, NT, H2], F32), ("knat", [P, H2, P], F32), ("bv", [P, NT, D], F32),
             ("dg", [P, 4, P], F32), ("dec", [P, 4, P], F32), ("AT", [P, HG, 4, P], F32),
             ("QKT", [P, HG, 4, P], F32), ("lvl", [P, 7, P], F32), ("maskT", [P, P], F32), ("S", [P, H2, P], F32),
             ("oss", [P, NT, H2], F32), ("oms", [P, NT, H2], F32), ("ors", [P, NT, H2], F32),
             ("v_or_TU", [P, H2 * SEQ], F32), ("u4", [P, 4, PAD4 + SEQ], F32), ("y4", [P, 4, SEQ], F32),
             ("sq4", [P, 4, SEQ], F32)])
        vT = v_or_TU[:].rearrange("p (h t) -> p h t", h=H2)
        T, U = (v_or_TU[:, i * HG * 512:(i + 1) * HG * 512].rearrange("p (g h c) -> p g h c", g=HG, h=4) for i in range(2))
        (vs, kn, xThi2, xTlo2, skT, sqT, sab, sq_s, spl, sw, smask, sbig, neg_tri, neg_one, kss, kms, krs) = region([
            ("vs", [P, NT, D], F32), ("kn", [P, NT, D], F32), ("xThi2", [P, KD, SEQ], F32R), ("xTlo2", [P, KD, SEQ], F32R),
            ("skT", [P, H2, SEQ], F32), ("sqT", [P, H2, SEQ], F32), ("sab", [P, 2, 384], F32), ("sq_s", [P, D], F32),
            ("spl", [P, 2, 384], F32), ("sw", [P, 2, 384], F32), ("smask", [P, 384], F32), ("sbig", [P, 384], F32),
            ("neg_tri", [P, P], F32), ("neg_one", [P, P], F32), ("kss", [P, 2, NT, H2], F32), ("kms", [P, 2, NT, H2], F32),
            ("krs", [P, 2, NT, H2], F32)])

        Lm = y4[:].rearrange("p h t -> p (h t)").rearrange("p (g h c) -> p g h c", g=HG, h=4)
        Y = u4[:].rearrange("p h t -> p (h t)")[:, 0:HG * 256].rearrange("p (g h c) -> p g h c", g=HG, h=4)
        vn = sq4[:, 0:2, :].rearrange("p a t -> p (a t)").rearrange("p (h c) -> p h c", h=4)
        vne = sq4[:, 2:4, :].rearrange("p a t -> p (a t)").rearrange("p (h c) -> p h c", h=4)
        DG, DEC = (dg, vn), (dec, vne)
        r2, tq = dg, dec
        o2 = xs
        prod4 = knat[:].rearrange("p h c -> p (h c)")[:, 0:3 * SEQ].rearrange("p (b t) -> p b t", b=3)
        G_, GL, ROWA, ROWQ, COL, CKS, CQS, CVN, BETA, TMP = range(10)

        raw_in = [sem(f"raw_in{i}") for i in range(RAW)]
        w_hi, w_lo, w_used = sem("w_hi"), sem("w_lo"), sem("w_used")

        def out_bank(t, h):
            return bank[(6, 7, 2, 3)[2 * t + h]]

        arrived, total = [], [0] * RAW
        for w, pieces in enumerate(slots):
            total[w % RAW] += 16 * len(pieces)
            arrived.append(total[w % RAW])

        def turn(name):
            return TURN.index(name)

        def turned_in(name, t):
            return 2 * [x for x in TURN if x != "sb"].index(name) + t + 1

        def last_group(name):
            return first[name] + wide_slots[name] - SPLIT

        N_LOADS = 15

        block = ctx.enter_context(nc.Block())

        @block.sync
        def _(sp):
            def load_consts():
                done = sem("consts_in")
                for i, name in enumerate(("conv_b", "conv_ln_g", "conv_ln_b", "out_norm_conv")):
                    sp.dma_start(row_chan[i * CT:(i + 1) * CT, :],
                                 a[name][0].rearrange("(c p) -> c p", p=P)).then_inc(done, 16)
                sp.dma_start(row_tap[:], a["conv_w"][0]).then_inc(done, 16)
                sp.dma_start(row_tap4[:], a["gdn_conv_2"][0]).then_inc(done, 16)
                sp.dma_start(attn_gain[:], a["out_norm_attn"][0].partition_broadcast(P)).then_inc(done, 16)
                sp.dma_start(forget_b[:], a["forget_b"][0].partition_broadcast(P)).then_inc(done, 16)
                sp.dma_start(a_log[:], a["gdn_a_log_2"][0].partition_broadcast(P)).then_inc(done, 16)
                sp.dma_start(dt_bias[:], a["gdn_dt_bias_2"][0].partition_broadcast(P)).then_inc(done, 16)
                sp.dma_start(head_gain[:, GDNG, :], a["gdn_norm_2"][0].partition_broadcast(P)).then_inc(done, 16)
                sp.dma_start(head_gain[:, KG, :], a["k_norm_2"].partition_broadcast(P)).then_inc(done, 16)
                sp.dma_start(head_gain[:, QG, :], a["sb_q_norm_2"][0].partition_broadcast(P)).then_inc(done, 16)
                sp.dma_start(narrow[:, :, 0:H1], a["w_in"][0].rearrange("(k p) n -> p k n", p=P)[:, :, 5 * 512:])\
                    .then_inc(done, 16)
                sp.dma_start(narrow[:, :, H1:H1 + 2 * H2],
                             a["gdn_w_in_2"][0].rearrange("(k p) n -> p k n", p=P)[:, :, 8 * 512:]).then_inc(done, 16)

            for w, pieces in enumerate(slots):
                for name, s0 in first.items():
                    if s0 != w:
                        continue
                    for n in gain_before.get(name, []):
                        if n - 2 == FINAL:
                            sp.wait_ge(sem("final_x"), NT)
                        elif n >= 2:
                            sp.wait_ge(sem("turn_in"), turned_in(f"n{n - 2}", 1))
                        sp.dma_start(gain[n % 2][:], NORM[n].partition_broadcast(P)).then_inc(sem(f"gain_in{n % 2}"), 16)
                    if name in ("down2", "down3"):
                        i = int(name[4]) - 2
                        if i:
                            sp.wait_ge(sem("p_T"), 1)
                        for t in range(NT):
                            sp.dma_start(p_in[:, t, :], a["p_2"][i, 0, t * P:(t + 1) * P, :]).then_inc(sem("p_in"), 16)
                if w == 0:
                    for t in range(NT):
                        sp.dma_start(X[:, t, :], a["x"][0, t * P:(t + 1) * P, :]).then_inc(sem(f"x_in{t}"), 16)
                if w == RAW:
                    load_consts()
                if w >= RAW:
                    sp.wait_ge(w_lo, w - RAW + 1)
                dst = raw[w % RAW]
                for (kind, k), src in pieces:
                    if kind == "rows":
                        view = dst[:].rearrange("p (k n) -> p k n", k=k)
                    else:
                        view = dst[:, k * 512:(k + 1) * 512].rearrange("p (g n) -> p g n", g=2)
                    sp.dma_start(view, src).then_inc(raw_in[w % RAW], 16)
            for t in range(NT):
                sp.wait_ge(sem("x_ready"), 2 * (len(WIDE) - 1) + t + 1)
                sp.dma_start(out[0, t * P:(t + 1) * P, :], X[:, t, :]).then_inc(sem("stored"), 16)
            sp.wait_ge(sem("stored"), 16 * NT)

        def wait_wide(eng, m, t):
            if t == 0:
                eng.wait_ge(sem("wide_mm0"), m + 1)
            else:
                eng.wait_ge(w_used, first[WIDE[m]] + wide_slots[WIDE[m]])

        @block.scalar
        def _(act):
            split_to = [0]
            steps = [0]

            def step(ins):
                steps[0] += 1
                ins.then_inc(sem("act_step"), 1)
                act.wait_ge(sem("act_step"), steps[0])

            def split(n):
                while split_to[0] < min(n, NSLOT):
                    w = split_to[0]
                    act.wait_ge(raw_in[w % RAW], arrived[w])
                    if w >= SPLIT:
                        act.wait_ge(w_used, w - SPLIT + 1)
                    act.activation(whi[w % SPLIT][:], raw[w % RAW][:], ACT.Copy).then_inc(w_hi, 1)
                    split_to[0] += 1

            def norm_sum(n, t, ready, value):
                act.wait_ge(ready, value)
                i = turn(f"n{max(n, 4) if n == FINAL else n}")
                if i:
                    act.wait_ge(sem("turn_T"), 4 * (i - 1) + 2 * t + 2)
                act.activation(xs[:, t, :], X[:, t, :], ACT.Square,
                               accum_out=sumsq[:, 2 * n + t:2 * n + t + 1]).then_inc(sem("norm_ss"), 1)

            def turn_hi(name, t, dst=None):
                dst = dst or xThi
                for b in range(2):
                    act.wait_ge(sem("turn_T"), 4 * turn(name) + 2 * t + b + 1)
                    act.activation(dst[:, 4 * b:4 * b + 4, t * P:(t + 1) * P],
                                   bank[4 + b][:].rearrange("p (k c) -> p k c", k=4),
                                   ACT.Copy).then_inc(sem("turn_hi"), 1)

            def norm(n, m, follows, dst=None, before=None):
                for t in range(NT):
                    if before:
                        before(t)
                    if m is None:
                        norm_sum(n, t, sem(f"x_in{t}"), 16)
                    else:
                        norm_sum(n, t, sem("x_ready"), 2 * m + t + 1)
                    turn_hi(f"n{n}", t, dst)
                    if t == 0 and follows:
                        split(first[follows] + 2)

            def ffn(f):
                def hidden_hi(j):
                    act.wait_ge(sem("ffn_T"), NBLK * f + j + 1)
                    act.activation(hThi[:, 2 * j:2 * j + 2, :], bank[4 + j % 2][:].rearrange("p (k c) -> p k c", k=2),
                                   ACT.Copy).then_inc(sem("ffn_hi"), 1)

                for j in range(NBLK):
                    s = first[f"up{f}"] + 2 * j
                    split(s + (0 if j == 0 else 1) + SPLIT)
                    for t in range(NT):
                        if t == 0:
                            act.wait_ge(sem("ffn_mm0"), NBLK * f + j + 1)
                        else:
                            split(s + 1 + SPLIT)
                            act.wait_ge(w_used, s + 2)
                        if f or j >= 2:
                            act.wait_ge(sem("ffn_h"), 2 * (NBLK * f + j - 2) + t + 1)
                        act.activation(silu[:, j % 2, t, :], bank[2 * (j % 2) + t][:, 0:256],
                                       ACT.Silu).then_inc(sem("ffn_silu"), 1)
                    split(s + 2 + SPLIT)
                    if j:
                        hidden_hi(j - 1)
                    if f == 0 and j == 4:
                        act.wait_ge(sem("consts_in"), 16 * N_LOADS)
                        act.activation(narrow_hi[:], narrow[:], ACT.Copy).then_inc(sem("narrow_hi"), 1)
                split(first[f"down{f}"] + SPLIT)
                hidden_hi(NBLK - 1)

            def mixer1():
                s = first["mix"]
                split(s + 3 + SPLIT)
                act.wait_ge(w_used, s + 4)
                for i in range(2):
                    ins = act.activation(gs[:, 2 * i:2 * i + 2, :].rearrange("p c t -> p (c t)"), bank[2 + i][:], ACT.Sigmoid)
                ins.then_inc(sem("m_sig"), 1)
                split(s + 4 + SPLIT)
                act.wait_ge(sem("m_z"), 1)
                step(act.activation(zfe[:], zfe[:], ACT.Exp))
                act.activation(zfe[:], zfe[:], ACT.Ln, bias=1.0).then_inc(sem("m_ln"), 1)
                act.wait_ge(sem("m_cum"), 1)
                act.activation(cum[:].rearrange("p t h -> p (t h)"), bank[6][:, 32:32 + NT * H1], ACT.Copy).then_inc(sem("m_cum_in"), 1)
                split(s + 5 + SPLIT)
                act.wait_ge(w_used, s + 6)
                act.wait_ge(sem("m_zero"), 2)
                for i in range(2):
                    for r in range(2):
                        rows = slice(r * D1, (r + 1) * D1)
                        ins = act.activation(qz[rows, 4 * i + r:4 * i + r + 3:2, :],
                                             bank[i][rows, :].rearrange("p (c t) -> p c t", c=2), ACT.Copy, scale=D1 ** -0.5)
                ins.then_inc(sem("m_q"), 1)
                split(s + 7 + SPLIT)
                act.wait_ge(w_used, s + 8)
                for i in range(2):
                    ins = act.activation(kT[:, 2 * i:2 * i + 2, :].rearrange("p c t -> p (c t)"), bank[2 + i][:], ACT.Copy)
                ins.then_inc(sem("m_k"), 1)
                split(s + 9 + SPLIT)
                act.wait_ge(w_used, s + 10)
                for t in range(NT):
                    ins = act.activation(v1[:, t, :], bank[t][:], ACT.Copy)
                ins.then_inc(sem("m_v"), 1)
                split(s + 10 + SPLIT)
                act.wait_ge(sem("c_centred"), 1)
                act.activation(ysq[:], y[:], ACT.Square).then_inc(sem("c_sq"), 1)
                act.wait_ge(sem("c_sum"), 2)
                act.activation(cmu[:], bank[7][:, 0:SEQ], ACT.Sqrt, bias=eps_col[:, 0:1]).then_inc(sem("c_sd"), 1)
                act.wait_ge(sem("c_scaled"), 1)
                for c in range(CT):
                    ins = act.activation(y[:, c, :], y[:, c, :], ACT.Silu, bias=chan[:, 2, c:c + 1], scale=chan[:, 1, c:c + 1])
                step(ins)
                act.activation(ysq[:], y[:], ACT.Square).then_inc(sem("c_sq"), 1)
                act.wait_ge(sem("c_sum"), 3)
                act.activation(cmu[:], bank[7][:, 0:SEQ], ACT.Sqrt, bias=eps_col[:, 0:1]).then_inc(sem("c_sd"), 1)
                act.wait_ge(sem("c_scaled"), 2)
                for c in range(CT):
                    ins = act.activation(xThi[:, c, :], y[:, c, :], ACT.Copy, scale=chan[:, 3, c:c + 1])
                ins.then_inc(sem("c_hi"), 1)
                for h in range(H1 + 1):
                    if h < H1:
                        act.wait_ge(sem("at_nm"), h + 1)
                        if h >= 2:
                            act.wait_ge(sem("at_T"), h - 1)
                        for t in range(NT):
                            c = slice(0, P) if t == 0 else slice(P, 384)
                            ins = act.activation(p2[:, h % 2, c], p1[:, h % 2, c], ACT.Exp, bias=nmx[:, h % 2, t:t + 1],
                                                 accum_out=rsum[:, t, h:h + 1])
                        ins.then_inc(sem("at_exp"), 1)
                    if h:
                        g = h - 1
                        act.wait_ge(sem("at_T"), g + 1)
                        if g >= 2:
                            act.wait_ge(sem("at_pv"), g - 1)
                        act.activation(pT1[:, g % 2, :], bank[2 + g % 2][:, 0:384], ACT.Copy).then_inc(sem("at_pT"), 1)
                for t in range(NT):
                    act.wait_ge(sem("a_y"), t + 1)
                    act.activation(xs[:, t, 0:DC], yA[:, t, :], ACT.Square, accum_out=yst[:, t:t + 1]).then_inc(sem("a_ss"), 1)
                for t in range(NT):
                    act.wait_ge(sem("a_T"), t + 1)
                    act.activation(xThi[:, CT:KD, t * P:(t + 1) * P], bank[t][:].rearrange("p (k c) -> p k c", k=4),
                                   ACT.Copy).then_inc(sem("a_hi"), 1)
                split(last_group("mix_out") + SPLIT)

            def mixer2():
                s = first["gdn"]
                act.wait_ge(sem("g_z"), 1)
                act.activation(a_log[:], a_log[:], ACT.Exp)
                step(act.activation(eab[:], eab[:], ACT.Exp))
                act.activation(eab[:], eab[:], ACT.Ln, bias=1.0).then_inc(sem("g_ln"), 1)
                for b in range(6):
                    split(s + 2 * b + 1 + SPLIT)
                    act.wait_ge(w_used, s + 2 * b + 2)
                    if b:
                        act.wait_ge(sem("g_conv"), 3 * W4 * b)
                        act.wait_ge(sem("pool_sum"), TAPS + W4 * b)
                    for i in range(2):
                        ins = act.activation(u4[:, 2 * i:2 * i + 2, PAD4:], bank[2 * (b % 2) + i][:].rearrange("p (c t) -> p c t", c=2),
                                             ACT.Copy)
                    ins.then_inc(sem("g_u"), 1)
                    if b == 1:
                        act.wait_ge(sem("g_cum"), 1)
                        act.activation(vec[:, G_:GL + 1, :, :].rearrange("p v t h -> p (v t h)"), bank[7][:, 64:64 + 4 * H2], ACT.Copy)\
                        .then_inc(sem("g_cum_in"), 1)
                    split(s + 2 * b + 2 + SPLIT)
                    act.wait_ge(sem("g_conv"), 3 * W4 * (b + 1))
                    act.wait_ge(sem("pool_sum"), TAPS + W4 * (b + 1))
                    dst = qkT[:, 4 * b:4 * b + 4, :] if b < 4 else vT[:, 4 * (b - 4):4 * (b - 4) + 4, :]
                    ins = act.activation(dst, y4[:], ACT.Silu)
                    if b < 4:
                        step(ins)
                        if b:
                            act.wait_ge(sem("g_ss"), b)
                        act.activation(sq4[:], dst, ACT.Square).then_inc(sem("g_sq"), 1)
                    else:
                        ins.then_inc(sem("g_v"), 1)
                act.wait_ge(sem("g_ss"), 4)
                step(act.activation(lkq[:].rearrange("p t h -> p (t h)"), bank[6][:, 0:4 * H2], ACT.Ln, bias=eps_col[:, 0:1]))
                act.activation(lkq[:], lkq[:], ACT.Copy, scale=-0.5).then_inc(sem("g_lkq"), 1)
                act.wait_ge(sem("g_vec"), 1)
                act.activation(vec[:, CKS:CQS + 1, :, :], vec[:, ROWA:ROWQ + 1, :, :], ACT.Exp)
                act.activation(vec[:, CVN:BETA + 1, :, :], vec[:, CVN:BETA + 1, :, :], ACT.Exp).then_inc(sem("g_vexp"), 1)
                for b in range(2):
                    split(s + 12 + 2 * b + 1 + SPLIT)
                    act.wait_ge(w_used, s + 12 + 2 * b + 2)
                    for t in range(NT):
                        ins = act.activation(sg[:, t, b * 512:(b + 1) * 512], bank[2 * (b % 2) + t][:], ACT.Silu)
                    ins.then_inc(sem("g_gate"), 1)
                split(s + 16 + SPLIT)
                for g in range(HG):
                    act.wait_ge(sem("g_kn"), g + 1)
                    act.activation(knat[:, 4 * g:4 * g + 4, :].rearrange("p h c -> p (h c)"), bank[4 + g][:], ACT.Copy)\
                        .then_inc(sem("g_knat"), 1)
                for t in range(NT):
                    for g in range(HG):
                        for i in range(2):
                            n = 2 * (HG * t + g) + i
                            act.wait_ge(sem("g_decm"), n + 1)
                            for h in range(4):
                                ins = act.activation(DEC[i][:, h, :], DG[i][:, h, :], ACT.Exp,
                                                     bias=vec[:, COL, t, 4 * g + h:4 * g + h + 1])
                            ins.then_inc(sem("g_dec"), 1)
                    for l in range(7):
                        for g in range(HG):
                            n = HG * (7 * t + l) + g
                            act.wait_ge(sem("i_Y"), n + 1)
                            act.activation(Y[:, g, :, :].rearrange("p h c -> p (h c)"), bank[2 * g][:, 0:256], ACT.Copy)\
                                .then_inc(sem("i_Y_in"), 1)
                        for g in range(HG):
                            n = HG * (7 * t + l) + g
                            act.wait_ge(sem("i_TT"), n + 1)
                            act.activation(U[:, g, :, :].rearrange("p h c -> p (h c)"), bank[4 + g][:], ACT.Copy)\
                                .then_inc(sem("i_U"), 1)
                    for g in range(HG):
                        n = HG * t + g
                        act.wait_ge(sem("r_vn"), n + 1)
                        act.activation(vn[:].rearrange("p h c -> p (h c)"), bank[1][:], ACT.Copy).then_inc(sem("r_vn_in"), 1)
                        if t == 0:
                            act.wait_ge(sem("r_o"), n + 1)
                            act.activation(o2[:, 0, g * 512:(g + 1) * 512], bank[2][:], ACT.Copy).then_inc(sem("r_o_in"), 1)
                            act.wait_ge(sem("r_S"), g + 1)
                            act.activation(S[:, 4 * g:4 * g + 4, :].rearrange("p h c -> p (h c)"), bank[3][:], ACT.Copy)\
                                .then_inc(sem("r_S_in"), 1)
                for t in range(NT):
                    act.wait_ge(sem("r_o_in"), HG)
                    if t:
                        act.wait_ge(sem("r_o1"), HG)
                    if t:
                        act.wait_ge(sem("g_oss"), t)
                    act.activation(bv[:, 0, :], o2[:, t, :], ACT.Square).then_inc(sem("g_osq"), 1)
                for t in range(NT):
                    turn_hi("gdn", t)
                split(last_group("gdn_out") + SPLIT)

            def embed(i, m_before, n):
                act.wait_ge(sem("p_T"), i + 1)
                act.activation(pThi[:].rearrange("p k t -> p (k t)"), bank[0][:], ACT.Copy).then_inc(sem("p_hi"), 1)
                split(first[f"ple_p{i}"] + SPLIT)
                for t in range(NT):
                    if t == 0:
                        act.wait_ge(sem("pp_mm0"), i + 1)
                    else:
                        act.wait_ge(w_used, first[f"ple_p{i}"] + 1)
                    for h in range(2):
                        ins = act.activation(pp[:, t, h * 512:(h + 1) * 512], bank[(0, 1, 4, 5)[2 * t + h]][:], ACT.Copy)
                    ins.then_inc(sem("pp_in"), 1)
                norm(n, m_before, f"ple_g{i}")
                m = WIDE.index(f"ple_g{i}")
                split(last_group(f"ple_g{i}") + SPLIT)

                def gate(t):
                    wait_wide(act, m, t)
                    for h in range(2):
                        ins = act.activation(gate_s[:, t, h * 512:(h + 1) * 512], out_bank(t, h)[:], ACT.Sigmoid)
                    ins.then_inc(sem("gate_s"), 1)
                return gate

            def mixer3(gate):
                s = first["kv"]
                norm(7, WIDE.index("ple_g0"), "kv", before=gate)
                n_sq = 0
                for b in range(4):
                    split(s + 2 * b + 1 + SPLIT)
                    act.wait_ge(w_used, s + 2 * b + 2)
                    dst = kn if b < 2 else vs
                    for t in range(NT):
                        ins = act.activation(dst[:, t, (b % 2) * 512:(b % 2 + 1) * 512], bank[2 * (b % 2) + t][:], ACT.Copy)
                    ins.then_inc(sem("s_kv"), 1)
                    if b == 0:
                        norm(8, WIDE.index("ple_g0"), None, xThi2)
                    if b == 1:
                        split(s + 2 * b + 2 + SPLIT)
                        for t in range(NT):
                            if t:
                                act.wait_ge(sem("s_kss"), t)
                            act.wait_ge(sem("s_kv"), 2)
                            act.activation(sq_s[:], kn[:, t, :], ACT.Square).then_inc(sem("s_sq"), 1)
                for t in range(NT):
                    for b in range(2):
                        act.wait_ge(sem("s_kT"), 2 * t + b + 1)
                        act.activation(skT[:, 4 * b:4 * b + 4, t * P:(t + 1) * P], bank[4 + b][:].rearrange("p (k c) -> p k c", k=4),
                                       ACT.Copy).then_inc(sem("s_kT_in"), 1)
                s = first["sbq"]
                for b in range(2):
                    split(s + 2 * b + 1 + SPLIT)
                    act.wait_ge(w_used, s + 2 * b + 2)
                    for t in range(NT):
                        ins = act.activation(kn[:, t, b * 512:(b + 1) * 512], bank[2 * (b % 2) + t][:], ACT.Copy)
                    ins.then_inc(sem("s_q"), 1)
                split(s + 4 + SPLIT)
                for t in range(NT):
                    act.wait_ge(sem("s_kss"), 2 + t)
                    act.wait_ge(sem("s_q"), 2)
                    act.activation(sq_s[:], kn[:, t, :], ACT.Square).then_inc(sem("s_sq"), 1)
                for t in range(NT):
                    for b in range(2):
                        act.wait_ge(sem("s_kT"), 4 + 2 * t + b + 1)
                        act.activation(sqT[:, 4 * b:4 * b + 4, t * P:(t + 1) * P], bank[4 + b][:].rearrange("p (k c) -> p k c", k=4),
                                       ACT.Copy).then_inc(sem("s_kT_in"), 1)
                for h in range(H2 + 1):
                    if h < H2:
                        act.wait_ge(sem("sb_z"), h + 1)
                        if h >= 2:
                            act.wait_ge(sem("sb_sp"), h - 1)
                        step(act.activation(sab[:, h % 2, :], bank[h % 2][:, 0:384], ACT.Abs))
                        step(act.activation(sab[:, h % 2, :], sab[:, h % 2, :], ACT.Exp, scale=-1.0))
                        act.activation(sab[:, h % 2, :], sab[:, h % 2, :], ACT.Ln, bias=1.0).then_inc(sem("sb_ln"), 1)
                    if h:
                        g = h - 1
                        act.wait_ge(sem("sb_lw"), g + 1)
                        act.activation(sw[:, g % 2, :], sw[:, g % 2, :], ACT.Exp).then_inc(sem("sb_w"), 1)
                    if h >= 2 and h % 2 == 0:
                        pair = h // 2 - 1
                        act.wait_ge(sem("sb_pv"), 2 * pair + 2)
                        act.activation(xs[:, :, pair * 256:(pair + 1) * 256].rearrange("p t (h c) -> p h t c", h=2),
                                       bank[4 + pair % 2][:].rearrange("p (h t c) -> p h t c", h=2, t=2), ACT.Copy)\
                            .then_inc(sem("sb_o_in"), 1)
                for t in range(NT):
                    turn_hi("sb", t)
                split(last_group("sb_out") + SPLIT)

            norm(0, None, "up0")
            ffn(0)
            split(last_group("down0") + SPLIT)
            norm(1, 0, "mix")
            mixer1()
            norm(2, 1, "up1")
            ffn(1)
            split(last_group("down1") + SPLIT)
            for t in range(NT):
                norm_sum(3, t, sem("x_ready"), 2 * 2 + t + 1)
            for t in range(NT):
                norm_sum(4, t, sem("final_x"), t + 1)
                turn_hi("n4", t)
                if t == 0:
                    split(first["gdn"] + 2)
            mixer2()
            norm(5, 3, "up2")
            ffn(2)
            split(last_group("down2") + SPLIT)
            gate = embed(0, 4, 6)
            mixer3(gate)
            norm(9, 6, "up3")
            ffn(3)
            split(last_group("down3") + SPLIT)
            gate = embed(1, 7, 10)
            for t in range(NT):
                gate(t)

        def y4_free(b):
            return (sem("g_sq"), b) if b <= 4 else (sem("g_v"), b - 4)

        @block.gpsimd
        def _(pool):
            steps = [0]

            def step(ins):
                steps[0] += 1
                ins.then_inc(sem("pool_step"), 1)
                pool.wait_ge(sem("pool_step"), steps[0])

            def select(ap, cmp, fill, base, pattern, by_partition):
                return pool.affine_select(out=ap, in_=ap, compare_op=cmp, fill=fill, base=base, pattern=pattern,
                                          channel_multiplier=by_partition)

            sums, added = [0], []

            def taps(prod, dst, src, n, weight, bias=None):
                def product(k):
                    q = len(added)
                    if q >= 3:
                        pool.wait_ge(sem("pool_sum"), added[q - 3])
                    pool.tensor_tensor(prod[:, q % 3, :], src(k), weight(k).broadcast_to([P, SEQ]), ALU.mult)\
                        .then_inc(sem("pool_prod"), 1)
                    added.append(base + k + 1)

                base = sums[0]
                if bias is None:
                    ins = pool.tensor_tensor(dst, src(0), weight(0).broadcast_to([P, SEQ]), ALU.mult)
                else:
                    ins = pool.tensor_scalar(dst, src(0), weight(0), bias, ALU.mult, ALU.add)
                ins.then_inc(sem("pool_sum"), 1)
                product(1)
                for k in range(1, n):
                    q = len(added)
                    if k + 1 < n:
                        product(k + 1)
                    pool.wait_ge(sem("pool_prod"), q)
                    pool.wait_ge(sem("pool_sum"), base + k)
                    pool.tensor_tensor(dst, dst, prod[:, (q - 1) % 3, :], ALU.add).then_inc(sem("pool_sum"), 1)
                sums[0] += n

            pool.memset(half[:], -0.5)
            pool.memset(eps_col[:], EPS)
            pool.memset(mean_of[:], 1.0 / DC)
            pool.memset(ones[:], 1.0)
            pool.memset(upto[:], 1.0)
            step(pool.memset(ident[:], 0.0))
            select(ident[:], ALU.not_equal, 1.0, 0, [[-1, P]], 1)
            select(upto[:], ALU.is_ge, 0.0, 0, [[1, P]], -1).then_inc(sem("consts"), 1)

            def root(dst, mean, sums, width, names, value):
                pool.wait_ge(sem(names[0]), value)
                step(pool.tensor_scalar(mean, sums, 1.0 / width, EPS, ALU.mult, ALU.add))
                pool.tensor_tensor(dst, mean, half[:, 0:sums.shape[-1]], ALU.pow).then_inc(sem(names[1]), 1)

            def norm(n):
                for t in range(NT):
                    c = slice(2 * n + t, 2 * n + t + 1)
                    root(rstd[:, c], meansq[:, c], sumsq[:, c], D, ("norm_ss", "norm_rstd"), 2 * n + t + 1)

            def mixer1():
                norm(1)
                pool.wait_ge(w_used, first["mix"])
                pool.memset(u[:, :, 0:PAD], 0.0).then_inc(sem("m_zero"), 1)
                pool.memset(qz[:], 0.0).then_inc(sem("m_zero"), 1)
                pool.memset(minus1[:], -1.0)
                step(pool.memset(mask1[:], 0.0))
                select(mask1[:, P:SEQ], ALU.is_ge, -BIG, 0, [[-1, P]], 1).then_inc(sem("m_mask"), 1)
                pool.wait_ge(sem("m_u"), 1)
                pool.wait_ge(sem("m_tap"), 1)
                c = CT - 1
                taps(prod1, y[:, c, :], lambda k: u[:, c, k:k + SEQ], TAPS, lambda k: tap[:, c, k:k + 1], chan[:, 0, c:c + 1])
                pool.wait_ge(sem("m_cum_in"), 1)
                for h in range(H1):
                    if h >= 2:
                        pool.wait_ge(sem("at_S"), h - 1)
                    pool.tensor_tensor(dg1[:, h % 2, :, :], ident[:].unsqueeze(1).broadcast_to([P, NT, P]),
                                       cum[:, :, h:h + 1].broadcast_to([P, NT, P]), ALU.mult).then_inc(sem("at_dg"), 1)
                for t in range(NT):
                    root(yrs[:, t:t + 1], yms[:, t:t + 1], yst[:, t:t + 1], DC, ("a_ss", "a_rs"), t + 1)

            def mixer2():
                norm(FINAL)
                norm(4)
                pool.wait_ge(w_used, first["gdn"])
                pool.memset(u4[:, :, 0:PAD4], 0.0).then_inc(sem("g_zero"), 1)
                pool.memset(maskT[:], 0.0)
                step(pool.memset(lvl[:], 0.0))
                select(maskT[:], ALU.is_ge, -BIG, 0, [[1, P]], -1)
                for l in range(7):
                    b = 2 ** l
                    v = lvl[:, l, :].rearrange("p (i j) -> p i j", j=2 * b)[:, :, b:2 * b]
                    step(pool.memset(v, 1.0))
                    step(select(v, ALU.is_ge, 0.0, 0, [[-2 * b, 64 // b], [0, b]], 1))
                    ins = select(v, ALU.is_ge, 0.0, b - 1, [[2 * b, 64 // b], [0, b]], -1)
                ins.then_inc(sem("g_masks"), 1)
                pool.wait_ge(sem("g_zero"), 1)
                for b in range(6):
                    pool.wait_ge(sem("g_u"), b + 1)
                    if b:
                        pool.wait_ge(*y4_free(b))
                    taps(prod4, y4[:, 3, :], lambda k: u4[:, 3, k:k + SEQ], W4, lambda k: tap4[:, 4 * b + 3, k:k + 1])
                pool.wait_ge(sem("g_vec"), 1)
                for t in range(NT):
                    for g in range(HG):
                        for i in range(2):
                            n = 2 * (HG * t + g) + i
                            if n >= 2:
                                pool.wait_ge(sem("g_dec"), n - 1)
                            if n == 2 * HG * t and t:
                                pool.wait_ge(sem("r_S"), HG)
                            pool.tensor_tensor(DG[i][:], ident[:].unsqueeze(1).broadcast_to([P, 4, P]),
                                               vec[:, ROWA + i, t, 4 * g:4 * g + 4].unsqueeze(2).broadcast_to([P, 4, P]),
                                               ALU.mult).then_inc(sem("g_dg"), 1)
                    for l in range(7):
                        for g in range(HG):
                            n = HG * (7 * t + l) + g
                            if l == 0:
                                pool.wait_ge(sem("g_AQ"), 2 * (HG * t + g) + 1)
                            else:
                                pool.wait_ge(sem("i_Y"), n - HG + 1)
                            pool.tensor_tensor(Lm[:, g, :, :], AT[:, g, :, :],
                                               lvl[:, l:l + 1, :].broadcast_to([P, 4, P]), ALU.mult).then_inc(sem("i_L"), 1)
                for t in range(NT):
                    root(ors[:, t, :], oms[:, t, :], oss[:, t, :], P, ("g_oss", "g_ors"), t + 1)

            def mixer3():
                norm(7)
                norm(8)
                pool.wait_ge(w_used, first["kv"])
                pool.memset(smask[:], 1.0)
                pool.memset(sbig[:], 0.0)
                pool.memset(neg_one[:], -1.0)
                step(pool.memset(neg_tri[:], -1.0))
                for c in (0, 2 * P):
                    select(smask[:, c:c + P], ALU.is_ge, 0.0, -1, [[1, P]], -1)
                    select(sbig[:, c:c + P], ALU.is_ge, -BIG, -1, [[1, P]], -1)
                select(neg_tri[:], ALU.is_ge, 0.0, 0, [[-1, P]], 1).then_inc(sem("s_masks"), 1)
                for i in range(2):
                    for t in range(NT):
                        root(krs[:, i, t, :], kms[:, i, t, :], kss[:, i, t, :], P, ("s_kss", "s_krs"), 2 * i + t + 1)

            norm(0)
            mixer1()
            norm(2)
            mixer2()
            norm(5)
            norm(6)
            mixer3()
            norm(9)
            norm(10)

        @block.vector
        def _(dve):
            split_to = [0]
            steps = [0]

            def step(ins):
                steps[0] += 1
                ins.then_inc(sem("dve_step"), 1)
                dve.wait_ge(sem("dve_step"), steps[0])

            def split(n):
                while split_to[0] < min(n, NSLOT):
                    w = split_to[0]
                    dve.wait_ge(w_hi, w + 1)
                    dve.tensor_tensor(wlo[w % SPLIT][:], raw[w % RAW][:], whi[w % SPLIT][:].bitcast(F32),
                                      ALU.subtract).then_inc(w_lo, 1)
                    split_to[0] += 1

            def norm_scale(n, t):
                dve.wait_ge(sem("norm_rstd"), 2 * n + t + 1)
                dve.wait_ge(sem(f"gain_in{n % 2}"), 16 * (n // 2 + 1))
                dst = X if n == FINAL else xs
                dve.scalar_tensor_tensor(out=dst[:, t, :], in0=X[:, t, :], scalar=rstd[:, 2 * n + t:2 * n + t + 1],
                                         in1=gain[n % 2][:], op0=ALU.mult, op1=ALU.mult)\
                   .then_inc(sem("final_x" if n == FINAL else "turn_in"), 1)

            def turn_lo(name, t, hi=None, lo=None):
                hi, lo = hi or xThi, lo or xTlo
                for b in range(2):
                    dve.wait_ge(sem("turn_hi"), 4 * turn(name) + 2 * t + b + 1)
                    part = (slice(None), slice(4 * b, 4 * b + 4), slice(t * P, (t + 1) * P))
                    dve.tensor_tensor(lo[part], bank[4 + b][:].rearrange("p (k c) -> p k c", k=4),
                                      hi[part].bitcast(F32), ALU.subtract).then_inc(sem("turn_lo"), 1)

            def norm(n, follows, hi=None, lo=None, before=None):
                for t in range(NT):
                    if before:
                        before(t)
                    norm_scale(n, t)
                    turn_lo(f"n{n}", t, hi, lo)
                    if t == 0 and follows:
                        split(first[follows] + 2)

            def residual(name, scale):
                m = WIDE.index(name)

                def add(t):
                    wait_wide(dve, m, t)
                    for h in range(2):
                        ins = dve.scalar_tensor_tensor(
                            out=X[:, t, h * 512:(h + 1) * 512], in0=out_bank(t, h)[:], scalar=scale,
                            in1=X[:, t, h * 512:(h + 1) * 512], op0=ALU.mult, op1=ALU.add)
                    ins.then_inc(sem("x_ready"), 1)
                split(last_group(name) + SPLIT)
                return add

            def ffn(f):
                def hidden_lo(j):
                    dve.wait_ge(sem("ffn_hi"), NBLK * f + j + 1)
                    dve.tensor_tensor(hTlo[:, 2 * j:2 * j + 2, :], bank[4 + j % 2][:].rearrange("p (k c) -> p k c", k=2),
                                      hThi[:, 2 * j:2 * j + 2, :].bitcast(F32), ALU.subtract).then_inc(sem("ffn_lo"), 1)

                for j in range(NBLK):
                    s = first[f"up{f}"] + 2 * j
                    split(s + (0 if j == 0 else 1) + SPLIT)
                    for t in range(NT):
                        if t:
                            split(s + 1 + SPLIT)
                        dve.wait_ge(sem("ffn_silu"), 2 * (NBLK * f + j) + t + 1)
                        if f or j >= 2:
                            dve.wait_ge(sem("ffn_T"), NBLK * f + j - 1)
                        dve.tensor_tensor(hnat[:, j % 2, t, :], silu[:, j % 2, t, :],
                                          bank[2 * (j % 2) + t][:, 256:512], ALU.mult).then_inc(sem("ffn_h"), 1)
                    split(s + 2 + SPLIT)
                    if j:
                        hidden_lo(j - 1)
                    if f == 0 and j == 4:
                        setup()
                split(first[f"down{f}"] + SPLIT)
                hidden_lo(NBLK - 1)

            def setup():
                dve.wait_ge(sem("setup_T"), 1)
                dve.tensor_copy(chan[:].rearrange("p v c -> p (v c)"), bank[7][:, 0:4 * CT])
                dve.tensor_copy(tap[:].rearrange("p c k -> p (c k)"), bank[7][:, 16:16 + CT * TAPS])
                dve.tensor_copy(tap4[:].rearrange("p c k -> p (c k)"), bank[7][:, 160:160 + QKV * W4]).then_inc(sem("m_tap"), 1)
                dve.wait_ge(sem("narrow_hi"), 1)
                dve.tensor_tensor(narrow_lo[:], narrow[:], narrow_hi[:].bitcast(F32), ALU.subtract).then_inc(sem("narrow_lo"), 1)

            def mixer1():
                s = first["mix"]
                split(s + 3 + SPLIT)
                dve.wait_ge(sem("m_sig"), 1)
                dve.wait_ge(sem("m_zero"), 1)
                for i in range(2):
                    ins = dve.tensor_tensor(u[:, 2 * i:2 * i + 2, PAD:], bank[i][:].rearrange("p (c t) -> p c t", c=2),
                                            gs[:, 2 * i:2 * i + 2, :], ALU.mult)
                ins.then_inc(sem("m_u"), 1)
                dve.wait_ge(sem("m_fl"), 1)
                step(dve.tensor_tensor(zf[:], bank[6][:, 0:NT * H1].rearrange("p (t h) -> p t h", t=NT),
                                       forget_b[:].unsqueeze(1).broadcast_to([P, NT, H1]), ALU.add))
                dve.scalar_tensor_tensor(out=zfe[:], in0=zf[:], scalar=-1.0, in1=zf[:], op0=ALU.mult, op1=ALU.min)\
                   .then_inc(sem("m_z"), 1)
                dve.wait_ge(sem("m_ln"), 1)
                dve.scalar_tensor_tensor(out=lf[:], in0=zf[:], scalar=0.0, in1=zfe[:], op0=ALU.min, op1=ALU.subtract)\
                   .then_inc(sem("m_lf"), 1)
                dve.wait_ge(sem("m_u"), 1)
                n = 0
                for k in range(TAPS):
                    for c in range(CT - 1):
                        src = u[:, c, k:k + SEQ]
                        if k == 0:
                            ins = dve.tensor_scalar(y[:, c, :], src, tap[:, c, k:k + 1], chan[:, 0, c:c + 1], ALU.mult, ALU.add)
                        else:
                            dve.wait_ge(sem("c_conv_d"), n - CT + 2)
                            ins = dve.scalar_tensor_tensor(out=y[:, c, :], in0=src, scalar=tap[:, c, k:k + 1],
                                                           in1=y[:, c, :], op0=ALU.mult, op1=ALU.add)
                        ins.then_inc(sem("c_conv_d"), 1)
                        n += 1
                    if k % 4 == 3:
                        split(s + 3 + SPLIT + (k + 1) // 4)
                split(s + 10 + SPLIT)
                dve.wait_ge(sem("c_sum"), 1)
                dve.tensor_tensor(y[:], y[:], bank[6][:, SEQ:].unsqueeze(1).broadcast_to([P, CT, SEQ]), ALU.subtract)\
                   .then_inc(sem("c_centred"), 1)
                for i in range(2):
                    dve.wait_ge(sem("c_sd"), i + 1)
                    step(dve.reciprocal(crs[:], cmu[:]))
                    if i:
                        dve.wait_ge(sem("c_sq"), 2)
                    dve.tensor_tensor(y[:], y[:], crs[:].unsqueeze(1).broadcast_to([P, CT, SEQ]), ALU.mult)\
                       .then_inc(sem("c_scaled"), 1)
                dve.wait_ge(sem("c_hi"), 1)
                for c in range(CT):
                    ins = dve.scalar_tensor_tensor(out=xTlo[:, c, :], in0=y[:, c, :], scalar=chan[:, 3, c:c + 1],
                                                   in1=xThi[:, c, :].bitcast(F32), op0=ALU.mult, op1=ALU.subtract)
                ins.then_inc(sem("c_lo"), 1)
                dve.wait_ge(sem("m_mask"), 1)
                for h in range(H1):
                    dve.wait_ge(sem("at_S"), h + 1)
                    if h >= 2:
                        dve.wait_ge(sem("at_exp"), h - 1)
                    dve.scalar_tensor_tensor(out=p1[:, h % 2, 0:P], in0=bank[h % 2][:, 0:P], scalar=cum[:, 0, h:h + 1],
                                             in1=mask1[:, P:SEQ], op0=ALU.add, op1=ALU.add)
                    step(dve.scalar_tensor_tensor(out=p1[:, h % 2, P:384], in0=bank[h % 2][:, P:384],
                                                  scalar=cum[:, 1, h:h + 1], in1=mask1[:], op0=ALU.add, op1=ALU.add))
                    dve.tensor_reduce(mx[:, h % 2, 0:1], p1[:, h % 2, 0:P], AX_X, ALU.max)
                    step(dve.tensor_reduce(mx[:, h % 2, 1:2], p1[:, h % 2, P:384], AX_X, ALU.max))
                    dve.tensor_scalar(nmx[:, h % 2, :], mx[:, h % 2, :], -1.0, None, ALU.mult).then_inc(sem("at_nm"), 1)
                dve.wait_ge(sem("at_exp"), H1)
                step(dve.reciprocal(rinv[:], rsum[:]))
                dve.wait_ge(sem("at_pv"), H1)
                for t in range(NT):
                    dve.tensor_tensor(yA[:, t, :].rearrange("p (h c) -> p h c", h=H1),
                                      bank[4 + t][:].rearrange("p (h c) -> p h c", h=H1),
                                      rinv[:, t, :].unsqueeze(2).broadcast_to([P, H1, D1]), ALU.mult).then_inc(sem("a_y"), 1)
                for t in range(NT):
                    dve.wait_ge(sem("a_rs"), t + 1)
                    dve.scalar_tensor_tensor(out=yA[:, t, :], in0=yA[:, t, :], scalar=yrs[:, t:t + 1], in1=attn_gain[:],
                                             op0=ALU.mult, op1=ALU.mult).then_inc(sem("a_in"), 1)
                for t in range(NT):
                    dve.wait_ge(sem("a_hi"), t + 1)
                    dve.tensor_tensor(xTlo[:, CT:KD, t * P:(t + 1) * P], bank[t][:].rearrange("p (k c) -> p k c", k=4),
                                      xThi[:, CT:KD, t * P:(t + 1) * P].bitcast(F32), ALU.subtract).then_inc(sem("a_lo"), 1)

            def by_head(v, t, g):
                return vec[:, v, t, 4 * g:4 * g + 4].unsqueeze(2).broadcast_to([P, 4, P])

            def mixer2():
                s = first["gdn"]
                dve.wait_ge(sem("g_ab"), 1)
                z7 = bank[7][:, 0:4 * H2].rearrange("p (t h) -> p t h", t=NT)
                dve.tensor_tensor(zab[:, :, 0:H2], z7[:, :, 0:H2], dt_bias[:].unsqueeze(1).broadcast_to([P, NT, H2]), ALU.add)
                step(dve.tensor_copy(zab[:, :, H2:], z7[:, :, H2:]))
                dve.scalar_tensor_tensor(out=eab[:], in0=zab[:], scalar=-1.0, in1=zab[:], op0=ALU.mult, op1=ALU.min)\
                   .then_inc(sem("g_z"), 1)
                dve.wait_ge(sem("g_ln"), 1)
                dve.scalar_tensor_tensor(out=gl[:, :, H2:], in0=zab[:, :, H2:], scalar=0.0, in1=eab[:, :, H2:],
                                         op0=ALU.min, op1=ALU.subtract)
                step(dve.scalar_tensor_tensor(out=gl[:, :, 0:H2], in0=zab[:, :, 0:H2], scalar=0.0, in1=eab[:, :, 0:H2],
                                              op0=ALU.max, op1=ALU.add))
                dve.scalar_tensor_tensor(out=gl[:, :, 0:H2], in0=gl[:, :, 0:H2], scalar=-1.0,
                                         in1=a_log[:].unsqueeze(1).broadcast_to([P, NT, H2]), op0=ALU.mult, op1=ALU.mult)\
                   .then_inc(sem("g_g"), 1)
                dve.wait_ge(sem("g_zero"), 1)
                for b in range(6):
                    split(s + 2 * b + 1 + SPLIT)
                    dve.wait_ge(sem("g_u"), b + 1)
                    if b:
                        dve.wait_ge(*y4_free(b))
                    for k in range(W4):
                        for c in range(3):
                            w, src = tap4[:, 4 * b + c, k:k + 1], u4[:, c, k:k + SEQ]
                            if k == 0:
                                ins = dve.tensor_scalar(y4[:, c, :], src, w, None, ALU.mult)
                            else:
                                dve.wait_ge(sem("g_conv"), 3 * (W4 * b + k - 1) + c + 1)
                                ins = dve.scalar_tensor_tensor(out=y4[:, c, :], in0=src, scalar=w, in1=y4[:, c, :],
                                                               op0=ALU.mult, op1=ALU.add)
                            ins.then_inc(sem("g_conv"), 1)
                    split(s + 2 * b + 2 + SPLIT)
                dve.wait_ge(sem("g_lkq"), 1)
                dve.wait_ge(sem("g_cum_in"), 1)
                lq, lk, lb = lkq[:, :, 0:H2], lkq[:, :, H2:], gl[:, :, H2:]
                dve.scalar_tensor_tensor(out=vec[:, ROWQ], in0=lq, scalar=-0.5 * math.log(P), in1=vec[:, G_],
                                         op0=ALU.add, op1=ALU.add)
                dve.tensor_copy(vec[:, BETA], lb)
                dve.tensor_tensor(vec[:, TMP], lb, vec[:, G_], ALU.add)
                step(dve.tensor_tensor(vec[:, COL], lk, vec[:, G_], ALU.subtract))
                dve.tensor_tensor(vec[:, CVN], vec[:, COL], vec[:, GL], ALU.add)
                dve.tensor_tensor(vec[:, ROWA], vec[:, TMP], lk, ALU.add).then_inc(sem("g_vec"), 1)
                for b in range(2):
                    split(s + 12 + 2 * b + 1 + SPLIT)
                    dve.wait_ge(sem("g_gate"), b + 1)
                    for t in range(NT):
                        v = sg[:, t, b * 512:(b + 1) * 512].rearrange("p (h c) -> p h c", h=4)
                        dve.tensor_tensor(v, v, head_gain[:, GDNG:GDNG + 1, :].broadcast_to([P, 4, P]), ALU.mult)\
                           .then_inc(sem("g_sg"), 1)
                split(s + 16 + SPLIT)
                dve.wait_ge(sem("g_vexp"), 1)
                for t in range(NT):
                    for g in range(HG):
                        n = HG * t + g
                        dve.wait_ge(sem("g_vn"), n + 1)
                        dve.tensor_tensor(bv[:, t, g * 512:(g + 1) * 512].rearrange("p (h c) -> p h c", h=4),
                                          bank[n][:].rearrange("p (h c) -> p h c", h=4), by_head(BETA, t, g), ALU.mult)\
                           .then_inc(sem("g_bv"), 1)
                dve.wait_ge(sem("g_masks"), 1)
                for t in range(NT):
                    for g in range(HG):
                        for i in range(2):
                            n = 2 * (HG * t + g) + i
                            dve.wait_ge(sem("g_row"), n + 1)
                            dve.tensor_tensor(DG[i][:], bank[i][:].rearrange("p (h c) -> p h c", h=4),
                                              maskT[:].unsqueeze(1).broadcast_to([P, 4, P]), ALU.add).then_inc(sem("g_decm"), 1)
                            dve.wait_ge(sem("g_dec"), n + 1)
                            dve.wait_ge(sem("g_kq"), n + 1)
                            dst = AT if i == 0 else QKT
                            dve.tensor_tensor(dst[:, g, :, :], bank[2 + i][:].rearrange("p (h c) -> p h c", h=4), DEC[i][:],
                                              ALU.mult).then_inc(sem("g_AQ"), 1)
                    if t:
                        dve.wait_ge(sem("r_vn"), HG)
                    for g in range(HG):
                        for x in (T, U):
                            ins = dve.tensor_copy(x[:, g, :, :], ident[:].unsqueeze(1).broadcast_to([P, 4, P]))
                    ins.then_inc(sem("i_one"), 1)
                    dve.wait_ge(sem("i_one"), t + 1)
                    for l in range(7):
                        b = 2 ** l
                        for g in range(HG):
                            n = HG * (7 * t + l) + g
                            v = T[:, g, :, :].rearrange("p h (i j) -> p (h i) j", j=2 * b)[:, :, 0:b]
                            dve.wait_ge(sem("i_Z"), n + 1)
                            if l:
                                dve.wait_ge(sem("i_T"), n + 1 - HG)
                            dve.tensor_tensor(v, v, bank[2 * g + 1][:, 0:256].rearrange("p (n j) -> p n j", j=b), ALU.subtract)\
                               .then_inc(sem("i_T"), 1)
                    for g in range(HG):
                        n = HG * t + g
                        if t:
                            dve.wait_ge(sem("r_kS"), g + 1)
                            step(dve.tensor_tensor(tq[:], bank[4 + g][:].rearrange("p (h c) -> p h c", h=4), by_head(CKS, t, g), ALU.mult))
                            if g:
                                dve.wait_ge(sem("r_vn"), n)
                            dve.tensor_tensor(r2[:], bv[:, t, g * 512:(g + 1) * 512].rearrange("p (h c) -> p h c", h=4), tq[:],
                                              ALU.subtract).then_inc(sem("r_r"), 1)
                            dve.wait_ge(sem("r_qS"), g + 1)
                            step(dve.tensor_tensor(vne[:], bank[0][:].rearrange("p (h c) -> p h c", h=4), by_head(CQS, t, g), ALU.mult))
                            dve.wait_ge(sem("r_o"), n + 1)
                            dve.tensor_tensor(o2[:, t, g * 512:(g + 1) * 512], bank[2][:], vne[:].rearrange("p h c -> p (h c)"), ALU.add)\
                               .then_inc(sem("r_o1"), 1)
                        else:
                            dve.wait_ge(sem("r_vn_in"), n + 1)
                            if g:
                                dve.wait_ge(sem("r_S"), g)
                            dve.tensor_tensor(vne[:], vn[:], by_head(CVN, t, g), ALU.mult).then_inc(sem("r_vne"), 1)
                for t in range(NT):
                    dve.wait_ge(sem("g_osq"), t + 1)
                    dve.tensor_reduce(oss[:, t, :], bv[:, 0, :].rearrange("p (h c) -> p h c", h=H2), AX_X, ALU.add)\
                       .then_inc(sem("g_oss"), 1)
                dve.wait_ge(sem("g_sg"), 4)
                for t in range(NT):
                    dve.wait_ge(sem("g_ors"), t + 1)
                    v = o2[:, t, :].rearrange("p (h c) -> p h c", h=H2)
                    step(dve.tensor_tensor(v, v, ors[:, t, :].unsqueeze(2).broadcast_to([P, H2, P]), ALU.mult))
                    dve.tensor_tensor(o2[:, t, :], o2[:, t, :], sg[:, t, :], ALU.mult).then_inc(sem("turn_in"), 1)
                for t in range(NT):
                    turn_lo("gdn", t)

            def embed(i, n):
                add = residual(("down2", "down3")[i], (1.0, 1.0)[i])
                add(0)
                dve.wait_ge(sem("p_hi"), i + 1)
                dve.tensor_tensor(pTlo[:].rearrange("p k t -> p (k t)"), bank[0][:],
                                  pThi[:].rearrange("p k t -> p (k t)").bitcast(F32), ALU.subtract).then_inc(sem("p_lo"), 1)
                split(first[f"ple_p{i}"] + SPLIT)
                norm(n, f"ple_g{i}", before=lambda t: add(t) if t else None)
                split(last_group(f"ple_g{i}") + SPLIT)

                def add_gated(t):
                    dve.wait_ge(sem("gate_s"), 2 * i + t + 1)
                    dve.wait_ge(sem("pp_in"), 2 * i + t + 1)
                    step(dve.tensor_tensor(gate_s[:, t, :], gate_s[:, t, :], pp[:, t, :], ALU.mult))
                    dve.tensor_tensor(X[:, t, :], X[:, t, :], gate_s[:, t, :], ALU.add).then_inc(sem("x_ready"), 1)
                return add_gated

            def head_norm(i, t, g_):
                dve.wait_ge(sem("s_krs"), 2 * i + t + 1)
                v = kn[:, t, :].rearrange("p (h c) -> p h c", h=H2)
                w = xs[:, t, :].rearrange("p (h c) -> p h c", h=H2)
                if i:
                    dve.wait_ge(sem("s_kT"), 4)
                else:
                    dve.wait_ge(sem("turn_T"), 4 * turn("n8") + 4)
                step(dve.tensor_tensor(w, v, krs[:, i, t, :].unsqueeze(2).broadcast_to([P, H2, P]), ALU.mult))
                dve.tensor_tensor(w, w, head_gain[:, g_:g_ + 1, :].broadcast_to([P, H2, P]), ALU.mult).then_inc(sem("s_rows"), 1)

            def mixer3(add):
                s = first["kv"]
                norm(7, "kv", before=add)
                for b in range(4):
                    split(s + 2 * b + 1 + SPLIT)
                    if b == 0:
                        norm(8, None, xThi2, xTlo2)
                    if b == 1:
                        split(s + 2 * b + 2 + SPLIT)
                        for t in range(NT):
                            dve.wait_ge(sem("s_sq"), t + 1)
                            dve.tensor_reduce(kss[:, 0, t, :], sq_s[:].rearrange("p (h c) -> p h c", h=H2), AX_X, ALU.add)\
                               .then_inc(sem("s_kss"), 1)
                        for t in range(NT):
                            head_norm(0, t, KG)
                        dve.tensor_scalar(head_gain[:, QG, :], head_gain[:, QG, :], P ** -0.5, None, ALU.mult).then_inc(sem("s_qg"), 1)
                s = first["sbq"]
                split(s + 4 + SPLIT)
                for t in range(NT):
                    dve.wait_ge(sem("s_sq"), 2 + t + 1)
                    dve.tensor_reduce(kss[:, 1, t, :], sq_s[:].rearrange("p (h c) -> p h c", h=H2), AX_X, ALU.add)\
                       .then_inc(sem("s_kss"), 1)
                dve.wait_ge(sem("s_qg"), 1)
                for t in range(NT):
                    head_norm(1, t, QG)
                dve.wait_ge(sem("s_masks"), 1)
                for h in range(H2 + 1):
                    if h < H2:
                        dve.wait_ge(sem("sb_ln"), h + 1)
                        if h >= 2:
                            dve.wait_ge(sem("sb_sfx"), h - 1)
                        step(dve.scalar_tensor_tensor(out=spl[:, h % 2, :], in0=bank[h % 2][:, 0:384], scalar=0.0,
                                                      in1=sab[:, h % 2, :], op0=ALU.max, op1=ALU.add))
                        dve.tensor_tensor(spl[:, h % 2, :], spl[:, h % 2, :], smask[:], ALU.mult).then_inc(sem("sb_sp"), 1)
                    if h:
                        g = h - 1
                        dve.wait_ge(sem("sb_sfx"), g + 1)
                        if g >= 2:
                            dve.wait_ge(sem("sb_pv"), g - 1)
                        dve.tensor_tensor(sw[:, g % 2, :], bank[g % 2][:, 0:384], sbig[:], ALU.add).then_inc(sem("sb_lw"), 1)
                for t in range(NT):
                    turn_lo("sb", t)

            norm(0, "up0")
            ffn(0)
            add = residual("down0", 0.5)
            norm(1, "mix", before=add)
            mixer1()
            add = residual("mix_out", 1.0)
            norm(2, "up1", before=add)
            ffn(1)
            add = residual("down1", 0.5)
            for t in range(NT):
                add(t)
                norm_scale(3, t)
            for t in range(NT):
                norm_scale(4, t)
                turn_lo("n4", t)
                if t == 0:
                    split(first["gdn"] + 2)
            mixer2()
            add = residual("gdn_out", 1.0)
            norm(5, "up2", before=add)
            ffn(2)
            add = embed(0, 6)
            mixer3(add)
            add = residual("sb_out", 1.0)
            norm(9, "up3", before=add)
            ffn(3)
            add = embed(1, 10)
            for t in range(NT):
                add(t)

        @block.tensor
        def _(pe):
            xT, hT, pT, xT2 = (xThi, xTlo), (hThi, hTlo), (pThi, pTlo), (xThi2, xTlo2)

            def passes(psum, lhs, rhs, start, stop):
                pe.matmul(psum, lhs[0], rhs[0], start=start, stop=False, skip_group_check=True)
                pe.matmul(psum, lhs[0], rhs[1], start=False, stop=False, skip_group_check=True)
                return pe.matmul(psum, lhs[1], rhs[0], start=False, stop=stop, skip_group_check=True)

            def ring(w):
                return whi[w % SPLIT], wlo[w % SPLIT]

            def rows(w, t, src, k0, nk, psums, k_last):
                for k in range(nk):
                    for c, psum in enumerate(psums):
                        at = (k * len(psums) + c) * 512
                        ins = passes(psum[:], [x[:, k0 + k, t * P:(t + 1) * P] for x in src],
                                     [x[:, at:at + 512] for x in ring(w)], k0 + k == 0, k0 + k == k_last)
                return ins

            def turn_T(name, t, wait=None):
                pe.wait_ge(*(wait or (sem("turn_in"), turned_in(name, t))))
                for b in range(2):
                    before = 4 * turn(name) + 2 * t + b - 1
                    if before > 0:
                        pe.wait_ge(sem("turn_lo"), before)
                    for k in range(4):
                        ins = pe.transpose(bank[4 + b][:, k * P:(k + 1) * P],
                                           xs[:, t, (4 * b + k) * P:(4 * b + k + 1) * P], ident[:])
                    ins.then_inc(sem("turn_T"), 1)

            def turned(name, t):
                pe.wait_ge(sem("turn_lo"), 4 * turn(name) + 2 * t + 2)

            def wide(name, src, ready=None, middle=None):
                s, n = first[name], wide_slots[name]
                for i in range(n - SPLIT):
                    pe.wait_ge(w_lo, s + i + 1)
                    if ready:
                        ready(i)
                    for t in range(NT):
                        ins = rows(s + i, t, src, 2 * i, 2, [out_bank(t, 0), out_bank(t, 1)], 2 * n - 1)
                    ins.then_inc(w_used, 1)
                for t in range(NT):
                    for i in range(n - SPLIT, n):
                        if t == 0:
                            pe.wait_ge(w_lo, s + i + 1)
                            if ready:
                                ready(i)
                        elif i == n - 1 and middle:
                            middle()
                        ins = rows(s + i, t, src, 2 * i, 2, [out_bank(t, 0), out_bank(t, 1)], 2 * n - 1)
                        if t == NT - 1:
                            ins.then_inc(w_used, 1)
                    if t == 0:
                        ins.then_inc(sem("wide_mm0"), 1)

            def block_rows(s, src, banks, k_ready=None, tilewise=False, done0=None, free=None):
                order = [(h, t) for h in range(2) for t in range(NT)]
                if tilewise:
                    order.sort(key=lambda x: x[1])
                seen = set()
                for h, t in order:
                    if h == 0 and k_ready:
                        k_ready(t)
                    if h not in seen:
                        pe.wait_ge(w_lo, s + h + 1)
                        seen.add(h)
                    if h == 0 and free:
                        free(t)
                    ins = rows(s + h, t, src, 4 * h, 4, [banks[t]], KD - 1)
                    if h == 1 and t == 0 and done0:
                        ins.then_inc(sem(done0), 1)
                    if t == NT - 1:
                        ins.then_inc(w_used, 1)

            def block_cols(s, src, banks, k_ready=None):
                tiles = [slice(0, SEQ)] if k_ready is None else [slice(t * P, (t + 1) * P) for t in range(NT)]
                for t, tok in enumerate(tiles):
                    for h in range(2):
                        if h == 0 and k_ready:
                            k_ready(t)
                        if t == 0:
                            pe.wait_ge(w_lo, s + h + 1)
                        for k in range(4):
                            for c in range(4):
                                at = k * 512 + c * P
                                off = (c % 2) * SEQ
                                ins = passes(banks[c // 2][:, off + tok.start:off + tok.stop],
                                             [x[:, at:at + P] for x in ring(s + h)],
                                             [x[:, 4 * h + k, tok] for x in src],
                                             t == 0 and h == 0 and k == 0 and c % 2 == 0, h == 1 and k == 3)
                        if t == len(tiles) - 1:
                            ins.then_inc(w_used, 1)

            def narrow_rows(psum, c0, n, src):
                for t in range(NT):
                    for k in range(KD):
                        ins = passes(psum[:, t * n:(t + 1) * n], [x[:, k, t * P:(t + 1) * P] for x in src],
                                     [x[:, k, c0:c0 + n] for x in (narrow_hi, narrow_lo)], t == 0 and k == 0, k == KD - 1)
                return ins

            def tile_ready(name):
                def ready(t):
                    if t:
                        turn_T(name, t)
                    turned(name, t)
                return ready

            def ffn(f):
                def hidden_T(j):
                    pe.wait_ge(sem("ffn_h"), 2 * (NBLK * f + j) + 2)
                    if j >= 2:
                        pe.wait_ge(sem("ffn_lo"), NBLK * f + j - 1)
                    for k in range(2):
                        for t in range(NT):
                            ins = pe.transpose(bank[4 + j % 2][:, k * SEQ + t * P:k * SEQ + (t + 1) * P],
                                               hnat[:, j % 2, t, k * P:(k + 1) * P], ident[:])
                    ins.then_inc(sem("ffn_T"), 1)

                name = turn_of_up[f]
                for j in range(NBLK):
                    block_rows(first[f"up{f}"] + 2 * j, xT, [bank[2 * (j % 2) + t] for t in range(NT)],
                               k_ready=tile_ready(name) if j == 0 else None, tilewise=j == 0, done0="ffn_mm0",
                               free=(lambda t: pe.wait_ge(sem("ffn_h"), 2 * (NBLK * f + j - 2) + t + 1)) if j >= 2 else None)
                    if j:
                        hidden_T(j - 1)
                    if f == 0 and j == 2:
                        setup()

                def ready(i):
                    if i == 1:
                        hidden_T(NBLK - 1)
                    if i == 2 and f >= 2:
                        p_turn(f - 2)
                    if i == 0:
                        if f == 0:
                            pe.wait_ge(sem("m_tap"), 1)
                        pe.wait_ge(sem("ffn_h"), 2 * (NBLK * f + NBLK - 2) + 2)
                    pe.wait_ge(sem("ffn_lo"), NBLK * f + i + 1)
                return ready

            def setup():
                pe.wait_ge(sem("consts_in"), 16 * N_LOADS)
                pe.transpose(bank[7][:, 0:4 * CT], row_chan[:], ident[0:4 * CT, 0:4 * CT])
                for c in range(CT):
                    pe.transpose(bank[7][:, 16 + c * TAPS:16 + (c + 1) * TAPS], row_tap[:, c * P:(c + 1) * P],
                                 ident[0:TAPS, 0:TAPS])
                for c in range(QKV):
                    ins = pe.transpose(bank[7][:, 160 + c * W4:160 + (c + 1) * W4], row_tap4[:, c * P:(c + 1) * P],
                                       ident[0:W4, 0:W4])
                ins.then_inc(sem("setup_T"), 1)

            def mixer1():
                s = first["mix"]
                block_cols(s, xT, [bank[0], bank[1]], tile_ready("n1"))
                pe.wait_ge(sem("x_ready"), 2)
                block_cols(s + 2, xT, [bank[2], bank[3]])
                pe.wait_ge(sem("narrow_lo"), 1)
                narrow_rows(bank[6], 0, H1, xT).then_inc(sem("m_fl"), 1)
                pe.wait_ge(sem("m_u"), 1)
                block_cols(s + 4, xT, [bank[0], bank[1]])
                pe.wait_ge(sem("m_lf"), 1)
                pe.matmul(bank[6][:, 32:32 + H1], upto[:], lf[:, 0, :], start=True, stop=True)
                pe.matmul(bank[6][:, 32 + H1:32 + 2 * H1], ones[:], lf[:, 0, :], start=True, stop=False)
                pe.matmul(bank[6][:, 32 + H1:32 + 2 * H1], upto[:], lf[:, 1, :], start=False, stop=True).then_inc(sem("m_cum"), 1)
                block_cols(s + 6, xT, [bank[2], bank[3]])
                pe.wait_ge(sem("m_q"), 1)
                block_rows(s + 8, xT, [bank[0], bank[1]])

                def channel_sum(psum, src):
                    for c in range(CT):
                        ins = pe.matmul(psum, mean_of[:], src[:, c, :], start=c == 0, stop=c == CT - 1)
                    ins.then_inc(sem("c_sum"), 1)
                pe.wait_ge(sem("c_conv_d"), (CT - 1) * TAPS)
                pe.wait_ge(sem("pool_sum"), TAPS)
                pe.wait_ge(sem("m_cum_in"), 1)
                channel_sum(bank[6][:, SEQ:], y)
                pe.wait_ge(sem("c_sq"), 1)
                channel_sum(bank[7][:, 0:SEQ], ysq)
                pe.wait_ge(sem("c_sq"), 2)
                channel_sum(bank[7][:, 0:SEQ], ysq)
                pe.wait_ge(sem("m_mask"), 1)
                pe.wait_ge(sem("m_v"), 1)
                for i in range(H1 + 2):
                    if i < H1:
                        h = i
                        pe.wait_ge(sem("at_dg"), h + 1)
                        if h >= 2:
                            pe.wait_ge(sem("at_nm"), h - 1)
                        S_ = bank[h % 2]
                        for t in range(NT):
                            c = slice(0, P) if t == 0 else slice(P, 384)
                            n = P * (t + 1)
                            pe.matmul(S_[:, c], qz[:, h, t * P:(t + 1) * P], kT[:, h // 2, 0:n], start=t == 0, stop=False,
                                      skip_group_check=True)
                            ins = pe.matmul(S_[:, c], minus1[:], dg1[:, h % 2, :, :].rearrange("p t k -> p (t k)")[:, 0:n],
                                            start=False, stop=True, skip_group_check=True)
                        ins.then_inc(sem("at_S"), 1)
                    if 1 <= i <= H1:
                        h = i - 1
                        pe.wait_ge(sem("at_exp"), h + 1)
                        if h >= 2:
                            pe.wait_ge(sem("at_pT"), h - 1)
                        for c in range(3):
                            ins = pe.transpose(bank[2 + h % 2][:, c * P:(c + 1) * P], p2[:, h % 2, c * P:(c + 1) * P], ident[:])
                        ins.then_inc(sem("at_T"), 1)
                    if i >= 2:
                        h = i - 2
                        pe.wait_ge(sem("at_pT"), h + 1)
                        o = slice(h * D1, (h + 1) * D1)
                        pe.matmul(bank[4][:, o], pT1[:, h % 2, 0:P], v1[:, 0, o], start=True, stop=True)
                        pe.matmul(bank[5][:, o], pT1[:, h % 2, P:2 * P], v1[:, 0, o], start=True, stop=False)
                        pe.matmul(bank[5][:, o], pT1[:, h % 2, 2 * P:], v1[:, 1, o], start=False, stop=True).then_inc(sem("at_pv"), 1)
                for t in range(NT):
                    pe.wait_ge(sem("a_in"), t + 1)
                    for k in range(4):
                        ins = pe.transpose(bank[t][:, k * P:(k + 1) * P], yA[:, t, k * P:(k + 1) * P], ident[:])
                    ins.then_inc(sem("a_T"), 1)

                def ready(i):
                    if i == 0:
                        pe.wait_ge(sem("c_lo"), 1)
                        pe.wait_ge(sem("at_pT"), H1)
                    if i == CT // 2:
                        pe.wait_ge(sem("a_lo"), NT)
                return ready

            def mixer2():
                s = first["gdn"]

                def both_ready(t):
                    turn_T("n4", t)
                    turned("n4", t)

                def squares(b):
                    pe.wait_ge(sem("g_sq"), b + 1)
                    for c in range(4):
                        for t in range(NT):
                            col = t * 2 * H2 + 4 * b + c
                            ins = pe.matmul(bank[6][:, col:col + 1], sq4[:, c, t * P:(t + 1) * P], ones[:, 0:1], start=True, stop=True)
                    ins.then_inc(sem("g_ss"), 1)
                for b in range(6):
                    if b >= 2:
                        pe.wait_ge(sem("g_u"), b - 1)
                    block_cols(s + 2 * b, xT, [bank[2 * (b % 2)], bank[2 * (b % 2) + 1]], both_ready if b == 0 else None)
                    if b == 0:
                        narrow_rows(bank[7], H1, 2 * H2, xT).then_inc(sem("g_ab"), 1)
                    if b == 1:
                        pe.wait_ge(sem("g_g"), 1)
                        for t in range(NT):
                            pe.matmul(bank[7][:, 64 + t * H2:64 + (t + 1) * H2], upto[:], gl[:, t, 0:H2], start=True, stop=True)
                            ins = pe.matmul(bank[7][:, 80 + t * H2:80 + (t + 1) * H2], ones[:], gl[:, t, 0:H2], start=True, stop=True)
                        ins.then_inc(sem("g_cum"), 1)
                    if 1 <= b <= 4:
                        squares(b - 1)
                for b in range(2):
                    pe.wait_ge(sem("g_u"), 5 + b)
                    block_rows(s + 12 + 2 * b, xT, [bank[2 * b], bank[2 * b + 1]])
                for g in range(HG):
                    for h in range(4):
                        ins = pe.transpose(bank[4 + g][:, h * P:(h + 1) * P], qkT[:, H2 + 4 * g + h, 0:P], ident[:])
                    ins.then_inc(sem("g_kn"), 1)
                pe.wait_ge(sem("g_gate"), 2)
                pe.wait_ge(sem("g_v"), 2)
                for t in range(NT):
                    for g in range(HG):
                        for h in range(4):
                            ins = pe.transpose(bank[HG * t + g][:, h * P:(h + 1) * P], vT[:, 4 * g + h, t * P:(t + 1) * P], ident[:])
                        ins.then_inc(sem("g_vn"), 1)
                pe.wait_ge(sem("g_bv"), 2 * HG)
                pe.wait_ge(sem("g_knat"), HG)

                for t in range(NT):
                    tok = slice(t * P, (t + 1) * P)
                    if t:
                        pe.wait_ge(sem("r_S_in"), HG)
                    for g in range(HG):
                        for i in range(2):
                            n = 2 * (HG * t + g) + i
                            pe.wait_ge(sem("g_dg"), n + 1)
                            if n >= 2:
                                pe.wait_ge(sem("g_AQ"), n - 1)
                            pe.matmul(bank[i][:], ones[:], DG[i][:].rearrange("p h c -> p (h c)"), start=True, stop=True)\
                              .then_inc(sem("g_row"), 1)
                            off = H2 if i == 0 else 0
                            for h in range(4):
                                ins = pe.matmul(bank[2 + i][:, h * P:(h + 1) * P], qkT[:, H2 + 4 * g + h, tok],
                                                qkT[:, off + 4 * g + h, tok], start=True, stop=True)
                            ins.then_inc(sem("g_kq"), 1)
                    pe.wait_ge(sem("i_one"), t + 1)
                    pe.wait_ge(sem("g_AQ"), 4 * (t + 1))
                    for l in range(7):
                        b = 2 ** l
                        for g in range(HG):
                            n = HG * (7 * t + l) + g
                            pe.wait_ge(sem("i_L"), n + 1)
                            if l:
                                pe.wait_ge(sem("i_T"), n + 1 - HG)
                            for h in range(4):
                                ins = pe.matmul(bank[2 * g][:, h * 64:(h + 1) * 64].rearrange("p (i j) -> p i j", j=b),
                                                Lm[:, g, h, :], T[:, g, h, :].rearrange("p (i j) -> p i j", j=2 * b)[:, :, 0:b],
                                                start=True, stop=True)
                            ins.then_inc(sem("i_Y"), 1)
                        for g in range(HG):
                            n = HG * (7 * t + l) + g
                            pe.wait_ge(sem("i_Y_in"), n + 1)
                            if l:
                                pe.wait_ge(sem("i_U"), n + 1 - HG)
                            for h in range(4):
                                ins = pe.matmul(bank[2 * g + 1][:, h * 64:(h + 1) * 64], U[:, g, h, :], Y[:, g, h, :],
                                                start=True, stop=True)
                            ins.then_inc(sem("i_Z"), 1)
                        for g in range(HG):
                            n = HG * (7 * t + l) + g
                            pe.wait_ge(sem("i_T"), n + 1)
                            for h in range(4):
                                ins = pe.transpose(bank[4 + g][:, h * P:(h + 1) * P], T[:, g, h, :], ident[:])
                            ins.then_inc(sem("i_TT"), 1)
                    pe.wait_ge(sem("i_U"), HG * 7 * (t + 1))
                    for g in range(HG):
                        n = HG * t + g
                        cols = lambda h: slice((4 * g + h) * P, (4 * g + h + 1) * P)
                        if t:
                            for h in range(4):
                                ins = pe.matmul(bank[4 + g][:, h * P:(h + 1) * P], qkT[:, H2 + 4 * g + h, tok], S[:, 4 * g + h, :],
                                                start=True, stop=True)
                            ins.then_inc(sem("r_kS"), 1)
                            if g:
                                pe.wait_ge(sem("r_o1"), g)
                            for h in range(4):
                                ins = pe.matmul(bank[0][:, h * P:(h + 1) * P], qkT[:, 4 * g + h, tok], S[:, 4 * g + h, :],
                                                start=True, stop=True)
                            ins.then_inc(sem("r_qS"), 1)
                            pe.wait_ge(sem("r_r"), g + 1)
                        if g:
                            pe.wait_ge(sem("r_vn_in"), n)
                        for h in range(4):
                            ins = pe.matmul(bank[1][:, h * P:(h + 1) * P], U[:, g, h, :], r2[:, h, :] if t else bv[:, 0, cols(h)],
                                            start=True, stop=True)
                        ins.then_inc(sem("r_vn"), 1)
                        pe.wait_ge(sem("r_vn_in"), n + 1)
                        if g:
                            pe.wait_ge(sem("r_o1" if t else "r_o_in"), g)
                        for h in range(4):
                            ins = pe.matmul(bank[2][:, h * P:(h + 1) * P], QKT[:, g, h, :], vn[:, h, :], start=True, stop=True)
                        ins.then_inc(sem("r_o"), 1)
                        if t == 0:
                            pe.wait_ge(sem("r_vne"), g + 1)
                            if g:
                                pe.wait_ge(sem("r_S_in"), g)
                            for h in range(4):
                                ins = pe.matmul(bank[3][:, h * P:(h + 1) * P], knat[:, 4 * g + h, :], vne[:, h, :],
                                                start=True, stop=True)
                            ins.then_inc(sem("r_S"), 1)
                for t in range(NT):
                    turn_T("gdn", t)

                def ready(i):
                    if i == 0:
                        for t in range(NT):
                            turned("gdn", t)
                        pe.wait_ge(sem("r_o1"), HG)
                return ready

            def p_turn(i):
                pe.wait_ge(sem("p_in"), 32 * (i + 1))
                for k in range(2):
                    for t in range(NT):
                        ins = pe.transpose(bank[0][:, k * SEQ + t * P:k * SEQ + (t + 1) * P], p_in[:, t, k * P:(k + 1) * P], ident[:])
                ins.then_inc(sem("p_T"), 1)

            def embed(i, n):
                s = first[f"ple_p{i}"]
                pe.wait_ge(sem("p_lo"), i + 1)
                pe.wait_ge(w_lo, s + 1)
                for t in range(NT):
                    ins = rows(s, t, pT, 0, 2, [bank[(0, 1, 4, 5)[2 * t + h]] for h in range(2)], 1)
                    ins.then_inc(sem("pp_mm0") if t == 0 else w_used, 1)
                for t in range(NT):
                    if t == 0:
                        pe.wait_ge(sem("pp_in"), 2 * i + 2)
                    turn_T(f"n{n}", t)
                def ready(j):
                    if j == 0:
                        pe.wait_ge(sem("x_ready"), 2 * WIDE.index(f"ple_g{i}"))
                        for t in range(NT):
                            turned(f"n{n}", t)
                return ready

            def mixer3():
                s = first["kv"]
                for b in range(4):
                    if b >= 2:
                        pe.wait_ge(sem("s_kv"), b - 1)
                    block_rows(s + 2 * b, xT, [bank[2 * (b % 2) + t] for t in range(NT)],
                               k_ready=tile_ready("n7") if b == 0 else None, tilewise=b == 0)
                    if b == 0:
                        for t in range(NT):
                            turn_T("n8", t)
                def head_turn(i):
                    for t in range(NT):
                        pe.wait_ge(sem("s_rows"), 2 * i + t + 1)
                        for b in range(2):
                            if i == 0 and t == 0:
                                pe.wait_ge(sem("turn_lo"), 4 * turn("n8") + 4)
                            if 4 * i + 2 * t + b - 1 > 0:
                                pe.wait_ge(sem("s_kT_in"), 4 * i + 2 * t + b - 1)
                            for k in range(4):
                                ins = pe.transpose(bank[4 + b][:, k * P:(k + 1) * P], xs[:, t, (4 * b + k) * P:(4 * b + k + 1) * P],
                                                   ident[:])
                            ins.then_inc(sem("s_kT"), 1)
                head_turn(0)
                s = first["sbq"]
                for b in range(2):
                    pe.wait_ge(sem("s_kv"), 3 + b)
                    block_rows(s + 2 * b, xT2, [bank[2 * b + t] for t in range(NT)])
                head_turn(1)
                pe.wait_ge(sem("s_masks"), 1)
                pe.wait_ge(sem("s_q"), 2)
                pe.wait_ge(sem("s_kT_in"), 8)
                for i in range(H2 + 2):
                    if i < H2:
                        h = i
                        if h >= 2:
                            pe.wait_ge(sem("sb_lw"), h - 1)
                        z = bank[h % 2]
                        pe.matmul(z[:, 0:SEQ], skT[:, h, 0:P], sqT[:, h, :], start=True, stop=False, skip_group_check=True)
                        pe.matmul(z[:, SEQ:384], skT[:, h, P:], sqT[:, h, P:], start=False, stop=False, skip_group_check=True)\
                          .then_inc(sem("sb_z"), 1)
                    if 1 <= i <= H2:
                        h = i - 1
                        z, sp_ = bank[h % 2], spl[:, h % 2, :]
                        pe.wait_ge(sem("sb_sp"), h + 1)
                        pe.matmul(z[:, 0:SEQ], neg_tri[:], sp_[:, 0:SEQ], start=False, stop=False, skip_group_check=True)
                        pe.matmul(z[:, P:SEQ], neg_one[:], sp_[:, SEQ:], start=False, stop=True, skip_group_check=True)
                        pe.matmul(z[:, SEQ:384], neg_tri[:], sp_[:, SEQ:], start=False, stop=True, skip_group_check=True)\
                          .then_inc(sem("sb_sfx"), 1)
                    if i >= 2:
                        h = i - 2
                        pe.wait_ge(sem("sb_w"), h + 1)
                        pair = h // 2
                        if pair >= 2 and h % 2 == 0:
                            pe.wait_ge(sem("sb_o_in"), pair - 1)
                        o, c = bank[4 + pair % 2], (h % 2) * SEQ
                        v = [vs[:, t, h * P:(h + 1) * P] for t in range(NT)]
                        pe.matmul(o[:, c:c + P], sw[:, h % 2, 0:P], v[0], start=True, stop=True)
                        pe.matmul(o[:, c + P:c + SEQ], sw[:, h % 2, P:SEQ], v[0], start=True, stop=False)
                        ins = pe.matmul(o[:, c + P:c + SEQ], sw[:, h % 2, SEQ:], v[1], start=False, stop=True)
                        ins.then_inc(sem("sb_pv"), 1)
                for t in range(NT):
                    turn_T("sb", t, (sem("sb_o_in"), 4))

                def ready(i):
                    if i == 0:
                        for t in range(NT):
                            turned("sb", t)
                return ready

            def next_turn(name):
                return lambda: turn_T(name, 0)

            pe.wait_ge(sem("consts"), 1)
            turn_T("n0", 0)
            wide("down0", hT, ffn(0), next_turn("n1"))
            wide("mix_out", xT, mixer1(), next_turn("n2"))
            wide("down1", hT, ffn(1))
            wide("gdn_out", xT, mixer2(), next_turn("n5"))
            wide("down2", hT, ffn(2))
            wide("ple_g0", xT, embed(0, 6), next_turn("n7"))
            wide("sb_out", xT, mixer3(), next_turn("n9"))
            wide("down3", hT, ffn(3))
            wide("ple_g1", xT, embed(1, 10))
_INS = ["x", "ffn1_norm", "ffn1_w13", "ffn1_w2", "mix_norm", "w_in", "conv_w", "conv_b", "conv_ln_g", "conv_ln_b",
    "forget_b", "out_norm_conv", "out_norm_attn", "w_out", "ffn2_norm", "ffn2_w13", "ffn2_w2", "final_norm",
    "p_2", "ln_mix_2", "ln_ffn_2", "ln_ple_2", "gdn_w_in_2", "gdn_conv_2", "gdn_a_log_2", "gdn_dt_bias_2",
    "gdn_norm_2", "gdn_w_out_2", "kv_norm_2", "w_kv_2", "k_norm_2", "sb_w_q_2", "sb_q_norm_2", "sb_w_out_2",
    "ffn_w_in_2", "ffn_w_out_2", "ple_w_proj_2", "ple_w_gate_2"]
def kernel(**inputs):
    import numpy as _np
    import concourse.bacc as _bacc
    from concourse import mybir as _mybir
    from concourse.bass_utils import run_bass_kernel_spmd as _run
    nc = _bacc.Bacc("TRN2", target_bir_lowering=False, num_devices=1)
    arrays, args = {}, {}
    for name in _INS:
        v = _np.ascontiguousarray(inputs[name])
        arrays[f"in_{name}_dram"] = v
        args[name] = nc.dram_tensor(f"in_{name}_dram", v.shape, _mybir.dt.from_np(v.dtype), kind="ExternalInput").ap()
    out = nc.dram_tensor("out_0_dram", (1, 256, 1024), _mybir.dt.float32, kind="ExternalOutput").ap()
    build_program(nc, args, out)
    r = _run(nc, [arrays], core_ids=[0])
    return r.results[0]["out_0_dram"]
```

```python
from contextlib import ExitStack
import math

import concourse.bass as bass
from concourse import mybir

F32 = mybir.dt.float32
F32R = mybir.dt.float32r
ALU = mybir.AluOpType
ACT = mybir.ActivationFunctionType
AX_X = mybir.AxisListType.X

P = 128
EPS = 1e-6
BIG = 1e30


def build_program(nc, a, out):
    SEQ, D = a["x"].shape[1:]
    NT = SEQ // P
    KD = D // P
    KF = a["ffn1_w2"].shape[1] // P
    NBLK = KF // 2
    DC = a["conv_b"].shape[1]
    CT = DC // P
    TAPS = a["conv_w"].shape[1]
    PAD = TAPS - 1
    H1 = a["forget_b"].shape[1]
    D1 = DC // H1
    H2 = a["gdn_a_log_2"].shape[1]
    HG = H2 // 4
    W4 = a["gdn_conv_2"].shape[1]
    PAD4 = W4 - 1
    QKV = 3 * H2
    PLE = a["p_2"].shape[3]
    RAW, SPLIT = 4, 3
    SLOT = 4 * 512

    slots, first = [], {}

    def stream_gate_up(name, w):
        first[name] = len(slots)
        v = w.rearrange("(k p) (g n) -> p k g n", p=P, g=2)
        for j in range(NBLK):
            for h in range(2):
                slots.append([(("k", k), v[:, 4 * h + k, :, j * 256:(j + 1) * 256]) for k in range(4)])

    def stream_blocks(name, w, blocks):
        first[name] = len(slots)
        v = w.rearrange("(k p) n -> p k n", p=P)
        for c in blocks:
            for h in range(2):
                slots.append([(("rows", 4), v[:, 4 * h:4 * h + 4, c * 512:(c + 1) * 512])])

    def stream_wide(name, w, pairs=None):
        first[name] = len(slots)
        v = w.rearrange("(k p) n -> p k n", p=P)
        for s in pairs or range(w.shape[0] // (2 * P)):
            slots.append([(("rows", 2), v[:, 2 * s:2 * s + 2, :])])

    stream_gate_up("up0", a["ffn1_w13"][0])
    stream_wide("down0", a["ffn1_w2"][0])
    stream_blocks("mix", a["w_in"][0], (4, 0, 1, 2, 3))
    MIX_PAIRS = (2, 3, 0, 1)
    stream_wide("mix_out", a["w_out"][0], MIX_PAIRS)
    stream_gate_up("up1", a["ffn2_w13"][0])
    stream_wide("down1", a["ffn2_w2"][0])
    stream_blocks("gdn", a["gdn_w_in_2"][0], (6, 7, 0, 1, 2, 3, 4, 5))
    stream_wide("gdn_out", a["gdn_w_out_2"][0])
    stream_gate_up("up2", a["ffn_w_in_2"][0])
    stream_wide("down2", a["ffn_w_out_2"][0])
    stream_wide("ple_p0", a["ple_w_proj_2"][0])
    stream_wide("ple_g0", a["ple_w_gate_2"][0])
    stream_blocks("kv", a["w_kv_2"], (0, 1))
    stream_blocks("sbq", a["sb_w_q_2"][0], (0, 1))
    stream_blocks("sbv", a["w_kv_2"], (2, 3))
    stream_wide("sb_out", a["sb_w_out_2"][0])
    stream_gate_up("up3", a["ffn_w_in_2"][1])
    stream_wide("down3", a["ffn_w_out_2"][1])
    stream_wide("ple_p1", a["ple_w_proj_2"][1])
    stream_wide("ple_g1", a["ple_w_gate_2"][1])
    NSLOT = len(slots)

    WIDE = ["down0", "mix_out", "down1", "gdn_out", "down2", "ple_g0", "sb_out", "down3", "ple_g1"]
    wide_slots = {n: (KF if n[:4] == "down" else KD) // 2 for n in WIDE}

    NORM = [a["ffn1_norm"][0], a["mix_norm"][0], a["ffn2_norm"][0], a["final_norm"], a["ln_mix_2"][0],
            a["ln_ffn_2"][0], a["ln_ple_2"][0], a["kv_norm_2"], a["ln_mix_2"][1], a["ln_ffn_2"][1],
            a["ln_ple_2"][1]]
    FINAL = 3
    gain_before = {"up0": [0], "mix": [1], "up1": [2], "gdn": [3, 4], "up2": [5], "ple_p0": [6],
                   "kv": [7, 8], "up3": [9], "ple_p1": [10]}
    TURN = ["n0", "n1", "n2", "n4", "gdn", "n5", "n6", "n7", "n8", "sb", "n9", "n10"]
    turn_of_up = ["n0", "n2", "n5", "n9"]

    with ExitStack() as ctx:
        def sb(name, shape, dt=F32):
            return ctx.enter_context(nc.sbuf_tensor(name, shape, dt))

        made = {}

        def sem(name):
            if name not in made:
                made[name] = ctx.enter_context(nc.semaphore(name))
            return made[name]

        bank = [ctx.enter_context(nc.psum_tensor(f"bank{i}", [P, 512], F32)) for i in range(8)]
        raw = [sb(f"raw{i}", [P, SLOT]) for i in range(RAW)]
        whi = [sb(f"whi{i}", [P, SLOT], F32R) for i in range(SPLIT)]
        wlo = [sb(f"wlo{i}", [P, SLOT], F32R) for i in range(SPLIT)]
        X = sb("X", [P, NT, D])
        xs = sb("xs", [P, NT, D])
        xThi = sb("xThi", [P, KD, SEQ], F32R)
        xTlo = sb("xTlo", [P, KD, SEQ], F32R)
        gain = [sb(f"gain{i}", [P, D]) for i in range(2)]
        ident = sb("ident", [P, P])
        ones = sb("ones", [P, P])
        upto = sb("upto", [P, P])
        sumsq = sb("sumsq", [P, 2 * len(NORM)])
        meansq = sb("meansq", [P, 2 * len(NORM)])
        rstd = sb("rstd", [P, 2 * len(NORM)])
        eps_col = sb("eps_col", [P, 1])
        mean_of = sb("mean_of", [P, P])
        half = sb("half", [P, 16])
        chan = sb("chan", [P, 4, CT])
        tap = sb("tap", [P, CT, TAPS])
        tap4 = sb("tap4", [P, QKV, W4])
        attn_gain = sb("attn_gain", [P, DC])
        forget_b = sb("forget_b", [P, H1])
        narrow = sb("narrow", [P, KD, 24])
        narrow_hi = sb("narrow_hi", [P, KD, 24], F32R)
        narrow_lo = sb("narrow_lo", [P, KD, 24], F32R)
        a_log = sb("a_log", [P, H2])
        dt_bias = sb("dt_bias", [P, H2])
        head_gain = sb("head_gain", [P, 3, P])
        GDNG, KG, QG = range(3)

        def region(always, *turns):
            got = []
            with ExitStack() as phase:
                got += [phase.enter_context(nc.sbuf_tensor(n, s, d)) for n, s, d in always]
                for specs in turns:
                    with ExitStack() as turn:
                        got += [turn.enter_context(nc.sbuf_tensor(n, s, d)) for n, s, d in specs]
            return got

        hThi, hTlo, hnat, silu, p_in, pThi, pTlo, row_chan, row_tap, row_tap4 = region(
            [("hThi", [P, KF, SEQ], F32R), ("hTlo", [P, KF, SEQ], F32R),
             ("hnat", [P, 2, NT, 256], F32), ("silu", [P, 2, NT, 256], F32)],
            [("p_in", [P, NT, PLE], F32), ("pThi", [P, 2, SEQ], F32R), ("pTlo", [P, 2, SEQ], F32R)],
            [("row_chan", [4 * CT, P], F32), ("row_tap", [TAPS, DC], F32), ("row_tap4", [W4, QKV * P], F32)])
        pp, gate_s = region([("pp", [P, NT, D], F32), ("gate_s", [P, NT, D], F32)])
        (u, gs, y, ysq, stat, stat_r, qz, kT, v1, mask1, zf, zfe, lf, cum, cumT, p1, p2, pT1, mx, nmx, rsum, rinv, yA,
         yst, yms, yrs, pick, prod) = region([
            ("u", [P, CT, PAD + SEQ], F32), ("gs", [P, CT, SEQ], F32), ("y", [P, CT, SEQ], F32),
            ("ysq", [P, CT, SEQ], F32), ("stat", [P, 2, NT], F32), ("stat_r", [P, 2, NT], F32),
            ("qz", [P, H1, SEQ], F32), ("kT", [P, CT, SEQ], F32), ("v1", [P, NT, DC], F32),
            ("mask1", [P, SEQ], F32), ("zf", [P, NT, H1], F32), ("zfe", [P, NT, H1], F32),
            ("lf", [P, NT, H1], F32), ("cum", [P, NT, H1], F32), ("cumT", [H1, SEQ], F32),
            ("p1", [P, 2, 384], F32), ("p2", [P, 2, 384], F32), ("pT1", [P, 2, 384], F32),
            ("mx", [P, 2, 2], F32), ("nmx", [P, 2, 2], F32), ("rsum", [P, NT, H1], F32),
            ("rinv", [P, NT, H1], F32), ("yA", [P, NT, DC], F32), ("yst", [P, 2], F32), ("yms", [P, 2], F32),
            ("yrs", [P, 2], F32), ("pick", [H1, H1, P], F32), ("prod", [P, 3, 2, SEQ], F32)])
        (qkT, sg, zab, eab, gl, lkq, vec, knat, bv, dg, dec, AT, QKT, lvl, maskT, S, oss, oms, ors, v_or_TU, u4, y4,
         sq4) = region(
            [("qkT", [P, 2 * H2, SEQ], F32), ("sg", [P, NT, D], F32), ("zab", [P, NT, 2 * H2], F32),
             ("eab", [P, NT, 2 * H2], F32), ("gl", [P, NT, 2 * H2], F32), ("lkq", [P, NT, 2 * H2], F32),
             ("vec", [P, 10, NT, H2], F32), ("knat", [P, H2, P], F32), ("bv", [P, NT, D], F32),
             ("dg", [P, 4, P], F32), ("dec", [P, 4, P], F32), ("AT", [P, HG, 4, P], F32),
             ("QKT", [P, HG, 4, P], F32), ("lvl", [P, 7, P], F32), ("maskT", [P, P], F32), ("S", [P, H2, P], F32),
             ("oss", [P, NT, H2], F32), ("oms", [P, NT, H2], F32), ("ors", [P, NT, H2], F32),
             ("v_or_TU", [P, H2 * SEQ], F32), ("u4", [P, 4, PAD4 + SEQ], F32), ("y4", [P, 4, SEQ], F32),
             ("sq4", [P, 4, SEQ], F32)])
        vT = v_or_TU[:].rearrange("p (h t) -> p h t", h=H2)
        T, U = (v_or_TU[:, i * HG * 512:(i + 1) * HG * 512].rearrange("p (g h c) -> p g h c", g=HG, h=4) for i in range(2))
        (vs, kn, xThi2, xTlo2, skT, sqT, sab, sq_s, smask, sbig, neg_tri, neg_one, kss, kms, krs) = region([
            ("vs", [P, NT, D], F32), ("kn", [P, NT, D], F32), ("xThi2", [P, KD, SEQ], F32R), ("xTlo2", [P, KD, SEQ], F32R),
            ("skT", [P, H2, SEQ], F32), ("sqT", [P, H2, SEQ], F32), ("sab", [P, H2, 384], F32), ("sq_s", [P, D], F32),
            ("smask", [P, 384], F32), ("sbig", [P, P], F32),
            ("neg_tri", [P, P], F32), ("neg_one", [P, P], F32), ("kss", [P, 2, NT, H2], F32), ("kms", [P, 2, NT, H2], F32),
            ("krs", [P, 2, NT, H2], F32)])

        Lm = y4[:].rearrange("p h t -> p (h t)").rearrange("p (g h c) -> p g h c", g=HG, h=4)
        Y = u4[:].rearrange("p h t -> p (h t)")[:, 0:HG * 256].rearrange("p (g h c) -> p g h c", g=HG, h=4)
        vn = sq4[:, 0:2, :].rearrange("p a t -> p (a t)").rearrange("p (h c) -> p h c", h=4)
        vne = sq4[:, 2:4, :].rearrange("p a t -> p (a t)").rearrange("p (h c) -> p h c", h=4)
        DG, DEC = (dg, vn), (dec, vne)
        r2, tq = dg, dec
        o2 = xs
        prod4 = knat[:].rearrange("p h c -> p (h c)")[:, 0:3 * SEQ].rearrange("p (b t) -> p b t", b=3)
        G_, GL, ROWA, ROWQ, COL, CKS, CQS, CVN, BETA, TMP = range(10)

        raw_in = [sem(f"raw_in{i}") for i in range(RAW)]
        w_hi, w_lo, w_used = sem("w_hi"), sem("w_lo"), sem("w_used")

        def out_bank(t, h):
            return bank[(6, 7, 2, 3)[2 * t + h]]

        arrived, total = [], [0] * RAW
        for w, pieces in enumerate(slots):
            total[w % RAW] += 16 * len(pieces)
            arrived.append(total[w % RAW])

        def turn(name):
            return TURN.index(name)

        def turned_in(name, t):
            return 2 * [x for x in TURN if x != "sb"].index(name) + t + 1

        def nth(n, t):
            if n in (FINAL, FINAL + 1):
                return 2 * FINAL + 2 * t + n - FINAL + 1
            return 2 * (n - (n > 8)) + t + 1

        def last_group(name):
            return first[name] + wide_slots[name] - SPLIT

        N_LOADS = 15

        block = ctx.enter_context(nc.Block())

        @block.sync
        def _(sp):
            def load_consts():
                done = sem("consts_in")
                for i, name in enumerate(("conv_b", "conv_ln_g", "conv_ln_b", "out_norm_conv")):
                    sp.dma_start(row_chan[i * CT:(i + 1) * CT, :],
                                 a[name][0].rearrange("(c p) -> c p", p=P)).then_inc(done, 16)
                sp.dma_start(row_tap[:], a["conv_w"][0]).then_inc(done, 16)
                sp.dma_start(row_tap4[:], a["gdn_conv_2"][0]).then_inc(done, 16)
                sp.dma_start(attn_gain[:], a["out_norm_attn"][0].partition_broadcast(P)).then_inc(done, 16)
                sp.dma_start(forget_b[:], a["forget_b"][0].partition_broadcast(P)).then_inc(done, 16)
                sp.dma_start(a_log[:], a["gdn_a_log_2"][0].partition_broadcast(P)).then_inc(done, 16)
                sp.dma_start(dt_bias[:], a["gdn_dt_bias_2"][0].partition_broadcast(P)).then_inc(done, 16)
                sp.dma_start(head_gain[:, GDNG, :], a["gdn_norm_2"][0].partition_broadcast(P)).then_inc(done, 16)
                sp.dma_start(head_gain[:, KG, :], a["k_norm_2"].partition_broadcast(P)).then_inc(done, 16)
                sp.dma_start(head_gain[:, QG, :], a["sb_q_norm_2"][0].partition_broadcast(P)).then_inc(done, 16)
                sp.dma_start(narrow[:, :, 0:H1], a["w_in"][0].rearrange("(k p) n -> p k n", p=P)[:, :, 5 * 512:])\
                    .then_inc(done, 16)
                sp.dma_start(narrow[:, :, H1:H1 + 2 * H2],
                             a["gdn_w_in_2"][0].rearrange("(k p) n -> p k n", p=P)[:, :, 8 * 512:]).then_inc(done, 16)

            for w, pieces in enumerate(slots):
                for name, s0 in first.items():
                    if s0 != w:
                        continue
                    for n in gain_before.get(name, []):
                        if n - 2 == FINAL:
                            sp.wait_ge(sem("final_x"), NT)
                        elif n >= 2:
                            sp.wait_ge(sem("turn_in"), turned_in(f"n{n - 2}", 1))
                        sp.dma_start(gain[n % 2][:], NORM[n].partition_broadcast(P)).then_inc(sem(f"gain_in{n % 2}"), 16)
                    if name in ("down2", "down3"):
                        i = int(name[4]) - 2
                        if i:
                            sp.wait_ge(sem("p_T"), 1)
                        for t in range(NT):
                            sp.dma_start(p_in[:, t, :], a["p_2"][i, 0, t * P:(t + 1) * P, :]).then_inc(sem("p_in"), 16)
                if w == 0:
                    for t in range(NT):
                        sp.dma_start(X[:, t, :], a["x"][0, t * P:(t + 1) * P, :]).then_inc(sem(f"x_in{t}"), 16)
                if w == RAW:
                    load_consts()
                if w >= RAW:
                    sp.wait_ge(w_lo, w - RAW + 1)
                dst = raw[w % RAW]
                for (kind, k), src in pieces:
                    if kind == "rows":
                        view = dst[:].rearrange("p (k n) -> p k n", k=k)
                    else:
                        view = dst[:, k * 512:(k + 1) * 512].rearrange("p (g n) -> p g n", g=2)
                    sp.dma_start(view, src).then_inc(raw_in[w % RAW], 16)
            for t in range(NT):
                sp.wait_ge(sem("x_ready"), 2 * (len(WIDE) - 1) + t + 1)
                sp.dma_start(out[0, t * P:(t + 1) * P, :], X[:, t, :]).then_inc(sem("stored"), 16)
            sp.wait_ge(sem("stored"), 16 * NT)

        def wait_wide(eng, m, t):
            if t == 0:
                eng.wait_ge(sem("wide_mm0"), m + 1)
            else:
                eng.wait_ge(w_used, first[WIDE[m]] + wide_slots[WIDE[m]])

        def z_bank(h):
            return bank[(h + 2) % 8]

        @block.scalar
        def _(act):
            split_to = [0]
            steps = [0]

            def step(ins):
                steps[0] += 1
                ins.then_inc(sem("act_step"), 1)
                act.wait_ge(sem("act_step"), steps[0])

            def split(n):
                while split_to[0] < min(n, NSLOT):
                    w = split_to[0]
                    act.wait_ge(raw_in[w % RAW], arrived[w])
                    if w >= SPLIT:
                        act.wait_ge(w_used, w - SPLIT + 1)
                    act.activation(whi[w % SPLIT][:], raw[w % RAW][:], ACT.Copy).then_inc(w_hi, 1)
                    split_to[0] += 1

            def norm_sum(n, t, ready, value):
                act.wait_ge(ready, value)
                i = turn(f"n{max(n, 4) if n == FINAL else n}")
                if i:
                    act.wait_ge(sem("turn_T"), 4 * (i - 1) + 2 * t + 2)
                act.activation(xs[:, t, :], X[:, t, :], ACT.Square,
                               accum_out=sumsq[:, 2 * n + t:2 * n + t + 1]).then_inc(sem("norm_ss"), 1)

            def turn_hi(name, t, dst=None):
                dst = dst or xThi
                for b in range(2):
                    act.wait_ge(sem("turn_T"), 4 * turn(name) + 2 * t + b + 1)
                    act.activation(dst[:, 4 * b:4 * b + 4, t * P:(t + 1) * P],
                                   bank[4 + b][:].rearrange("p (k c) -> p k c", k=4),
                                   ACT.Copy).then_inc(sem("turn_hi"), 1)

            def norm(n, m, follows, dst=None, before=None):
                for t in range(NT):
                    if before:
                        before(t)
                    if m is None:
                        norm_sum(n, t, sem(f"x_in{t}"), 16)
                    elif n == FINAL + 1:
                        norm_sum(n, t, sem("final_x"), t + 1)
                    elif n != 8:
                        norm_sum(n, t, sem("x_ready"), 2 * m + t + 1)
                    if t == 0 and follows:
                        split(first[follows] + 1)
                    turn_hi(f"n{n}", t, dst)
                    if t == 0 and follows:
                        split(first[follows] + 2)

            def ffn(f):
                def hidden_hi(j):
                    act.wait_ge(sem("ffn_T"), NBLK * f + j + 1)
                    act.activation(hThi[:, 2 * j:2 * j + 2, :], bank[4 + j % 2][:].rearrange("p (k c) -> p k c", k=2),
                                   ACT.Copy).then_inc(sem("ffn_hi"), 1)

                for j in range(NBLK):
                    s = first[f"up{f}"] + 2 * j
                    split(s + (0 if j == 0 else 1) + SPLIT)
                    for t in range(NT):
                        if t == 0:
                            act.wait_ge(sem("ffn_mm0"), NBLK * f + j + 1)
                        else:
                            split(s + 1 + SPLIT)
                            act.wait_ge(w_used, s + 2)
                        if f or j >= 2:
                            act.wait_ge(sem("ffn_h"), 2 * (NBLK * f + j - 2) + t + 1)
                        act.activation(silu[:, j % 2, t, :], bank[2 * (j % 2) + t][:, 0:256],
                                       ACT.Silu).then_inc(sem("ffn_silu"), 1)
                    split(s + 2 + SPLIT)
                    if j:
                        hidden_hi(j - 1)
                    if f == 0 and j == 4:
                        act.wait_ge(sem("consts_in"), 16 * N_LOADS)
                        act.activation(narrow_hi[:], narrow[:], ACT.Copy).then_inc(sem("narrow_hi"), 1)
                split(first[f"down{f}"] + SPLIT)
                hidden_hi(NBLK - 1)

            def mixer1():
                s = first["mix"]
                taps = [0]

                def products(n):
                    for k in range(taps[0], min(taps[0] + n, TAPS)):
                        if k % 4 == 3:
                            continue
                        if k == 0:
                            act.wait_ge(sem("m_u"), 1)
                        if k >= 4:
                            act.wait_ge(sem("c_conv_p"), k - 3)
                        for i in range(2):
                            c = CT - 2 + i
                            src, w = u[:, c, k:k + SEQ], tap[:, c, k:k + 1]
                            if k == 0:
                                ins = act.activation(y[:, c, :], src, ACT.Identity, bias=chan[:, 0, c:c + 1], scale=w)
                            else:
                                ins = act.activation(prod[:, k % 3, i, :], src, ACT.Copy, scale=w)
                        ins.then_inc(sem("c_prod_a"), 1)
                    taps[0] = min(taps[0] + n, TAPS)

                split(s + 1 + SPLIT)
                act.wait_ge(w_used, s + 2)
                for t in range(NT):
                    ins = act.activation(v1[:, t, :], bank[t][:], ACT.Copy)
                ins.then_inc(sem("m_v"), 1)
                split(s + 5 + SPLIT)
                act.wait_ge(w_used, s + 6)
                for i in range(2):
                    ins = act.activation(gs[:, 2 * i:2 * i + 2, :].rearrange("p c t -> p (c t)"), bank[i][:], ACT.Sigmoid)
                ins.then_inc(sem("m_sig"), 1)
                split(s + 6 + SPLIT)
                act.wait_ge(sem("m_z"), 1)
                step(act.activation(zfe[:], zfe[:], ACT.Exp))
                act.activation(zfe[:], zfe[:], ACT.Ln, bias=1.0).then_inc(sem("m_ln"), 1)
                products(4)
                split(s + 7 + SPLIT)
                products(3)
                act.wait_ge(w_used, s + 8)
                act.wait_ge(sem("m_zero"), 2)
                for i in range(2):
                    for r in range(2):
                        rows = slice(r * D1, (r + 1) * D1)
                        ins = act.activation(qz[rows, 4 * i + r:4 * i + r + 3:2, :],
                                             bank[2 + i][rows, :].rearrange("p (c t) -> p c t", c=2), ACT.Copy, scale=D1 ** -0.5)
                ins.then_inc(sem("m_q"), 1)
                act.wait_ge(sem("m_cum"), 1)
                act.activation(cum[:].rearrange("p t h -> p (t h)"), bank[6][:, 32:32 + NT * H1], ACT.Copy).then_inc(sem("m_cum_in"), 1)
                split(s + 8 + SPLIT)
                products(4)
                split(s + 9 + SPLIT)
                products(4)
                act.wait_ge(w_used, s + 10)
                for i in range(2):
                    ins = act.activation(kT[:, 2 * i:2 * i + 2, :].rearrange("p c t -> p (c t)"), bank[i][:], ACT.Copy)
                ins.then_inc(sem("m_k"), 1)
                act.wait_ge(sem("m_cumT"), 1)
                act.activation(cumT[:], bank[6][0:H1, 128:128 + SEQ], ACT.Copy).then_inc(sem("m_cumT_in"), 1)
                split(s + 10 + SPLIT)
                for h in range(H1 + 2):
                    if h < H1:
                        act.wait_ge(sem("at_nm"), h + 1)
                        if h >= 2:
                            act.wait_ge(sem("at_T"), h - 1)
                        for t in range(NT):
                            c = slice(0, P) if t == 0 else slice(P, 384)
                            ins = act.activation(p2[:, h % 2, c], p1[:, h % 2, c], ACT.Exp, bias=nmx[:, h % 2, t:t + 1],
                                                 accum_out=rsum[:, t, h:h + 1])
                        ins.then_inc(sem("at_exp"), 1)
                    if h >= 2:
                        g = h - 2
                        act.wait_ge(sem("at_T"), g + 1)
                        if g >= 2:
                            act.wait_ge(sem("at_pv"), g - 1)
                        act.activation(pT1[:, g % 2, :], bank[2 + g % 2][:, 0:384], ACT.Copy).then_inc(sem("at_pT"), 1)
                    products(3)
                    if h == H1:
                        act.wait_ge(sem("c_centred"), 1)
                        act.activation(ysq[:], y[:], ACT.Square).then_inc(sem("c_sq"), 1)
                for t in range(NT):
                    act.wait_ge(sem("a_y"), t + 1)
                    act.activation(xs[:, t, 0:DC], yA[:, t, :], ACT.Square, accum_out=yst[:, t:t + 1]).then_inc(sem("a_ss"), 1)
                act.wait_ge(sem("c_scaled"), 1)
                for c in range(CT):
                    ins = act.activation(y[:, c, :], y[:, c, :], ACT.Silu, bias=chan[:, 2, c:c + 1], scale=chan[:, 1, c:c + 1])
                step(ins)
                act.activation(ysq[:], y[:], ACT.Square).then_inc(sem("c_sq"), 1)
                for t in range(NT):
                    act.wait_ge(sem("a_T"), t + 1)
                    act.activation(xThi[:, CT:KD, t * P:(t + 1) * P], bank[t][:].rearrange("p (k c) -> p k c", k=4),
                                   ACT.Copy).then_inc(sem("a_hi"), 1)
                act.wait_ge(sem("c_scaled"), 2)
                for c in range(CT):
                    ins = act.activation(xThi[:, c, :], y[:, c, :], ACT.Copy, scale=chan[:, 3, c:c + 1])
                ins.then_inc(sem("c_hi"), 1)
                split(last_group("mix_out") + SPLIT)

            def mixer2():
                s = first["gdn"]
                split(s + 1 + SPLIT)
                act.wait_ge(sem("g_z"), 1)
                act.activation(a_log[:], a_log[:], ACT.Exp)
                step(act.activation(eab[:], eab[:], ACT.Exp))
                act.activation(eab[:], eab[:], ACT.Ln, bias=1.0).then_inc(sem("g_ln"), 1)
                for b in range(2):
                    split(s + 2 * b + 1 + SPLIT)
                    act.wait_ge(w_used, s + 2 * b + 2)
                    for t in range(NT):
                        ins = act.activation(sg[:, t, b * 512:(b + 1) * 512], bank[2 * b + t][:], ACT.Silu)
                    ins.then_inc(sem("g_gate"), 1)
                    split(s + 2 * b + 2 + SPLIT)
                s += 4
                for b in range(6):
                    split(s + 2 * b + 1 + SPLIT)
                    act.wait_ge(w_used, s + 2 * b + 2)
                    if b:
                        act.wait_ge(sem("g_conv"), 3 * W4 * b)
                        act.wait_ge(sem("pool_sum"), W4 * b)
                    for i in range(2):
                        ins = act.activation(u4[:, 2 * i:2 * i + 2, PAD4:], bank[2 * (b % 2) + i][:].rearrange("p (c t) -> p c t", c=2),
                                             ACT.Copy)
                    ins.then_inc(sem("g_u"), 1)
                    if b == 0:
                        act.wait_ge(sem("g_cum"), 1)
                        act.activation(vec[:, G_:GL + 1, :, :].rearrange("p v t h -> p (v t h)"), bank[7][:, 64:64 + 4 * H2], ACT.Copy)\
                        .then_inc(sem("g_cum_in"), 1)
                    split(s + 2 * b + 2 + SPLIT)
                    act.wait_ge(sem("g_conv"), 3 * W4 * (b + 1))
                    act.wait_ge(sem("pool_sum"), W4 * (b + 1))
                    dst = qkT[:, 4 * b:4 * b + 4, :] if b < 4 else vT[:, 4 * (b - 4):4 * (b - 4) + 4, :]
                    ins = act.activation(dst, y4[:], ACT.Silu)
                    if b < 4:
                        step(ins)
                        if b:
                            act.wait_ge(sem("g_ss"), b)
                        act.activation(sq4[:], dst, ACT.Square).then_inc(sem("g_sq"), 1)
                    else:
                        ins.then_inc(sem("g_v"), 1)
                act.wait_ge(sem("g_ss"), 4)
                step(act.activation(lkq[:].rearrange("p t h -> p (t h)"), bank[6][:, 0:4 * H2], ACT.Ln, bias=eps_col[:, 0:1]))
                act.activation(lkq[:], lkq[:], ACT.Copy, scale=-0.5).then_inc(sem("g_lkq"), 1)
                act.wait_ge(sem("g_vec"), 1)
                act.activation(vec[:, CKS:CQS + 1, :, :], vec[:, ROWA:ROWQ + 1, :, :], ACT.Exp)
                act.activation(vec[:, CVN:BETA + 1, :, :], vec[:, CVN:BETA + 1, :, :], ACT.Exp).then_inc(sem("g_vexp"), 1)
                for g in range(HG):
                    act.wait_ge(sem("g_kn"), g + 1)
                    act.activation(knat[:, 4 * g:4 * g + 4, :].rearrange("p h c -> p (h c)"), bank[4 + g][:], ACT.Copy)\
                        .then_inc(sem("g_knat"), 1)
                for t in range(NT):
                    for g in range(HG):
                        for i in range(2):
                            n = 2 * (HG * t + g) + i
                            act.wait_ge(sem("g_decm"), n + 1)
                            for h in range(4):
                                ins = act.activation(DEC[i][:, h, :], DG[i][:, h, :], ACT.Exp,
                                                     bias=vec[:, COL, t, 4 * g + h:4 * g + h + 1])
                            ins.then_inc(sem("g_dec"), 1)
                    for l in range(7):
                        for g in range(HG):
                            n = HG * (7 * t + l) + g
                            act.wait_ge(sem("i_Y"), n + 1)
                            act.activation(Y[:, g, :, :].rearrange("p h c -> p (h c)"), bank[2 * g][:, 0:256], ACT.Copy)\
                                .then_inc(sem("i_Y_in"), 1)
                        for g in range(HG):
                            n = HG * (7 * t + l) + g
                            act.wait_ge(sem("i_TT"), n + 1)
                            act.activation(U[:, g, :, :].rearrange("p h c -> p (h c)"), bank[4 + g][:], ACT.Copy)\
                                .then_inc(sem("i_U"), 1)
                    for g in range(HG):
                        n = HG * t + g
                        act.wait_ge(sem("r_vn"), n + 1)
                        act.activation(vn[:].rearrange("p h c -> p (h c)"), bank[1][:], ACT.Copy).then_inc(sem("r_vn_in"), 1)
                        if t == 0:
                            act.wait_ge(sem("r_o"), n + 1)
                            act.activation(o2[:, 0, g * 512:(g + 1) * 512], bank[2][:], ACT.Copy).then_inc(sem("r_o_in"), 1)
                            act.wait_ge(sem("r_S"), g + 1)
                            act.activation(S[:, 4 * g:4 * g + 4, :].rearrange("p h c -> p (h c)"), bank[3][:], ACT.Copy)\
                                .then_inc(sem("r_S_in"), 1)
                for t in range(NT):
                    act.wait_ge(sem("r_o_in"), HG)
                    if t:
                        act.wait_ge(sem("r_o1"), HG)
                    if t:
                        act.wait_ge(sem("g_oss"), t)
                    act.activation(bv[:, 0, :], o2[:, t, :], ACT.Square).then_inc(sem("g_osq"), 1)
                for t in range(NT):
                    turn_hi("gdn", t)
                split(last_group("gdn_out") + SPLIT)

            def embed(i, m_before, n):
                act.wait_ge(sem("p_T"), i + 1)
                act.activation(pThi[:].rearrange("p k t -> p (k t)"), bank[0][:], ACT.Copy).then_inc(sem("p_hi"), 1)
                split(first[f"ple_p{i}"] + SPLIT)
                for t in range(NT):
                    if t == 0:
                        act.wait_ge(sem("pp_mm0"), i + 1)
                    else:
                        act.wait_ge(w_used, first[f"ple_p{i}"] + 1)
                    for h in range(2):
                        ins = act.activation(pp[:, t, h * 512:(h + 1) * 512], bank[(0, 1, 4, 5)[2 * t + h]][:], ACT.Copy)
                    ins.then_inc(sem("pp_in"), 1)
                norm(n, m_before, f"ple_g{i}")
                m = WIDE.index(f"ple_g{i}")
                split(last_group(f"ple_g{i}") + SPLIT)

                def gate(t):
                    wait_wide(act, m, t)
                    for h in range(2):
                        ins = act.activation(gate_s[:, t, h * 512:(h + 1) * 512], out_bank(t, h)[:], ACT.Sigmoid)
                    ins.then_inc(sem("gate_s"), 1)
                return gate

            def mixer3(gate):
                s = first["kv"]

                def evacuate(b, dst):
                    for t in range(NT):
                        ins = act.activation(dst[:, t, (b % 2) * 512:(b % 2 + 1) * 512], bank[2 * (b % 2 if b < 4 else 0) + t][:],
                                             ACT.Copy)
                    ins.then_inc(sem("s_kqv"), 1)

                def squares(i):
                    for t in range(NT):
                        if 2 * i + t:
                            act.wait_ge(sem("s_kss"), 2 * i + t)
                        act.wait_ge(sem("s_kqv"), 2 * i + 2)
                        act.activation(sq_s[:], kn[:, t, :], ACT.Square).then_inc(sem("s_sq"), 1)

                def turned_heads(i, dst):
                    for t in range(NT):
                        for b in range(2):
                            act.wait_ge(sem("s_kT"), 4 * i + 2 * t + b + 1)
                            act.activation(dst[:, 4 * b:4 * b + 4, t * P:(t + 1) * P],
                                           bank[4 + b][:].rearrange("p (k c) -> p k c", k=4), ACT.Copy).then_inc(sem("s_kT_in"), 1)

                def exp_abs(heads):
                    for h in heads:
                        act.wait_ge(sem("sb_z"), h + 1)
                        act.activation(sab[:, h, :], z_bank(h)[:, 0:384], ACT.Abs).then_inc(sem("sb_abs"), 1)
                    for h in heads:
                        act.wait_ge(sem("sb_abs"), h + 1)
                        act.activation(sab[:, h, :], sab[:, h, :], ACT.Exp, scale=-1.0).then_inc(sem("sb_exp"), 1)

                def ln(heads):
                    for h in heads:
                        act.wait_ge(sem("sb_exp"), h + 1)
                        act.activation(sab[:, h, :], sab[:, h, :], ACT.Ln, bias=1.0).then_inc(sem("sb_ln"), 1)

                def weights(heads):
                    for h in heads:
                        act.wait_ge(sem("sb_sfx"), h + 1)
                        act.activation(sab[:, h, :], z_bank(h)[:, 0:384], ACT.Exp).then_inc(sem("sb_w"), 1)

                norm(7, WIDE.index("ple_g0"), "kv", before=gate)
                split(s + 1 + SPLIT)
                act.wait_ge(w_used, s + 2)
                evacuate(0, kn)
                split(s + 2 + SPLIT)
                norm(8, WIDE.index("ple_g0"), None, xThi2)
                split(s + 3 + SPLIT)
                act.wait_ge(w_used, s + 4)
                evacuate(1, kn)
                split(s + 4 + SPLIT)
                squares(0)
                split(s + 5 + SPLIT)
                act.wait_ge(w_used, s + 6)
                act.wait_ge(sem("s_rows"), 2)
                evacuate(2, kn)
                split(s + 7 + SPLIT)
                act.wait_ge(w_used, s + 8)
                evacuate(3, kn)
                turned_heads(0, skT)
                split(s + 8 + SPLIT)
                squares(1)
                split(s + 9 + SPLIT)
                act.wait_ge(w_used, s + 10)
                evacuate(4, vs)
                split(s + 10 + SPLIT)
                turned_heads(1, sqT)
                exp_abs(range(6))
                ln(range(6))
                split(s + 11 + SPLIT)
                act.wait_ge(w_used, s + 12)
                evacuate(5, vs)
                split(s + 12 + SPLIT)
                exp_abs((6, 7))
                weights(range(6))
                ln((6, 7))
                weights((6, 7))
                for pair in range(H2 // 2):
                    act.wait_ge(sem("sb_pv"), 2 * pair + 2)
                    act.activation(xs[:, :, pair * 256:(pair + 1) * 256].rearrange("p t (h c) -> p h t c", h=2),
                                   z_bank(2 * pair)[:].rearrange("p (h t c) -> p h t c", h=2, t=2), ACT.Copy)\
                        .then_inc(sem("sb_o_in"), 1)
                for t in range(NT):
                    turn_hi("sb", t)
                split(last_group("sb_out") + SPLIT)

            norm(0, None, "up0")
            ffn(0)
            split(last_group("down0") + SPLIT)
            norm(1, 0, "mix")
            mixer1()
            norm(2, 1, "up1")
            ffn(1)
            split(last_group("down1") + SPLIT)
            norm(4, 2, "gdn", before=lambda t: norm_sum(FINAL, t, sem("x_ready"), 2 * 2 + t + 1))
            mixer2()
            norm(5, 3, "up2")
            ffn(2)
            split(last_group("down2") + SPLIT)
            gate = embed(0, 4, 6)
            mixer3(gate)
            norm(9, 6, "up3")
            ffn(3)
            split(last_group("down3") + SPLIT)
            gate = embed(1, 7, 10)
            for t in range(NT):
                gate(t)

        def y4_free(b):
            return (sem("g_sq"), b) if b <= 4 else (sem("g_v"), b - 4)

        @block.gpsimd
        def _(pool):
            steps = [0]

            def step(ins):
                steps[0] += 1
                ins.then_inc(sem("pool_step"), 1)
                pool.wait_ge(sem("pool_step"), steps[0])

            def select(ap, cmp, fill, base, pattern, by_partition):
                return pool.affine_select(out=ap, in_=ap, compare_op=cmp, fill=fill, base=base, pattern=pattern,
                                          channel_multiplier=by_partition)

            sums, added = [0], []

            def taps(prod, dst, src, n, weight, bias=None):
                def product(k):
                    q = len(added)
                    if q >= 3:
                        pool.wait_ge(sem("pool_sum"), added[q - 3])
                    pool.tensor_tensor(prod[:, q % 3, :], src(k), weight(k).broadcast_to([P, SEQ]), ALU.mult)\
                        .then_inc(sem("pool_prod"), 1)
                    added.append(base + k + 1)

                base = sums[0]
                if bias is None:
                    ins = pool.tensor_tensor(dst, src(0), weight(0).broadcast_to([P, SEQ]), ALU.mult)
                else:
                    ins = pool.tensor_scalar(dst, src(0), weight(0), bias, ALU.mult, ALU.add)
                ins.then_inc(sem("pool_sum"), 1)
                product(1)
                for k in range(1, n):
                    q = len(added)
                    if k + 1 < n:
                        product(k + 1)
                    pool.wait_ge(sem("pool_prod"), q)
                    pool.wait_ge(sem("pool_sum"), base + k)
                    pool.tensor_tensor(dst, dst, prod[:, (q - 1) % 3, :], ALU.add).then_inc(sem("pool_sum"), 1)
                sums[0] += n

            pool.memset(half[:], -0.5)
            pool.memset(eps_col[:], EPS)
            pool.memset(mean_of[:], 1.0 / DC)
            pool.memset(ones[:], 1.0)
            pool.memset(upto[:], 1.0)
            step(pool.memset(ident[:], 0.0))
            select(ident[:], ALU.not_equal, 1.0, 0, [[-1, P]], 1)
            select(upto[:], ALU.is_ge, 0.0, 0, [[1, P]], -1).then_inc(sem("consts"), 1)

            def root(dst, mean, sums, width, names, value):
                pool.wait_ge(sem(names[0]), value)
                step(pool.tensor_scalar(mean, sums, 1.0 / width, EPS, ALU.mult, ALU.add))
                pool.tensor_tensor(dst, mean, half[:, 0:sums.shape[-1]], ALU.pow).then_inc(sem(names[1]), 1)

            def norm(n, tiles=range(NT)):
                for t in tiles:
                    c = slice(2 * n + t, 2 * n + t + 1)
                    root(rstd[:, c], meansq[:, c], sumsq[:, c], D, ("norm_ss", "norm_rstd"), nth(n, t))

            def mixer1():
                def out_roots():
                    for t in range(NT):
                        root(yrs[:, t:t + 1], yms[:, t:t + 1], yst[:, t:t + 1], DC, ("a_ss", "a_rs"), t + 1)

                norm(1)
                pool.wait_ge(w_used, first["mix"])
                pool.memset(u[:, :, 0:PAD], 0.0).then_inc(sem("m_zero"), 1)
                pool.memset(qz[:], 0.0).then_inc(sem("m_zero"), 1)
                step(pool.memset(pick[:], 0.0))
                select(pick[:], ALU.not_equal, -1.0, 0, [[-1, H1], [0, P]], 1)
                step(pool.memset(mask1[:], 0.0))
                select(mask1[:, P:SEQ], ALU.is_ge, -BIG, 0, [[-1, P]], 1).then_inc(sem("m_mask"), 1)

                def product(k):
                    if k >= 4:
                        pool.wait_ge(sem("c_conv_p"), k - 3)
                    pool.tensor_tensor(prod[:, k % 3, :, :], u[:, CT - 2:, k:k + SEQ],
                                       tap[:, CT - 2:, k:k + 1].broadcast_to([P, 2, SEQ]), ALU.mult).then_inc(sem("c_prod_p"), 1)
                pool.wait_ge(sem("m_u"), 1)
                for k in range(1, TAPS):
                    if k % 4 == 2 and k + 1 < TAPS:
                        product(k + 1)
                    if k % 4 == 3:
                        pool.wait_ge(sem("c_prod_p"), (k + 1) // 4)
                    else:
                        pool.wait_ge(sem("c_prod_a"), k + 1 - (k + 1) // 4)
                    if k > 1:
                        pool.wait_ge(sem("c_conv_p"), k - 1)
                    pool.tensor_tensor(y[:, CT - 2:, :], y[:, CT - 2:, :], prod[:, k % 3, :, :], ALU.add)\
                        .then_inc(sem("c_conv_p"), 1)
                for i in range(2):
                    pool.wait_ge(sem("c_eps"), i + 1)
                    pool.tensor_tensor(stat_r[:, i, :], stat[:, i, :], half[:, 0:NT], ALU.pow).then_inc(sem("c_root"), 1)
                    if i == 0:
                        out_roots()

            def mixer2():
                for t in range(NT):
                    norm(FINAL, (t,))
                    norm(FINAL + 1, (t,))
                pool.wait_ge(w_used, first["gdn"])
                pool.memset(u4[:, :, 0:PAD4], 0.0).then_inc(sem("g_zero"), 1)
                pool.memset(maskT[:], 0.0)
                step(pool.memset(lvl[:], 0.0))
                select(maskT[:], ALU.is_ge, -BIG, 0, [[1, P]], -1)
                for l in range(7):
                    b = 2 ** l
                    v = lvl[:, l, :].rearrange("p (i j) -> p i j", j=2 * b)[:, :, b:2 * b]
                    step(pool.memset(v, 1.0))
                    step(select(v, ALU.is_ge, 0.0, 0, [[-2 * b, 64 // b], [0, b]], 1))
                    ins = select(v, ALU.is_ge, 0.0, b - 1, [[2 * b, 64 // b], [0, b]], -1)
                ins.then_inc(sem("g_masks"), 1)
                pool.wait_ge(sem("g_zero"), 1)
                for b in range(6):
                    pool.wait_ge(sem("g_u"), b + 1)
                    if b:
                        pool.wait_ge(*y4_free(b))
                    taps(prod4, y4[:, 3, :], lambda k: u4[:, 3, k:k + SEQ], W4, lambda k: tap4[:, 4 * b + 3, k:k + 1])
                pool.wait_ge(sem("g_vec"), 1)
                for t in range(NT):
                    for g in range(HG):
                        for i in range(2):
                            n = 2 * (HG * t + g) + i
                            if n >= 2:
                                pool.wait_ge(sem("g_dec"), n - 1)
                            if n == 2 * HG * t and t:
                                pool.wait_ge(sem("r_S"), HG)
                            pool.tensor_tensor(DG[i][:], ident[:].unsqueeze(1).broadcast_to([P, 4, P]),
                                               vec[:, ROWA + i, t, 4 * g:4 * g + 4].unsqueeze(2).broadcast_to([P, 4, P]),
                                               ALU.mult).then_inc(sem("g_dg"), 1)
                    for l in range(7):
                        for g in range(HG):
                            n = HG * (7 * t + l) + g
                            if l == 0:
                                pool.wait_ge(sem("g_AQ"), 2 * (HG * t + g) + 1)
                            else:
                                pool.wait_ge(sem("i_Y"), n - HG + 1)
                            pool.tensor_tensor(Lm[:, g, :, :], AT[:, g, :, :],
                                               lvl[:, l:l + 1, :].broadcast_to([P, 4, P]), ALU.mult).then_inc(sem("i_L"), 1)
                for t in range(NT):
                    root(ors[:, t, :], oms[:, t, :], oss[:, t, :], P, ("g_oss", "g_ors"), t + 1)

            def mixer3():
                norm(7)
                pool.wait_ge(w_used, first["kv"])
                pool.memset(smask[:], 1.0)
                pool.memset(sbig[:], 0.0)
                pool.memset(neg_one[:], -1.0)
                step(pool.memset(neg_tri[:], -1.0))
                for c in (0, 2 * P):
                    select(smask[:, c:c + P], ALU.is_ge, 0.0, -1, [[1, P]], -1)
                select(sbig[:], ALU.is_ge, -BIG, -1, [[1, P]], -1)
                select(neg_tri[:], ALU.is_ge, 0.0, 0, [[-1, P]], 1).then_inc(sem("s_masks"), 1)
                for i in range(2):
                    for t in range(NT):
                        root(krs[:, i, t, :], kms[:, i, t, :], kss[:, i, t, :], P, ("s_kss", "s_krs"), 2 * i + t + 1)

            norm(0)
            mixer1()
            norm(2)
            mixer2()
            norm(5)
            norm(6)
            mixer3()
            norm(9)
            norm(10)

        @block.vector
        def _(dve):
            split_to = [0]
            steps = [0]

            def step(ins):
                steps[0] += 1
                ins.then_inc(sem("dve_step"), 1)
                dve.wait_ge(sem("dve_step"), steps[0])

            def split(n):
                while split_to[0] < min(n, NSLOT):
                    w = split_to[0]
                    dve.wait_ge(w_hi, w + 1)
                    dve.tensor_tensor(wlo[w % SPLIT][:], raw[w % RAW][:], whi[w % SPLIT][:].bitcast(F32),
                                      ALU.subtract).then_inc(w_lo, 1)
                    split_to[0] += 1

            def norm_scale(n, t):
                if n == 8:
                    dve.wait_ge(sem("turn_T"), 4 * turn("n7") + 2 * t + 2)
                else:
                    dve.wait_ge(sem("norm_rstd"), nth(n, t))
                c = 2 * (7 if n == 8 else n) + t
                dve.wait_ge(sem(f"gain_in{n % 2}"), 16 * (n // 2 + 1))
                dst = X if n == FINAL else xs
                dve.scalar_tensor_tensor(out=dst[:, t, :], in0=X[:, t, :], scalar=rstd[:, c:c + 1],
                                         in1=gain[n % 2][:], op0=ALU.mult, op1=ALU.mult)\
                   .then_inc(sem("final_x" if n == FINAL else "turn_in"), 1)

            def turn_lo(name, t, hi=None, lo=None):
                hi, lo = hi or xThi, lo or xTlo
                for b in range(2):
                    dve.wait_ge(sem("turn_hi"), 4 * turn(name) + 2 * t + b + 1)
                    part = (slice(None), slice(4 * b, 4 * b + 4), slice(t * P, (t + 1) * P))
                    dve.tensor_tensor(lo[part], bank[4 + b][:].rearrange("p (k c) -> p k c", k=4),
                                      hi[part].bitcast(F32), ALU.subtract).then_inc(sem("turn_lo"), 1)

            def norm(n, follows, hi=None, lo=None, before=None):
                for t in range(NT):
                    if before:
                        before(t)
                    if t and follows:
                        split(first[follows] + 2)
                    norm_scale(n, t)
                    if t == 0 and follows:
                        split(first[follows] + 1)
                    turn_lo(f"n{n}", t, hi, lo)

            def residual(name, scale):
                m = WIDE.index(name)

                def add(t):
                    wait_wide(dve, m, t)
                    for h in range(2):
                        ins = dve.scalar_tensor_tensor(
                            out=X[:, t, h * 512:(h + 1) * 512], in0=out_bank(t, h)[:], scalar=scale,
                            in1=X[:, t, h * 512:(h + 1) * 512], op0=ALU.mult, op1=ALU.add)
                    ins.then_inc(sem("x_ready"), 1)
                split(last_group(name) + SPLIT)
                return add

            def ffn(f):
                def hidden_lo(j):
                    dve.wait_ge(sem("ffn_hi"), NBLK * f + j + 1)
                    dve.tensor_tensor(hTlo[:, 2 * j:2 * j + 2, :], bank[4 + j % 2][:].rearrange("p (k c) -> p k c", k=2),
                                      hThi[:, 2 * j:2 * j + 2, :].bitcast(F32), ALU.subtract).then_inc(sem("ffn_lo"), 1)

                for j in range(NBLK):
                    s = first[f"up{f}"] + 2 * j
                    split(s + (0 if j == 0 else 1) + SPLIT)
                    for t in range(NT):
                        if t:
                            split(s + 1 + SPLIT)
                        dve.wait_ge(sem("ffn_silu"), 2 * (NBLK * f + j) + t + 1)
                        if f or j >= 2:
                            dve.wait_ge(sem("ffn_T"), NBLK * f + j - 1)
                        dve.tensor_tensor(hnat[:, j % 2, t, :], silu[:, j % 2, t, :],
                                          bank[2 * (j % 2) + t][:, 256:512], ALU.mult).then_inc(sem("ffn_h"), 1)
                    split(s + 2 + SPLIT)
                    if j:
                        hidden_lo(j - 1)
                    if f == 0 and j == 4:
                        setup()
                split(first[f"down{f}"] + SPLIT)
                hidden_lo(NBLK - 1)

            def setup():
                dve.wait_ge(sem("setup_T"), 1)
                dve.tensor_copy(chan[:].rearrange("p v c -> p (v c)"), bank[7][:, 0:4 * CT])
                dve.tensor_copy(tap[:].rearrange("p c k -> p (c k)"), bank[7][:, 16:16 + CT * TAPS])
                dve.tensor_copy(tap4[:].rearrange("p c k -> p (c k)"), bank[7][:, 160:160 + QKV * W4]).then_inc(sem("m_tap"), 1)
                dve.wait_ge(sem("narrow_hi"), 1)
                dve.tensor_tensor(narrow_lo[:], narrow[:], narrow_hi[:].bitcast(F32), ALU.subtract).then_inc(sem("narrow_lo"), 1)

            def mixer1():
                s = first["mix"]
                taps = [0]

                def convolve(n):
                    for k in range(taps[0], min(taps[0] + n, TAPS)):
                        for c in range(CT - 2):
                            src = u[:, c, k:k + SEQ]
                            if k == 0:
                                ins = dve.tensor_scalar(y[:, c, :], src, tap[:, c, k:k + 1], chan[:, 0, c:c + 1], ALU.mult, ALU.add)
                            else:
                                dve.wait_ge(sem("c_conv_d"), 2 * (k - 1) + c + 1)
                                ins = dve.scalar_tensor_tensor(out=y[:, c, :], in0=src, scalar=tap[:, c, k:k + 1],
                                                               in1=y[:, c, :], op0=ALU.mult, op1=ALU.add)
                            ins.then_inc(sem("c_conv_d"), 1)
                    taps[0] = min(taps[0] + n, TAPS)

                def add_eps(i, src):
                    dve.wait_ge(sem("c_sum"), i + 2)
                    dve.tensor_scalar(stat[:, i, :], src, EPS, None, ALU.add).then_inc(sem("c_eps"), 1)

                def scale_y(i, row):
                    dve.wait_ge(sem("c_row"), i + 1)
                    if i:
                        dve.wait_ge(sem("c_sq"), 2)
                    dve.tensor_tensor(y[:], y[:], row.unsqueeze(1).broadcast_to([P, CT, SEQ]), ALU.mult)\
                       .then_inc(sem("c_scaled"), 1)

                split(s + 5 + SPLIT)
                dve.wait_ge(sem("m_sig"), 1)
                dve.wait_ge(sem("m_zero"), 1)
                for i in range(2):
                    ins = dve.tensor_tensor(u[:, 2 * i:2 * i + 2, PAD:], bank[2 + i][:].rearrange("p (c t) -> p c t", c=2),
                                            gs[:, 2 * i:2 * i + 2, :], ALU.mult)
                ins.then_inc(sem("m_u"), 1)
                dve.wait_ge(sem("m_fl"), 1)
                step(dve.tensor_tensor(zf[:], bank[6][:, 0:NT * H1].rearrange("p (t h) -> p t h", t=NT),
                                       forget_b[:].unsqueeze(1).broadcast_to([P, NT, H1]), ALU.add))
                dve.scalar_tensor_tensor(out=zfe[:], in0=zf[:], scalar=-1.0, in1=zf[:], op0=ALU.mult, op1=ALU.min)\
                   .then_inc(sem("m_z"), 1)
                dve.wait_ge(sem("m_u"), 1)
                split(s + 6 + SPLIT)
                convolve(2)
                dve.wait_ge(sem("m_ln"), 1)
                dve.scalar_tensor_tensor(out=lf[:], in0=zf[:], scalar=0.0, in1=zfe[:], op0=ALU.min, op1=ALU.subtract)\
                   .then_inc(sem("m_lf"), 1)
                for i in range(4):
                    convolve(4 if i else 3)
                    split(s + 7 + i + SPLIT)
                dve.wait_ge(sem("m_mask"), 1)
                for h in range(H1):
                    convolve(3)
                    dve.wait_ge(sem("at_S"), h + 1)
                    if h >= 2:
                        dve.wait_ge(sem("at_exp"), h - 1)
                    dve.scalar_tensor_tensor(out=p1[:, h % 2, 0:P], in0=bank[h % 2][:, 0:P], scalar=cum[:, 0, h:h + 1],
                                             in1=mask1[:, P:SEQ], op0=ALU.add, op1=ALU.add)
                    step(dve.scalar_tensor_tensor(out=p1[:, h % 2, P:384], in0=bank[h % 2][:, P:384],
                                                  scalar=cum[:, 1, h:h + 1], in1=mask1[:], op0=ALU.add, op1=ALU.add))
                    dve.tensor_reduce(mx[:, h % 2, 0:1], p1[:, h % 2, 0:P], AX_X, ALU.max)
                    step(dve.tensor_reduce(mx[:, h % 2, 1:2], p1[:, h % 2, P:384], AX_X, ALU.max))
                    dve.tensor_scalar(nmx[:, h % 2, :], mx[:, h % 2, :], -1.0, None, ALU.mult).then_inc(sem("at_nm"), 1)
                    if h == H1 - 3:
                        convolve(TAPS)
                    if h == H1 - 1:
                        dve.wait_ge(sem("c_sum"), 1)
                        dve.tensor_tensor(y[:], y[:], bank[7][:, 0:SEQ].unsqueeze(1).broadcast_to([P, CT, SEQ]), ALU.subtract)\
                           .then_inc(sem("c_centred"), 1)
                add_eps(0, bank[7][:, SEQ:SEQ + NT])
                dve.wait_ge(sem("at_exp"), H1)
                step(dve.reciprocal(rinv[:], rsum[:]))
                dve.wait_ge(sem("at_pv"), H1)
                for t in range(NT):
                    dve.tensor_tensor(yA[:, t, :].rearrange("p (h c) -> p h c", h=H1),
                                      bank[4 + t][:].rearrange("p (h c) -> p h c", h=H1),
                                      rinv[:, t, :].unsqueeze(2).broadcast_to([P, H1, D1]), ALU.mult).then_inc(sem("a_y"), 1)
                scale_y(0, bank[6][:, 0:SEQ])
                for t in range(NT):
                    dve.wait_ge(sem("a_rs"), t + 1)
                    dve.scalar_tensor_tensor(out=yA[:, t, :], in0=yA[:, t, :], scalar=yrs[:, t:t + 1], in1=attn_gain[:],
                                             op0=ALU.mult, op1=ALU.mult).then_inc(sem("a_in"), 1)
                for t in range(NT):
                    dve.wait_ge(sem("a_hi"), t + 1)
                    dve.tensor_tensor(xTlo[:, CT:KD, t * P:(t + 1) * P], bank[t][:].rearrange("p (k c) -> p k c", k=4),
                                      xThi[:, CT:KD, t * P:(t + 1) * P].bitcast(F32), ALU.subtract).then_inc(sem("a_lo"), 1)
                add_eps(1, bank[4][:, 0:NT])
                scale_y(1, bank[4][:, SEQ:])
                dve.wait_ge(sem("c_hi"), 1)
                for c in range(CT):
                    ins = dve.scalar_tensor_tensor(out=xTlo[:, c, :], in0=y[:, c, :], scalar=chan[:, 3, c:c + 1],
                                                   in1=xThi[:, c, :].bitcast(F32), op0=ALU.mult, op1=ALU.subtract)
                ins.then_inc(sem("c_lo"), 1)

            def by_head(v, t, g):
                return vec[:, v, t, 4 * g:4 * g + 4].unsqueeze(2).broadcast_to([P, 4, P])

            def mixer2():
                s = first["gdn"]
                split(s + 1 + SPLIT)
                dve.wait_ge(sem("g_ab"), 1)
                z7 = bank[7][:, 0:4 * H2].rearrange("p (t h) -> p t h", t=NT)
                dve.tensor_tensor(zab[:, :, 0:H2], z7[:, :, 0:H2], dt_bias[:].unsqueeze(1).broadcast_to([P, NT, H2]), ALU.add)
                step(dve.tensor_copy(zab[:, :, H2:], z7[:, :, H2:]))
                dve.scalar_tensor_tensor(out=eab[:], in0=zab[:], scalar=-1.0, in1=zab[:], op0=ALU.mult, op1=ALU.min)\
                   .then_inc(sem("g_z"), 1)
                dve.wait_ge(sem("g_ln"), 1)
                dve.scalar_tensor_tensor(out=gl[:, :, H2:], in0=zab[:, :, H2:], scalar=0.0, in1=eab[:, :, H2:],
                                         op0=ALU.min, op1=ALU.subtract)
                step(dve.scalar_tensor_tensor(out=gl[:, :, 0:H2], in0=zab[:, :, 0:H2], scalar=0.0, in1=eab[:, :, 0:H2],
                                              op0=ALU.max, op1=ALU.add))
                dve.scalar_tensor_tensor(out=gl[:, :, 0:H2], in0=gl[:, :, 0:H2], scalar=-1.0,
                                         in1=a_log[:].unsqueeze(1).broadcast_to([P, NT, H2]), op0=ALU.mult, op1=ALU.mult)\
                   .then_inc(sem("g_g"), 1)
                for b in range(2):
                    split(s + 2 * b + 1 + SPLIT)
                    dve.wait_ge(sem("g_gate"), b + 1)
                    for t in range(NT):
                        v = sg[:, t, b * 512:(b + 1) * 512].rearrange("p (h c) -> p h c", h=4)
                        dve.tensor_tensor(v, v, head_gain[:, GDNG:GDNG + 1, :].broadcast_to([P, 4, P]), ALU.mult)\
                           .then_inc(sem("g_sg"), 1)
                    split(s + 2 * b + 2 + SPLIT)
                s += 4
                dve.wait_ge(sem("g_zero"), 1)
                for b in range(6):
                    split(s + 2 * b + 1 + SPLIT)
                    dve.wait_ge(sem("g_u"), b + 1)
                    if b:
                        dve.wait_ge(*y4_free(b))
                    for k in range(W4):
                        for c in range(3):
                            w, src = tap4[:, 4 * b + c, k:k + 1], u4[:, c, k:k + SEQ]
                            if k == 0:
                                ins = dve.tensor_scalar(y4[:, c, :], src, w, None, ALU.mult)
                            else:
                                dve.wait_ge(sem("g_conv"), 3 * (W4 * b + k - 1) + c + 1)
                                ins = dve.scalar_tensor_tensor(out=y4[:, c, :], in0=src, scalar=w, in1=y4[:, c, :],
                                                               op0=ALU.mult, op1=ALU.add)
                            ins.then_inc(sem("g_conv"), 1)
                    split(s + 2 * b + 2 + SPLIT)
                dve.wait_ge(sem("g_lkq"), 1)
                dve.wait_ge(sem("g_cum_in"), 1)
                lq, lk, lb = lkq[:, :, 0:H2], lkq[:, :, H2:], gl[:, :, H2:]
                dve.scalar_tensor_tensor(out=vec[:, ROWQ], in0=lq, scalar=-0.5 * math.log(P), in1=vec[:, G_],
                                         op0=ALU.add, op1=ALU.add)
                dve.tensor_copy(vec[:, BETA], lb)
                dve.tensor_tensor(vec[:, TMP], lb, vec[:, G_], ALU.add)
                step(dve.tensor_tensor(vec[:, COL], lk, vec[:, G_], ALU.subtract))
                dve.tensor_tensor(vec[:, CVN], vec[:, COL], vec[:, GL], ALU.add)
                dve.tensor_tensor(vec[:, ROWA], vec[:, TMP], lk, ALU.add).then_inc(sem("g_vec"), 1)
                dve.wait_ge(sem("g_vexp"), 1)
                for t in range(NT):
                    for g in range(HG):
                        n = HG * t + g
                        dve.wait_ge(sem("g_vn"), n + 1)
                        dve.tensor_tensor(bv[:, t, g * 512:(g + 1) * 512].rearrange("p (h c) -> p h c", h=4),
                                          bank[n][:].rearrange("p (h c) -> p h c", h=4), by_head(BETA, t, g), ALU.mult)\
                           .then_inc(sem("g_bv"), 1)
                dve.wait_ge(sem("g_masks"), 1)
                for t in range(NT):
                    for g in range(HG):
                        for i in range(2):
                            n = 2 * (HG * t + g) + i
                            dve.wait_ge(sem("g_row"), n + 1)
                            dve.tensor_tensor(DG[i][:], bank[i][:].rearrange("p (h c) -> p h c", h=4),
                                              maskT[:].unsqueeze(1).broadcast_to([P, 4, P]), ALU.add).then_inc(sem("g_decm"), 1)
                            dve.wait_ge(sem("g_dec"), n + 1)
                            dve.wait_ge(sem("g_kq"), n + 1)
                            dst = AT if i == 0 else QKT
                            dve.tensor_tensor(dst[:, g, :, :], bank[2 + i][:].rearrange("p (h c) -> p h c", h=4), DEC[i][:],
                                              ALU.mult).then_inc(sem("g_AQ"), 1)
                    if t:
                        dve.wait_ge(sem("r_vn"), HG)
                    for g in range(HG):
                        for x in (T, U):
                            ins = dve.tensor_copy(x[:, g, :, :], ident[:].unsqueeze(1).broadcast_to([P, 4, P]))
                    ins.then_inc(sem("i_one"), 1)
                    dve.wait_ge(sem("i_one"), t + 1)
                    for l in range(7):
                        b = 2 ** l
                        for g in range(HG):
                            n = HG * (7 * t + l) + g
                            v = T[:, g, :, :].rearrange("p h (i j) -> p (h i) j", j=2 * b)[:, :, 0:b]
                            dve.wait_ge(sem("i_Z"), n + 1)
                            if l:
                                dve.wait_ge(sem("i_T"), n + 1 - HG)
                            dve.tensor_tensor(v, v, bank[2 * g + 1][:, 0:256].rearrange("p (n j) -> p n j", j=b), ALU.subtract)\
                               .then_inc(sem("i_T"), 1)
                    for g in range(HG):
                        n = HG * t + g
                        if t:
                            dve.wait_ge(sem("r_kS"), g + 1)
                            step(dve.tensor_tensor(tq[:], bank[4 + g][:].rearrange("p (h c) -> p h c", h=4), by_head(CKS, t, g), ALU.mult))
                            if g:
                                dve.wait_ge(sem("r_vn"), n)
                            dve.tensor_tensor(r2[:], bv[:, t, g * 512:(g + 1) * 512].rearrange("p (h c) -> p h c", h=4), tq[:],
                                              ALU.subtract).then_inc(sem("r_r"), 1)
                            dve.wait_ge(sem("r_qS"), g + 1)
                            step(dve.tensor_tensor(vne[:], bank[0][:].rearrange("p (h c) -> p h c", h=4), by_head(CQS, t, g), ALU.mult))
                            dve.wait_ge(sem("r_o"), n + 1)
                            dve.tensor_tensor(o2[:, t, g * 512:(g + 1) * 512], bank[2][:], vne[:].rearrange("p h c -> p (h c)"), ALU.add)\
                               .then_inc(sem("r_o1"), 1)
                        else:
                            dve.wait_ge(sem("r_vn_in"), n + 1)
                            if g:
                                dve.wait_ge(sem("r_S"), g)
                            dve.tensor_tensor(vne[:], vn[:], by_head(CVN, t, g), ALU.mult).then_inc(sem("r_vne"), 1)
                for t in range(NT):
                    dve.wait_ge(sem("g_osq"), t + 1)
                    dve.tensor_reduce(oss[:, t, :], bv[:, 0, :].rearrange("p (h c) -> p h c", h=H2), AX_X, ALU.add)\
                       .then_inc(sem("g_oss"), 1)
                dve.wait_ge(sem("g_sg"), 4)
                for t in range(NT):
                    dve.wait_ge(sem("g_ors"), t + 1)
                    v = o2[:, t, :].rearrange("p (h c) -> p h c", h=H2)
                    step(dve.tensor_tensor(v, v, ors[:, t, :].unsqueeze(2).broadcast_to([P, H2, P]), ALU.mult))
                    dve.tensor_tensor(o2[:, t, :], o2[:, t, :], sg[:, t, :], ALU.mult).then_inc(sem("turn_in"), 1)
                for t in range(NT):
                    turn_lo("gdn", t)

            def embed(i, n):
                add = residual(("down2", "down3")[i], (1.0, 1.0)[i])
                add(0)
                dve.wait_ge(sem("p_hi"), i + 1)
                dve.tensor_tensor(pTlo[:].rearrange("p k t -> p (k t)"), bank[0][:],
                                  pThi[:].rearrange("p k t -> p (k t)").bitcast(F32), ALU.subtract).then_inc(sem("p_lo"), 1)
                split(first[f"ple_p{i}"] + SPLIT)
                norm(n, f"ple_g{i}", before=lambda t: add(t) if t else None)
                split(last_group(f"ple_g{i}") + SPLIT)

                def add_gated(t):
                    dve.wait_ge(sem("gate_s"), 2 * i + t + 1)
                    dve.wait_ge(sem("pp_in"), 2 * i + t + 1)
                    step(dve.tensor_tensor(gate_s[:, t, :], gate_s[:, t, :], pp[:, t, :], ALU.mult))
                    dve.tensor_tensor(X[:, t, :], X[:, t, :], gate_s[:, t, :], ALU.add).then_inc(sem("x_ready"), 1)
                return add_gated

            def head_norm(i, t, g_):
                dve.wait_ge(sem("s_krs"), 2 * i + t + 1)
                v = kn[:, t, :].rearrange("p (h c) -> p h c", h=H2)
                w = xs[:, t, :].rearrange("p (h c) -> p h c", h=H2)
                if i:
                    dve.wait_ge(sem("s_kT"), 4)
                else:
                    dve.wait_ge(sem("turn_T"), 4 * turn("n8") + 4)
                step(dve.tensor_tensor(w, v, krs[:, i, t, :].unsqueeze(2).broadcast_to([P, H2, P]), ALU.mult))
                dve.tensor_tensor(w, w, head_gain[:, g_:g_ + 1, :].broadcast_to([P, H2, P]), ALU.mult).then_inc(sem("s_rows"), 1)

            def mixer3(add):
                s = first["kv"]

                def head_sums(i):
                    for t in range(NT):
                        dve.wait_ge(sem("s_sq"), 2 * i + t + 1)
                        dve.tensor_reduce(kss[:, i, t, :], sq_s[:].rearrange("p (h c) -> p h c", h=H2), AX_X, ALU.add)\
                           .then_inc(sem("s_kss"), 1)

                def softplus(heads):
                    for h in heads:
                        dve.wait_ge(sem("sb_ln"), h + 1)
                        step(dve.scalar_tensor_tensor(out=sab[:, h, :], in0=z_bank(h)[:, 0:384], scalar=0.0,
                                                      in1=sab[:, h, :], op0=ALU.max, op1=ALU.add))
                        dve.tensor_tensor(sab[:, h, :], sab[:, h, :], smask[:], ALU.mult).then_inc(sem("sb_sp"), 1)

                norm(7, "kv", before=add)
                split(s + 2 + SPLIT)
                norm(8, None, xThi2, xTlo2)
                split(s + 4 + SPLIT)
                head_sums(0)
                dve.tensor_scalar(head_gain[:, QG, :], head_gain[:, QG, :], P ** -0.5, None, ALU.mult).then_inc(sem("s_qg"), 1)
                for t in range(NT):
                    head_norm(0, t, KG)
                split(s + 8 + SPLIT)
                head_sums(1)
                dve.wait_ge(sem("s_qg"), 1)
                for t in range(NT):
                    head_norm(1, t, QG)
                split(s + 10 + SPLIT)
                dve.wait_ge(sem("s_masks"), 1)
                softplus(range(6))
                split(s + 12 + SPLIT)
                softplus((6, 7))
                for t in range(NT):
                    turn_lo("sb", t)

            norm(0, "up0")
            ffn(0)
            add = residual("down0", 0.5)
            norm(1, "mix", before=add)
            mixer1()
            add = residual("mix_out", 1.0)
            norm(2, "up1", before=add)
            ffn(1)
            add = residual("down1", 0.5)
            def final_norm(t):
                add(t)
                norm_scale(FINAL, t)
            norm(4, "gdn", before=final_norm)
            mixer2()
            add = residual("gdn_out", 1.0)
            norm(5, "up2", before=add)
            ffn(2)
            add = embed(0, 6)
            mixer3(add)
            add = residual("sb_out", 1.0)
            norm(9, "up3", before=add)
            ffn(3)
            add = embed(1, 10)
            for t in range(NT):
                add(t)

        @block.tensor
        def _(pe):
            xT, hT, pT, xT2 = (xThi, xTlo), (hThi, hTlo), (pThi, pTlo), (xThi2, xTlo2)

            def passes(psum, lhs, rhs, start, stop):
                pe.matmul(psum, lhs[0], rhs[0], start=start, stop=False, skip_group_check=True)
                pe.matmul(psum, lhs[0], rhs[1], start=False, stop=False, skip_group_check=True)
                return pe.matmul(psum, lhs[1], rhs[0], start=False, stop=stop, skip_group_check=True)

            def ring(w):
                return whi[w % SPLIT], wlo[w % SPLIT]

            def rows(w, t, src, k0, nk, psums, begins, ends):
                for k in range(nk):
                    for c, psum in enumerate(psums):
                        at = (k * len(psums) + c) * 512
                        ins = passes(psum[:], [x[:, k0 + k, t * P:(t + 1) * P] for x in src],
                                     [x[:, at:at + 512] for x in ring(w)], begins and k == 0, ends and k == nk - 1)
                return ins

            def turn_T(name, t, wait=None):
                pe.wait_ge(*(wait or (sem("turn_in"), turned_in(name, t))))
                for b in range(2):
                    before = 4 * turn(name) + 2 * t + b - 1
                    if before > 0:
                        pe.wait_ge(sem("turn_lo"), before)
                    for k in range(4):
                        ins = pe.transpose(bank[4 + b][:, k * P:(k + 1) * P],
                                           xs[:, t, (4 * b + k) * P:(4 * b + k + 1) * P], ident[:])
                    ins.then_inc(sem("turn_T"), 1)

            def turned(name, t):
                pe.wait_ge(sem("turn_lo"), 4 * turn(name) + 2 * t + 2)

            def wide(name, src, ready=None, middle=None, pairs=None):
                s, n = first[name], wide_slots[name]

                def part(i, t):
                    k0 = 2 * (pairs[i] if pairs else i)
                    return rows(s + i, t, src, k0, 2, [out_bank(t, 0), out_bank(t, 1)], i == 0, i == n - 1)
                for i in range(n - SPLIT):
                    pe.wait_ge(w_lo, s + i + 1)
                    if ready:
                        ready(i)
                    for t in range(NT):
                        ins = part(i, t)
                    ins.then_inc(w_used, 1)
                for t in range(NT):
                    for i in range(n - SPLIT, n):
                        if t == 0:
                            pe.wait_ge(w_lo, s + i + 1)
                            if ready:
                                ready(i)
                        elif i == n - 1 and middle:
                            middle()
                        ins = part(i, t)
                        if t == NT - 1:
                            ins.then_inc(w_used, 1)
                    if t == 0:
                        ins.then_inc(sem("wide_mm0"), 1)

            def block_rows(s, src, banks, k_ready=None, tilewise=False, done0=None, free=None):
                order = [(h, t) for h in range(2) for t in range(NT)]
                if tilewise:
                    order.sort(key=lambda x: x[1])
                seen = set()
                for h, t in order:
                    if h == 0 and k_ready:
                        k_ready(t)
                    if h not in seen:
                        pe.wait_ge(w_lo, s + h + 1)
                        seen.add(h)
                    if h == 0 and free:
                        free(t)
                    ins = rows(s + h, t, src, 4 * h, 4, [banks[t]], h == 0, h == 1)
                    if h == 1 and t == 0 and done0:
                        ins.then_inc(sem(done0), 1)
                    if t == NT - 1:
                        ins.then_inc(w_used, 1)

            def block_cols(s, src, banks, k_ready=None):
                tiles = [slice(0, SEQ)] if k_ready is None else [slice(t * P, (t + 1) * P) for t in range(NT)]
                for t, tok in enumerate(tiles):
                    for h in range(2):
                        if h == 0 and k_ready:
                            k_ready(t)
                        if t == 0:
                            pe.wait_ge(w_lo, s + h + 1)
                        for k in range(4):
                            for c in range(4):
                                at = k * 512 + c * P
                                off = (c % 2) * SEQ
                                ins = passes(banks[c // 2][:, off + tok.start:off + tok.stop],
                                             [x[:, at:at + P] for x in ring(s + h)],
                                             [x[:, 4 * h + k, tok] for x in src],
                                             t == 0 and h == 0 and k == 0 and c % 2 == 0, h == 1 and k == 3)
                        if t == len(tiles) - 1:
                            ins.then_inc(w_used, 1)

            def narrow_rows(psum, c0, n, src):
                for t in range(NT):
                    for k in range(KD):
                        ins = passes(psum[:, t * n:(t + 1) * n], [x[:, k, t * P:(t + 1) * P] for x in src],
                                     [x[:, k, c0:c0 + n] for x in (narrow_hi, narrow_lo)], t == 0 and k == 0, k == KD - 1)
                return ins

            def tile_ready(name):
                def ready(t):
                    if t:
                        turn_T(name, t)
                    turned(name, t)
                return ready

            def ffn(f):
                def hidden_T(j):
                    pe.wait_ge(sem("ffn_h"), 2 * (NBLK * f + j) + 2)
                    if j >= 2:
                        pe.wait_ge(sem("ffn_lo"), NBLK * f + j - 1)
                    for k in range(2):
                        for t in range(NT):
                            ins = pe.transpose(bank[4 + j % 2][:, k * SEQ + t * P:k * SEQ + (t + 1) * P],
                                               hnat[:, j % 2, t, k * P:(k + 1) * P], ident[:])
                    ins.then_inc(sem("ffn_T"), 1)

                name = turn_of_up[f]
                for j in range(NBLK):
                    block_rows(first[f"up{f}"] + 2 * j, xT, [bank[2 * (j % 2) + t] for t in range(NT)],
                               k_ready=tile_ready(name) if j == 0 else None, tilewise=j == 0, done0="ffn_mm0",
                               free=(lambda t: pe.wait_ge(sem("ffn_h"), 2 * (NBLK * f + j - 2) + t + 1)) if j >= 2 else None)
                    if j:
                        hidden_T(j - 1)
                    if f == 0 and j == 2:
                        setup()

                def ready(i):
                    if i == 1:
                        hidden_T(NBLK - 1)
                    if i == 2 and f >= 2:
                        p_turn(f - 2)
                    if i == 0:
                        if f == 0:
                            pe.wait_ge(sem("m_tap"), 1)
                        pe.wait_ge(sem("ffn_h"), 2 * (NBLK * f + NBLK - 2) + 2)
                    pe.wait_ge(sem("ffn_lo"), NBLK * f + i + 1)
                return ready

            def setup():
                pe.wait_ge(sem("consts_in"), 16 * N_LOADS)
                pe.transpose(bank[7][:, 0:4 * CT], row_chan[:], ident[0:4 * CT, 0:4 * CT])
                for c in range(CT):
                    pe.transpose(bank[7][:, 16 + c * TAPS:16 + (c + 1) * TAPS], row_tap[:, c * P:(c + 1) * P],
                                 ident[0:TAPS, 0:TAPS])
                for c in range(QKV):
                    ins = pe.transpose(bank[7][:, 160 + c * W4:160 + (c + 1) * W4], row_tap4[:, c * P:(c + 1) * P],
                                       ident[0:W4, 0:W4])
                ins.then_inc(sem("setup_T"), 1)

            def mixer1():
                s = first["mix"]
                block_rows(s, xT, [bank[0], bank[1]], k_ready=tile_ready("n1"), tilewise=True)
                pe.wait_ge(sem("x_ready"), 2)
                block_cols(s + 2, xT, [bank[2], bank[3]])
                pe.wait_ge(sem("narrow_lo"), 1)
                narrow_rows(bank[6], 0, H1, xT).then_inc(sem("m_fl"), 1)
                pe.wait_ge(sem("m_v"), 1)
                block_cols(s + 4, xT, [bank[0], bank[1]])
                pe.wait_ge(sem("m_u"), 1)
                block_cols(s + 6, xT, [bank[2], bank[3]])
                pe.wait_ge(sem("m_lf"), 1)
                pe.matmul(bank[6][:, 32:32 + H1], upto[:], lf[:, 0, :], start=True, stop=True)
                pe.matmul(bank[6][:, 32 + H1:32 + 2 * H1], ones[:], lf[:, 0, :], start=True, stop=False)
                pe.matmul(bank[6][:, 32 + H1:32 + 2 * H1], upto[:], lf[:, 1, :], start=False, stop=True).then_inc(sem("m_cum"), 1)
                block_cols(s + 8, xT, [bank[0], bank[1]])
                pe.wait_ge(sem("m_cum_in"), 1)
                for t in range(NT):
                    ins = pe.transpose(bank[6][0:H1, 128 + t * P:128 + (t + 1) * P], cum[:, t, :], ident[:])
                ins.then_inc(sem("m_cumT"), 1)

                def layer_norm(i):
                    if i == 0:
                        pe.wait_ge(sem("c_conv_d"), 2 * TAPS)
                        pe.wait_ge(sem("c_conv_p"), TAPS - 1)
                        for c in range(CT):
                            ins = pe.matmul(bank[7][:, 0:SEQ], mean_of[:], y[:, c, :], start=c == 0, stop=c == CT - 1)
                        ins.then_inc(sem("c_sum"), 1)
                    elif i in (1, 3):
                        pe.wait_ge(sem("c_sq"), 1 + i // 2)
                        for t in range(NT):
                            dst = bank[7][:, SEQ + t:SEQ + t + 1] if i == 1 else bank[4][:, t:t + 1]
                            for c in range(CT):
                                ins = pe.matmul(dst, ysq[:, c, t * P:(t + 1) * P], mean_of[:, 0:1], start=c == 0, stop=c == CT - 1)
                        ins.then_inc(sem("c_sum"), 1)
                    else:
                        pe.wait_ge(sem("c_root"), i // 2)
                        for t in range(NT):
                            dst = bank[6][:, t * P:(t + 1) * P] if i == 2 else bank[4][:, SEQ + t * P:SEQ + (t + 1) * P]
                            ins = pe.matmul(dst, stat_r[:, i // 2 - 1, t:t + 1].broadcast_to([P, P]), ident[:], start=True, stop=True)
                        ins.then_inc(sem("c_row"), 1)

                pe.wait_ge(sem("m_mask"), 1)
                pe.wait_ge(sem("m_q"), 1)
                pe.wait_ge(sem("m_k"), 1)
                pe.wait_ge(sem("m_cumT_in"), 1)
                for i in range(H1 + 3):
                    if i < H1:
                        h = i
                        if h >= 2:
                            pe.wait_ge(sem("at_nm"), h - 1)
                        S_ = bank[h % 2]
                        for t in range(NT):
                            c = slice(0, P) if t == 0 else slice(P, 384)
                            n = P * (t + 1)
                            pe.matmul(S_[:, c], qz[:, h, t * P:(t + 1) * P], kT[:, h // 2, 0:n], start=t == 0, stop=False,
                                      skip_group_check=True)
                            ins = pe.matmul(S_[:, c], pick[:, h, :], cumT[:, 0:n], start=False, stop=True, skip_group_check=True)
                        ins.then_inc(sem("at_S"), 1)
                    if 2 <= i <= H1 + 1:
                        h = i - 2
                        pe.wait_ge(sem("at_exp"), h + 1)
                        if h >= 2:
                            pe.wait_ge(sem("at_pT"), h - 1)
                        for c in range(3):
                            ins = pe.transpose(bank[2 + h % 2][:, c * P:(c + 1) * P], p2[:, h % 2, c * P:(c + 1) * P], ident[:])
                        ins.then_inc(sem("at_T"), 1)
                    if i >= 3:
                        h = i - 3
                        pe.wait_ge(sem("at_pT"), h + 1)
                        o = slice(h * D1, (h + 1) * D1)
                        pe.matmul(bank[4][:, o], pT1[:, h % 2, 0:P], v1[:, 0, o], start=True, stop=True)
                        pe.matmul(bank[5][:, o], pT1[:, h % 2, P:2 * P], v1[:, 0, o], start=True, stop=False)
                        pe.matmul(bank[5][:, o], pT1[:, h % 2, 2 * P:], v1[:, 1, o], start=False, stop=True).then_inc(sem("at_pv"), 1)
                    if i == H1 - 1:
                        layer_norm(0)
                    if i == H1 + 1:
                        layer_norm(1)
                layer_norm(2)
                for t in range(NT):
                    pe.wait_ge(sem("a_in"), t + 1)
                    for k in range(4):
                        ins = pe.transpose(bank[t][:, k * P:(k + 1) * P], yA[:, t, k * P:(k + 1) * P], ident[:])
                    ins.then_inc(sem("a_T"), 1)

                def ready(i):
                    if i == 0:
                        pe.wait_ge(sem("a_lo"), NT)
                        pe.wait_ge(sem("c_scaled"), 1)
                        layer_norm(3)
                    if i == 1:
                        layer_norm(4)
                    if i == 2:
                        pe.wait_ge(sem("c_lo"), 1)
                return ready

            def mixer2():
                s = first["gdn"]

                def squares(b):
                    pe.wait_ge(sem("g_sq"), b + 1)
                    for c in range(4):
                        for t in range(NT):
                            col = t * 2 * H2 + 4 * b + c
                            ins = pe.matmul(bank[6][:, col:col + 1], sq4[:, c, t * P:(t + 1) * P], ones[:, 0:1], start=True, stop=True)
                    ins.then_inc(sem("g_ss"), 1)
                for b in range(2):
                    block_rows(s + 2 * b, xT, [bank[2 * b], bank[2 * b + 1]], k_ready=tile_ready("n4") if b == 0 else None,
                               tilewise=b == 0)
                    if b == 0:
                        narrow_rows(bank[7], H1, 2 * H2, xT).then_inc(sem("g_ab"), 1)
                pe.wait_ge(sem("g_g"), 1)
                for t in range(NT):
                    pe.matmul(bank[7][:, 64 + t * H2:64 + (t + 1) * H2], upto[:], gl[:, t, 0:H2], start=True, stop=True)
                    ins = pe.matmul(bank[7][:, 80 + t * H2:80 + (t + 1) * H2], ones[:], gl[:, t, 0:H2], start=True, stop=True)
                ins.then_inc(sem("g_cum"), 1)
                s += 4
                for b in range(6):
                    pe.wait_ge(*((sem("g_gate"), b + 1) if b < 2 else (sem("g_u"), b - 1)))
                    block_cols(s + 2 * b, xT, [bank[2 * (b % 2)], bank[2 * (b % 2) + 1]])
                    if 1 <= b <= 4:
                        squares(b - 1)
                for g in range(HG):
                    for h in range(4):
                        ins = pe.transpose(bank[4 + g][:, h * P:(h + 1) * P], qkT[:, H2 + 4 * g + h, 0:P], ident[:])
                    ins.then_inc(sem("g_kn"), 1)
                pe.wait_ge(sem("g_v"), 2)
                for t in range(NT):
                    for g in range(HG):
                        for h in range(4):
                            ins = pe.transpose(bank[HG * t + g][:, h * P:(h + 1) * P], vT[:, 4 * g + h, t * P:(t + 1) * P], ident[:])
                        ins.then_inc(sem("g_vn"), 1)
                pe.wait_ge(sem("g_bv"), 2 * HG)
                pe.wait_ge(sem("g_knat"), HG)

                for t in range(NT):
                    tok = slice(t * P, (t + 1) * P)
                    if t:
                        pe.wait_ge(sem("r_S_in"), HG)
                    for g in range(HG):
                        for i in range(2):
                            n = 2 * (HG * t + g) + i
                            pe.wait_ge(sem("g_dg"), n + 1)
                            if n >= 2:
                                pe.wait_ge(sem("g_AQ"), n - 1)
                            pe.matmul(bank[i][:], ones[:], DG[i][:].rearrange("p h c -> p (h c)"), start=True, stop=True)\
                              .then_inc(sem("g_row"), 1)
                            off = H2 if i == 0 else 0
                            for h in range(4):
                                ins = pe.matmul(bank[2 + i][:, h * P:(h + 1) * P], qkT[:, H2 + 4 * g + h, tok],
                                                qkT[:, off + 4 * g + h, tok], start=True, stop=True)
                            ins.then_inc(sem("g_kq"), 1)
                    pe.wait_ge(sem("i_one"), t + 1)
                    pe.wait_ge(sem("g_AQ"), 4 * (t + 1))
                    for l in range(7):
                        b = 2 ** l
                        for g in range(HG):
                            n = HG * (7 * t + l) + g
                            pe.wait_ge(sem("i_L"), n + 1)
                            if l:
                                pe.wait_ge(sem("i_T"), n + 1 - HG)
                            for h in range(4):
                                ins = pe.matmul(bank[2 * g][:, h * 64:(h + 1) * 64].rearrange("p (i j) -> p i j", j=b),
                                                Lm[:, g, h, :], T[:, g, h, :].rearrange("p (i j) -> p i j", j=2 * b)[:, :, 0:b],
                                                start=True, stop=True)
                            ins.then_inc(sem("i_Y"), 1)
                        for g in range(HG):
                            n = HG * (7 * t + l) + g
                            pe.wait_ge(sem("i_Y_in"), n + 1)
                            if l:
                                pe.wait_ge(sem("i_U"), n + 1 - HG)
                            for h in range(4):
                                ins = pe.matmul(bank[2 * g + 1][:, h * 64:(h + 1) * 64], U[:, g, h, :], Y[:, g, h, :],
                                                start=True, stop=True)
                            ins.then_inc(sem("i_Z"), 1)
                        for g in range(HG):
                            n = HG * (7 * t + l) + g
                            pe.wait_ge(sem("i_T"), n + 1)
                            for h in range(4):
                                ins = pe.transpose(bank[4 + g][:, h * P:(h + 1) * P], T[:, g, h, :], ident[:])
                            ins.then_inc(sem("i_TT"), 1)
                    pe.wait_ge(sem("i_U"), HG * 7 * (t + 1))
                    for g in range(HG):
                        n = HG * t + g
                        cols = lambda h: slice((4 * g + h) * P, (4 * g + h + 1) * P)
                        if t:
                            for h in range(4):
                                ins = pe.matmul(bank[4 + g][:, h * P:(h + 1) * P], qkT[:, H2 + 4 * g + h, tok], S[:, 4 * g + h, :],
                                                start=True, stop=True)
                            ins.then_inc(sem("r_kS"), 1)
                            if g:
                                pe.wait_ge(sem("r_o1"), g)
                            for h in range(4):
                                ins = pe.matmul(bank[0][:, h * P:(h + 1) * P], qkT[:, 4 * g + h, tok], S[:, 4 * g + h, :],
                                                start=True, stop=True)
                            ins.then_inc(sem("r_qS"), 1)
                            pe.wait_ge(sem("r_r"), g + 1)
                        if g:
                            pe.wait_ge(sem("r_vn_in"), n)
                        for h in range(4):
                            ins = pe.matmul(bank[1][:, h * P:(h + 1) * P], U[:, g, h, :], r2[:, h, :] if t else bv[:, 0, cols(h)],
                                            start=True, stop=True)
                        ins.then_inc(sem("r_vn"), 1)
                        pe.wait_ge(sem("r_vn_in"), n + 1)
                        if g:
                            pe.wait_ge(sem("r_o1" if t else "r_o_in"), g)
                        for h in range(4):
                            ins = pe.matmul(bank[2][:, h * P:(h + 1) * P], QKT[:, g, h, :], vn[:, h, :], start=True, stop=True)
                        ins.then_inc(sem("r_o"), 1)
                        if t == 0:
                            pe.wait_ge(sem("r_vne"), g + 1)
                            if g:
                                pe.wait_ge(sem("r_S_in"), g)
                            for h in range(4):
                                ins = pe.matmul(bank[3][:, h * P:(h + 1) * P], knat[:, 4 * g + h, :], vne[:, h, :],
                                                start=True, stop=True)
                            ins.then_inc(sem("r_S"), 1)
                for t in range(NT):
                    turn_T("gdn", t)

                def ready(i):
                    if i == 0:
                        for t in range(NT):
                            turned("gdn", t)
                        pe.wait_ge(sem("r_o1"), HG)
                return ready

            def p_turn(i):
                pe.wait_ge(sem("p_in"), 32 * (i + 1))
                for k in range(2):
                    for t in range(NT):
                        ins = pe.transpose(bank[0][:, k * SEQ + t * P:k * SEQ + (t + 1) * P], p_in[:, t, k * P:(k + 1) * P], ident[:])
                ins.then_inc(sem("p_T"), 1)

            def embed(i, n):
                s = first[f"ple_p{i}"]
                pe.wait_ge(sem("p_lo"), i + 1)
                pe.wait_ge(w_lo, s + 1)
                for t in range(NT):
                    ins = rows(s, t, pT, 0, 2, [bank[(0, 1, 4, 5)[2 * t + h]] for h in range(2)], True, True)
                    ins.then_inc(sem("pp_mm0") if t == 0 else w_used, 1)
                for t in range(NT):
                    if t == 0:
                        pe.wait_ge(sem("pp_in"), 2 * i + 2)
                    turn_T(f"n{n}", t)
                def ready(j):
                    if j == 0:
                        pe.wait_ge(sem("x_ready"), 2 * WIDE.index(f"ple_g{i}"))
                        for t in range(NT):
                            turned(f"n{n}", t)
                return ready

            def mixer3():
                s = first["kv"]

                def head_turn(i):
                    for t in range(NT):
                        pe.wait_ge(sem("s_rows"), 2 * i + t + 1)
                        for b in range(2):
                            if i == 0 and t == 0:
                                pe.wait_ge(sem("turn_lo"), 4 * turn("n8") + 4)
                            if 4 * i + 2 * t + b - 1 > 0:
                                pe.wait_ge(sem("s_kT_in"), 4 * i + 2 * t + b - 1)
                            for k in range(4):
                                ins = pe.transpose(bank[4 + b][:, k * P:(k + 1) * P], xs[:, t, (4 * b + k) * P:(4 * b + k + 1) * P],
                                                   ident[:])
                            ins.then_inc(sem("s_kT"), 1)

                def scores(heads):
                    for h in heads:
                        z = z_bank(h)
                        pe.matmul(z[:, 0:SEQ], skT[:, h, 0:P], sqT[:, h, :], start=True, stop=False, skip_group_check=True)
                        pe.matmul(z[:, SEQ:384], skT[:, h, P:], sqT[:, h, P:], start=False, stop=False, skip_group_check=True)\
                          .then_inc(sem("sb_z"), 1)

                def suffix(h):
                    z, sp_ = z_bank(h), sab[:, h, :]
                    pe.wait_ge(sem("sb_sp"), h + 1)
                    pe.matmul(z[:, 0:SEQ], neg_tri[:], sp_[:, 0:SEQ], start=False, stop=False, skip_group_check=True)
                    pe.matmul(z[:, P:SEQ], neg_one[:], sp_[:, SEQ:], start=False, stop=True, skip_group_check=True)
                    pe.matmul(z[:, SEQ:384], neg_tri[:], sp_[:, SEQ:], start=False, stop=False, skip_group_check=True)
                    pe.matmul(z[:, 0:P], ident[:], sbig[:], start=False, stop=True, skip_group_check=True)
                    pe.matmul(z[:, SEQ:384], ident[:], sbig[:], start=False, stop=True, skip_group_check=True)\
                      .then_inc(sem("sb_sfx"), 1)

                def output(h):
                    pe.wait_ge(sem("sb_w"), h + 1 + (h % 2 == 0))
                    o, c = z_bank(h - h % 2), (h % 2) * SEQ
                    v = [vs[:, t, h * P:(h + 1) * P] for t in range(NT)]
                    pe.matmul(o[:, c:c + P], sab[:, h, 0:P], v[0], start=True, stop=True)
                    pe.matmul(o[:, c + P:c + SEQ], sab[:, h, P:SEQ], v[0], start=True, stop=False)
                    pe.matmul(o[:, c + P:c + SEQ], sab[:, h, SEQ:], v[1], start=False, stop=True).then_inc(sem("sb_pv"), 1)

                block_rows(s, xT, [bank[0], bank[1]], k_ready=tile_ready("n7"), tilewise=True)
                block_rows(s + 2, xT, [bank[2], bank[3]])
                for t in range(NT):
                    turn_T("n8", t)
                pe.wait_ge(sem("s_kqv"), 1)
                pe.wait_ge(sem("turn_lo"), 4 * turn("n8") + 4)
                block_rows(s + 4, xT2, [bank[0], bank[1]])
                pe.wait_ge(sem("s_kqv"), 2)
                block_rows(s + 6, xT2, [bank[2], bank[3]])
                head_turn(0)
                pe.wait_ge(sem("s_kqv"), 3)
                block_rows(s + 8, xT, [bank[0], bank[1]])
                head_turn(1)
                pe.wait_ge(sem("s_kT_in"), 8)
                pe.wait_ge(sem("s_kqv"), 4)
                scores(range(6))
                pe.wait_ge(sem("s_kqv"), 5)
                block_rows(s + 10, xT, [bank[0], bank[1]])
                pe.wait_ge(sem("s_kqv"), 6)
                scores((6, 7))
                pe.wait_ge(sem("s_masks"), 1)
                for i in range(H2 + 2):
                    if i < H2:
                        suffix(i)
                    if i >= 2:
                        output(i - 2)
                for t in range(NT):
                    turn_T("sb", t, (sem("sb_o_in"), 4))

                def ready(i):
                    if i == 0:
                        for t in range(NT):
                            turned("sb", t)
                return ready

            def next_turn(name):
                return lambda: turn_T(name, 0)

            pe.wait_ge(sem("consts"), 1)
            turn_T("n0", 0)
            wide("down0", hT, ffn(0), next_turn("n1"))
            wide("mix_out", xT, mixer1(), next_turn("n2"), MIX_PAIRS)
            wide("down1", hT, ffn(1), next_turn("n4"))
            wide("gdn_out", xT, mixer2(), next_turn("n5"))
            wide("down2", hT, ffn(2))
            wide("ple_g0", xT, embed(0, 6), next_turn("n7"))
            wide("sb_out", xT, mixer3(), next_turn("n9"))
            wide("down3", hT, ffn(3))
            wide("ple_g1", xT, embed(1, 10))
_INS = ["x", "ffn1_norm", "ffn1_w13", "ffn1_w2", "mix_norm", "w_in", "conv_w", "conv_b", "conv_ln_g", "conv_ln_b",
    "forget_b", "out_norm_conv", "out_norm_attn", "w_out", "ffn2_norm", "ffn2_w13", "ffn2_w2", "final_norm",
    "p_2", "ln_mix_2", "ln_ffn_2", "ln_ple_2", "gdn_w_in_2", "gdn_conv_2", "gdn_a_log_2", "gdn_dt_bias_2",
    "gdn_norm_2", "gdn_w_out_2", "kv_norm_2", "w_kv_2", "k_norm_2", "sb_w_q_2", "sb_q_norm_2", "sb_w_out_2",
    "ffn_w_in_2", "ffn_w_out_2", "ple_w_proj_2", "ple_w_gate_2"]
def kernel(**inputs):
    import numpy as _np
    import concourse.bacc as _bacc
    from concourse import mybir as _mybir
    from concourse.bass_utils import run_bass_kernel_spmd as _run
    nc = _bacc.Bacc("TRN2", target_bir_lowering=False, num_devices=1)
    arrays, args = {}, {}
    for name in _INS:
        v = _np.ascontiguousarray(inputs[name])
        arrays[f"in_{name}_dram"] = v
        args[name] = nc.dram_tensor(f"in_{name}_dram", v.shape, _mybir.dt.from_np(v.dtype), kind="ExternalInput").ap()
    out = nc.dram_tensor("out_0_dram", (1, 256, 1024), _mybir.dt.float32, kind="ExternalOutput").ap()
    build_program(nc, args, out)
    r = _run(nc, [arrays], core_ids=[0])
    return r.results[0]["out_0_dram"]
```

```python
from contextlib import ExitStack
import math

import concourse.bass as bass
from concourse import mybir

F32 = mybir.dt.float32
F32R = mybir.dt.float32r
ALU = mybir.AluOpType
ACT = mybir.ActivationFunctionType
AX_X = mybir.AxisListType.X

P = 128
EPS = 1e-6
BIG = 1e30


def build_program(nc, a, out):
    SEQ, D = a["x"].shape[1:]
    NT = SEQ // P
    KD = D // P
    KF = a["ffn1_w2"].shape[1] // P
    NBLK = KF // 2
    DC = a["conv_b"].shape[1]
    CT = DC // P
    TAPS = a["conv_w"].shape[1]
    PAD = TAPS - 1
    H1 = a["forget_b"].shape[1]
    D1 = DC // H1
    H2 = a["gdn_a_log_2"].shape[1]
    HG = H2 // 4
    W4 = a["gdn_conv_2"].shape[1]
    PAD4 = W4 - 1
    QKV = 3 * H2
    PLE = a["p_2"].shape[3]
    RAW, SPLIT = 4, 3
    SLOT = 4 * 512

    slots, first = [], {}

    BESIDE = NBLK - 2

    def stream_gate_up(name, w, ple=None):
        first[name] = len(slots)
        v = w.rearrange("(k p) (g n) -> p k g n", p=P, g=2)
        for j in range(NBLK):
            if ple is not None and j == BESIDE:
                stream_wide(f"ple_p{ple}", a["ple_w_proj_2"][ple])
            for h in range(2):
                slots.append([(("k", k), v[:, 4 * h + k, :, j * 256:(j + 1) * 256]) for k in range(4)])

    def stream_blocks(name, w, blocks):
        first[name] = len(slots)
        v = w.rearrange("(k p) n -> p k n", p=P)
        for c in blocks:
            for h in range(2):
                slots.append([(("rows", 4), v[:, 4 * h:4 * h + 4, c * 512:(c + 1) * 512])])

    def stream_wide(name, w, pairs=None):
        first[name] = len(slots)
        v = w.rearrange("(k p) n -> p k n", p=P)
        for s in pairs or range(w.shape[0] // (2 * P)):
            slots.append([(("rows", 2), v[:, 2 * s:2 * s + 2, :])])

    stream_gate_up("up0", a["ffn1_w13"][0])
    stream_wide("down0", a["ffn1_w2"][0])
    stream_blocks("mix", a["w_in"][0], (4, 0, 1, 2, 3))
    MIX_PAIRS = (2, 3, 0, 1)
    stream_wide("mix_out", a["w_out"][0], MIX_PAIRS)
    stream_gate_up("up1", a["ffn2_w13"][0])
    stream_wide("down1", a["ffn2_w2"][0])
    stream_blocks("gdn", a["gdn_w_in_2"][0], (6, 7, 0, 1, 2, 3, 4, 5))
    stream_wide("gdn_out", a["gdn_w_out_2"][0])
    stream_gate_up("up2", a["ffn_w_in_2"][0], 0)
    stream_wide("down2", a["ffn_w_out_2"][0])
    stream_wide("ple_g0", a["ple_w_gate_2"][0])
    stream_blocks("kv", a["w_kv_2"], (0, 1))
    stream_blocks("sbq", a["sb_w_q_2"][0], (0, 1))
    stream_blocks("sbv", a["w_kv_2"], (2, 3))
    stream_wide("sb_out", a["sb_w_out_2"][0])
    stream_gate_up("up3", a["ffn_w_in_2"][1], 1)
    stream_wide("down3", a["ffn_w_out_2"][1])
    stream_wide("ple_g1", a["ple_w_gate_2"][1])
    NSLOT = len(slots)

    def up_slot(f, j):
        return first[f"up{f}"] + 2 * j + (1 if f >= 2 and j >= BESIDE else 0)

    WIDE = ["down0", "mix_out", "down1", "gdn_out", "down2", "ple_g0", "sb_out", "down3", "ple_g1"]
    wide_slots = {n: (KF if n[:4] == "down" else KD) // 2 for n in WIDE}

    NORM = [a["ffn1_norm"][0], a["mix_norm"][0], a["ffn2_norm"][0], a["final_norm"], a["ln_mix_2"][0],
            a["ln_ffn_2"][0], a["ln_ple_2"][0], a["kv_norm_2"], a["ln_mix_2"][1], a["ln_ffn_2"][1],
            a["ln_ple_2"][1]]
    FINAL = 3
    gain_before = {"up0": [0], "mix": [1], "up1": [2], "gdn": [3, 4], "up2": [5], "ple_p0": [6],
                   "kv": [7, 8], "up3": [9], "ple_p1": [10]}
    TURN = ["n0", "n1", "n2", "n4", "gdn", "n5", "n6", "n7", "n8", "sb", "n9", "n10"]
    turn_of_up = ["n0", "n2", "n5", "n9"]

    with ExitStack() as ctx:
        def sb(name, shape, dt=F32):
            return ctx.enter_context(nc.sbuf_tensor(name, shape, dt))

        made = {}

        def sem(name):
            if name not in made:
                made[name] = ctx.enter_context(nc.semaphore(name))
            return made[name]

        bank = [ctx.enter_context(nc.psum_tensor(f"bank{i}", [P, 512], F32)) for i in range(8)]
        raw = [sb(f"raw{i}", [P, SLOT]) for i in range(RAW)]
        whi = [sb(f"whi{i}", [P, SLOT], F32R) for i in range(SPLIT)]
        wlo = [sb(f"wlo{i}", [P, SLOT], F32R) for i in range(SPLIT)]
        X = sb("X", [P, NT, D])
        xs = sb("xs", [P, NT, D])
        with ExitStack() as lent:
            core_hi, core_lo = (lent.enter_context(nc.sbuf_tensor(n, [P, KD * SEQ], F32)) for n in ("core_hi", "core_lo"))
        xThi = sb("xThi", [P, KD, SEQ], F32R)
        xTlo = sb("xTlo", [P, KD, SEQ], F32R)
        gain = [sb(f"gain{i}", [P, D]) for i in range(2)]
        ident = sb("ident", [P, P])
        ones = sb("ones", [P, P])
        upto = sb("upto", [P, P])
        sumsq = sb("sumsq", [P, 2 * len(NORM)])
        meansq = sb("meansq", [P, 2 * len(NORM)])
        rstd = sb("rstd", [P, 2 * len(NORM)])
        eps_col = sb("eps_col", [P, 1])
        mean_of = sb("mean_of", [P, P])
        half = sb("half", [P, 16])
        chan = sb("chan", [P, 4, CT])
        tap = sb("tap", [P, CT, TAPS])
        tap4 = sb("tap4", [P, QKV, W4])
        attn_gain = sb("attn_gain", [P, DC])
        forget_b = sb("forget_b", [P, H1])
        narrow = sb("narrow", [P, KD, 24])
        narrow_hi = sb("narrow_hi", [P, KD, 24], F32R)
        narrow_lo = sb("narrow_lo", [P, KD, 24], F32R)
        a_log = sb("a_log", [P, H2])
        dt_bias = sb("dt_bias", [P, H2])
        head_gain = sb("head_gain", [P, 3, P])
        GDNG, KG, QG = range(3)

        def region(always, *turns):
            got = []
            with ExitStack() as phase:
                got += [phase.enter_context(nc.sbuf_tensor(n, s, d)) for n, s, d in always]
                for specs in turns:
                    with ExitStack() as turn:
                        got += [turn.enter_context(nc.sbuf_tensor(n, s, d)) for n, s, d in specs]
            return got

        hThi, hTlo, hnat, silu, p_in, pThi, pTlo, pp, gate_s, row_chan, row_tap, row_tap4 = region(
            [("hThi", [P, KF, SEQ], F32R), ("hTlo", [P, KF, SEQ], F32R),
             ("hnat", [P, 2, NT, 256], F32), ("silu", [P, 2, NT, 256], F32)],
            [("p_in", [P, NT, PLE], F32), ("pThi", [P, 2, SEQ], F32R), ("pTlo", [P, 2, SEQ], F32R),
             ("pp", [P, NT, D], F32), ("gate_s", [P, NT, D], F32)],
            [("row_chan", [4 * CT, P], F32), ("row_tap", [TAPS, DC], F32), ("row_tap4", [W4, QKV * P], F32)])
        (u, gs, y, ysq, stat, stat_r, qz, kT, v1, mask1, zf, zfe, lf, cum, cumT, p1, p2, pT1, mx, nmx, rsum, rinv, yA,
         yst, yms, yrs, pick, prod) = region([
            ("u", [P, CT, PAD + SEQ], F32), ("gs", [P, CT, SEQ], F32), ("y", [P, CT, SEQ], F32),
            ("ysq", [P, CT, SEQ], F32), ("stat", [P, 2, NT], F32), ("stat_r", [P, 2, NT], F32),
            ("qz", [P, H1, SEQ], F32), ("kT", [P, CT, SEQ], F32), ("v1", [P, NT, DC], F32),
            ("mask1", [P, SEQ], F32), ("zf", [P, NT, H1], F32), ("zfe", [P, NT, H1], F32),
            ("lf", [P, NT, H1], F32), ("cum", [P, NT, H1], F32), ("cumT", [H1, SEQ], F32),
            ("p1", [P, 2, 384], F32), ("p2", [P, 2, 384], F32), ("pT1", [P, 2, 384], F32),
            ("mx", [P, 2, 2], F32), ("nmx", [P, 2, 2], F32), ("rsum", [P, NT, H1], F32),
            ("rinv", [P, NT, H1], F32), ("yA", [P, NT, DC], F32), ("yst", [P, 2], F32), ("yms", [P, 2], F32),
            ("yrs", [P, 2], F32), ("pick", [H1, H1, P], F32), ("prod", [P, 3, 2, SEQ], F32)])
        (qkT, sg, zab, eab, gl, lkq, vec, knat, bv, dg, dec, AT, QKT, lvl, maskT, S, oss, oms, ors, v_or_TU, u4, y4,
         sq4) = region(
            [("qkT", [P, 2 * H2, SEQ], F32), ("sg", [P, NT, D], F32), ("zab", [P, NT, 2 * H2], F32),
             ("eab", [P, NT, 2 * H2], F32), ("gl", [P, NT, 2 * H2], F32), ("lkq", [P, NT, 2 * H2], F32),
             ("vec", [P, 10, NT, H2], F32), ("knat", [P, H2, P], F32), ("bv", [P, NT, D], F32),
             ("dg", [P, 4, P], F32), ("dec", [P, 4, P], F32), ("AT", [P, HG, 4, P], F32),
             ("QKT", [P, HG, 4, P], F32), ("lvl", [P, 7, P], F32), ("maskT", [P, P], F32), ("S", [P, H2, P], F32),
             ("oss", [P, NT, H2], F32), ("oms", [P, NT, H2], F32), ("ors", [P, NT, H2], F32),
             ("v_or_TU", [P, H2 * SEQ], F32), ("u4", [P, 4, PAD4 + SEQ], F32), ("y4", [P, 4, SEQ], F32),
             ("sq4", [P, 4, SEQ], F32)])
        vT = v_or_TU[:].rearrange("p (h t) -> p h t", h=H2)
        (vs, kn, xThi2, xTlo2, skT, sqT, sab, sq_s, smask, sbig, neg_tri, neg_one, kss, kms, krs) = region([
            ("vs", [P, NT, D], F32), ("kn", [P, NT, D], F32), ("xThi2", [P, KD, SEQ], F32R), ("xTlo2", [P, KD, SEQ], F32R),
            ("skT", [P, H2, SEQ], F32), ("sqT", [P, H2, SEQ], F32), ("sab", [P, H2, 384], F32), ("sq_s", [P, D], F32),
            ("smask", [P, 384], F32), ("sbig", [P, P], F32),
            ("neg_tri", [P, P], F32), ("neg_one", [P, P], F32), ("kss", [P, 2, NT, H2], F32), ("kms", [P, 2, NT, H2], F32),
            ("krs", [P, 2, NT, H2], F32)])

        def units(flat, n):
            return [flat[:, i * 512:(i + 1) * 512].rearrange("p (h c) -> p h c", h=4) for i in range(n)]
        flat = {name: x.rearrange("p a b -> p (a b)") for name, x in
                (("xs", xs[:]), ("u4", u4[:]), ("y4", y4[:]))}
        tu0, tu1, aq1, l1 = units(v_or_TU, 2 * HG), units(core_hi, 2 * HG), units(core_lo, 2 * HG), units(flat["xs"], HG)
        T, U = tu0[:HG] + tu1[:HG], tu0[HG:] + tu1[HG:]
        A_, QK = [AT[:, g] for g in range(HG)] + aq1[:HG], [QKT[:, g] for g in range(HG)] + aq1[HG:]
        Lm = units(flat["y4"], HG) + l1
        Y = [x[:, i * 256:(i + 1) * 256] for x in (flat["u4"], flat["xs"][:, HG * 512:]) for i in range(HG)]
        UNITS = NT * HG
        vn = sq4[:, 0:2, :].rearrange("p a t -> p (a t)").rearrange("p (h c) -> p h c", h=4)
        vne = sq4[:, 2:4, :].rearrange("p a t -> p (a t)").rearrange("p (h c) -> p h c", h=4)
        DG, DEC = (dg, vn), (dec, vne)
        r2, tq = dg, dec
        o2 = xs
        prod4 = S[:].rearrange("p h c -> p (h c)")[:, 0:3 * SEQ].rearrange("p (b t) -> p b t", b=3)
        G_, GL, ROWA, ROWQ, COL, CKS, CQS, CVN, BETA, TMP = range(10)

        raw_in = [sem(f"raw_in{i}") for i in range(RAW)]
        w_hi, w_lo, w_used = sem("w_hi"), sem("w_lo"), sem("w_used")

        def out_bank(t, h):
            return bank[(6, 7, 2, 3)[2 * t + h]]

        arrived, total = [], [0] * RAW
        for w, pieces in enumerate(slots):
            total[w % RAW] += 16 * len(pieces)
            arrived.append(total[w % RAW])

        def turn(name):
            return TURN.index(name)

        def turned_in(name, t):
            return 2 * [x for x in TURN if x != "sb"].index(name) + t + 1

        def nth(n, t):
            if n in (FINAL, FINAL + 1):
                return 2 * FINAL + 2 * t + n - FINAL + 1
            return 2 * (n - (n > 8)) + t + 1

        def last_group(name):
            return first[name] + wide_slots[name] - SPLIT

        N_LOADS = 15

        block = ctx.enter_context(nc.Block())

        @block.sync
        def _(sp):
            def load_consts():
                done = sem("consts_in")
                for i, name in enumerate(("conv_b", "conv_ln_g", "conv_ln_b", "out_norm_conv")):
                    sp.dma_start(row_chan[i * CT:(i + 1) * CT, :],
                                 a[name][0].rearrange("(c p) -> c p", p=P)).then_inc(done, 16)
                sp.dma_start(row_tap[:], a["conv_w"][0]).then_inc(done, 16)
                sp.dma_start(row_tap4[:], a["gdn_conv_2"][0]).then_inc(done, 16)
                sp.dma_start(attn_gain[:], a["out_norm_attn"][0].partition_broadcast(P)).then_inc(done, 16)
                sp.dma_start(forget_b[:], a["forget_b"][0].partition_broadcast(P)).then_inc(done, 16)
                sp.dma_start(a_log[:], a["gdn_a_log_2"][0].partition_broadcast(P)).then_inc(done, 16)
                sp.dma_start(dt_bias[:], a["gdn_dt_bias_2"][0].partition_broadcast(P)).then_inc(done, 16)
                sp.dma_start(head_gain[:, GDNG, :], a["gdn_norm_2"][0].partition_broadcast(P)).then_inc(done, 16)
                sp.dma_start(head_gain[:, KG, :], a["k_norm_2"].partition_broadcast(P)).then_inc(done, 16)
                sp.dma_start(head_gain[:, QG, :], a["sb_q_norm_2"][0].partition_broadcast(P)).then_inc(done, 16)
                sp.dma_start(narrow[:, :, 0:H1], a["w_in"][0].rearrange("(k p) n -> p k n", p=P)[:, :, 5 * 512:])\
                    .then_inc(done, 16)
                sp.dma_start(narrow[:, :, H1:H1 + 2 * H2],
                             a["gdn_w_in_2"][0].rearrange("(k p) n -> p k n", p=P)[:, :, 8 * 512:]).then_inc(done, 16)

            for w, pieces in enumerate(slots):
                if w < NT:
                    sp.dma_start(X[:, w, :], a["x"][0, w * P:(w + 1) * P, :]).then_inc(sem(f"x_in{w}"), 16)
                for name, s0 in first.items():
                    if s0 != w:
                        continue
                    for n in gain_before.get(name, []):
                        if n - 2 == FINAL:
                            sp.wait_ge(sem("final_x"), NT)
                        elif n >= 2:
                            sp.wait_ge(sem("turn_in"), turned_in(f"n{n - 2}", 1))
                        sp.dma_start(gain[n % 2][:], NORM[n].partition_broadcast(P)).then_inc(sem(f"gain_in{n % 2}"), 16)
                for i in range(2):
                    if w == up_slot(2 + i, 4):
                        if i:
                            sp.wait_ge(sem("p_T"), 1)
                        for t in range(NT):
                            sp.dma_start(p_in[:, t, :], a["p_2"][i, 0, t * P:(t + 1) * P, :]).then_inc(sem("p_in"), 16)
                if w == RAW:
                    load_consts()
                if w >= RAW:
                    sp.wait_ge(w_lo, w - RAW + 1)
                dst = raw[w % RAW]
                for (kind, k), src in pieces:
                    if kind == "rows":
                        view = dst[:].rearrange("p (k n) -> p k n", k=k)
                    else:
                        view = dst[:, k * 512:(k + 1) * 512].rearrange("p (g n) -> p g n", g=2)
                    sp.dma_start(view, src).then_inc(raw_in[w % RAW], 16)
            for t in range(NT):
                sp.wait_ge(sem("x_ready"), 2 * (len(WIDE) - 1) + t + 1)
                sp.dma_start(out[0, t * P:(t + 1) * P, :], X[:, t, :]).then_inc(sem("stored"), 16)
            sp.wait_ge(sem("stored"), 16 * NT)

        def wait_wide(eng, m, t):
            if t == 0:
                eng.wait_ge(sem("wide_mm0"), m + 1)
            else:
                eng.wait_ge(w_used, first[WIDE[m]] + wide_slots[WIDE[m]])

        def z_bank(h):
            return bank[(h + 2) % 8]

        @block.scalar
        def _(act):
            split_to = [0]
            steps = [0]

            def step(ins):
                steps[0] += 1
                ins.then_inc(sem("act_step"), 1)
                act.wait_ge(sem("act_step"), steps[0])

            def split(n):
                while split_to[0] < min(n, NSLOT):
                    w = split_to[0]
                    act.wait_ge(raw_in[w % RAW], arrived[w])
                    if w >= SPLIT:
                        act.wait_ge(w_used, w - SPLIT + 1)
                    act.activation(whi[w % SPLIT][:], raw[w % RAW][:], ACT.Copy).then_inc(w_hi, 1)
                    split_to[0] += 1

            def norm_sum(n, t, ready, value):
                act.wait_ge(ready, value)
                i = turn(f"n{max(n, 4) if n == FINAL else n}")
                if i:
                    act.wait_ge(sem("turn_T"), 4 * (i - 1) + 2 * t + 2)
                act.activation(xs[:, t, :], X[:, t, :], ACT.Square,
                               accum_out=sumsq[:, 2 * n + t:2 * n + t + 1]).then_inc(sem("norm_ss"), 1)

            def turn_hi(name, t, dst=None):
                dst = dst or xThi
                for b in range(2):
                    act.wait_ge(sem("turn_T"), 4 * turn(name) + 2 * t + b + 1)
                    act.activation(dst[:, 4 * b:4 * b + 4, t * P:(t + 1) * P],
                                   bank[4 + b][:].rearrange("p (k c) -> p k c", k=4),
                                   ACT.Copy).then_inc(sem("turn_hi"), 1)

            def norm(n, m, follows, dst=None, before=None):
                for t in range(NT):
                    if before:
                        before(t)
                    if m is None:
                        norm_sum(n, t, sem(f"x_in{t}"), 16)
                    elif n == FINAL + 1:
                        norm_sum(n, t, sem("final_x"), t + 1)
                    elif n != 8:
                        norm_sum(n, t, sem("x_ready"), 2 * m + t + 1)
                    if t == 0 and follows:
                        split(first[follows] + 1)
                    turn_hi(f"n{n}", t, dst)
                    if t == 0 and follows:
                        split(first[follows] + 2)

            def ffn(f):
                def hidden_hi(j):
                    act.wait_ge(sem("ffn_T"), NBLK * f + j + 1)
                    act.activation(hThi[:, 2 * j:2 * j + 2, :], bank[4 + j % 2][:].rearrange("p (k c) -> p k c", k=2),
                                   ACT.Copy).then_inc(sem("ffn_hi"), 1)

                for j in range(NBLK):
                    s = up_slot(f, j)
                    beside = f >= 2 and j == BESIDE
                    if f >= 2 and j == BESIDE - 2:
                        act.wait_ge(sem("p_T"), f - 1)
                        act.activation(pThi[:].rearrange("p k t -> p (k t)"), bank[6][:], ACT.Copy).then_inc(sem("p_hi"), 1)
                    if beside:
                        e = first[f"ple_p{f - 2}"]
                        split(e + SPLIT)
                        for t in range(NT):
                            act.wait_ge(*((sem("pp_mm0"), f - 1) if t == 0 else (w_used, e + 1)))
                            for h in range(2):
                                ins = act.activation(pp[:, t, h * 512:(h + 1) * 512], bank[6 + h][:], ACT.Copy)
                            ins.then_inc(sem("pp_in"), 1)
                            if t == 0:
                                hidden_hi(j - 1)
                    split(s + (0 if j == 0 else 1) + SPLIT)
                    for t in range(NT):
                        if t == 0:
                            act.wait_ge(sem("ffn_mm0"), NBLK * f + j + 1)
                        else:
                            split(s + 1 + SPLIT)
                            act.wait_ge(w_used, s + 2)
                        if f or j >= 2:
                            act.wait_ge(sem("ffn_h"), 2 * (NBLK * f + j - 2) + t + 1)
                        act.activation(silu[:, j % 2, t, :], bank[2 * (j % 2) + t][:, 0:256],
                                       ACT.Silu).then_inc(sem("ffn_silu"), 1)
                    split(s + 2 + SPLIT)
                    if j and not beside:
                        hidden_hi(j - 1)
                    if f == 0 and j == 4:
                        act.wait_ge(sem("consts_in"), 16 * N_LOADS)
                        act.activation(narrow_hi[:], narrow[:], ACT.Copy).then_inc(sem("narrow_hi"), 1)
                split(first[f"down{f}"] + SPLIT)
                hidden_hi(NBLK - 1)

            def mixer1():
                s = first["mix"]
                taps = [0]

                def products(n):
                    for k in range(taps[0], min(taps[0] + n, TAPS)):
                        if k % 4 == 3:
                            continue
                        if k == 0:
                            act.wait_ge(sem("m_u"), 1)
                        if k >= 4:
                            act.wait_ge(sem("c_conv_p"), k - 3)
                        for i in range(2):
                            c = CT - 2 + i
                            src, w = u[:, c, k:k + SEQ], tap[:, c, k:k + 1]
                            if k == 0:
                                ins = act.activation(y[:, c, :], src, ACT.Identity, bias=chan[:, 0, c:c + 1], scale=w)
                            else:
                                ins = act.activation(prod[:, k % 3, i, :], src, ACT.Copy, scale=w)
                        ins.then_inc(sem("c_prod_a"), 1)
                    taps[0] = min(taps[0] + n, TAPS)

                split(s + 1 + SPLIT)
                act.wait_ge(w_used, s + 2)
                for t in range(NT):
                    ins = act.activation(v1[:, t, :], bank[t][:], ACT.Copy)
                ins.then_inc(sem("m_v"), 1)
                split(s + 5 + SPLIT)
                act.wait_ge(w_used, s + 6)
                for i in range(2):
                    ins = act.activation(gs[:, 2 * i:2 * i + 2, :].rearrange("p c t -> p (c t)"), bank[i][:], ACT.Sigmoid)
                ins.then_inc(sem("m_sig"), 1)
                split(s + 6 + SPLIT)
                act.wait_ge(sem("m_z"), 1)
                step(act.activation(zfe[:], zfe[:], ACT.Exp))
                act.activation(zfe[:], zfe[:], ACT.Ln, bias=1.0).then_inc(sem("m_ln"), 1)
                products(4)
                split(s + 7 + SPLIT)
                products(3)
                act.wait_ge(w_used, s + 8)
                act.wait_ge(sem("m_zero"), 2)
                for i in range(2):
                    for r in range(2):
                        rows = slice(r * D1, (r + 1) * D1)
                        ins = act.activation(qz[rows, 4 * i + r:4 * i + r + 3:2, :],
                                             bank[4 + i][rows, :].rearrange("p (c t) -> p c t", c=2), ACT.Copy, scale=D1 ** -0.5)
                ins.then_inc(sem("m_q"), 1)
                act.wait_ge(sem("m_cum"), 1)
                act.activation(cum[:].rearrange("p t h -> p (t h)"), bank[6][:, 32:32 + NT * H1], ACT.Copy).then_inc(sem("m_cum_in"), 1)
                split(s + 8 + SPLIT)
                products(4)
                split(s + 9 + SPLIT)
                products(1)
                act.wait_ge(w_used, s + 10)
                for i in range(2):
                    ins = act.activation(kT[:, 2 * i:2 * i + 2, :].rearrange("p c t -> p (c t)"), bank[i][:], ACT.Copy)
                ins.then_inc(sem("m_k"), 1)
                act.wait_ge(sem("m_cumT"), 1)
                act.activation(cumT[:], bank[6][0:H1, 128:128 + SEQ], ACT.Copy).then_inc(sem("m_cumT_in"), 1)
                split(s + 10 + SPLIT)
                products(4)
                for h in range(H1 + 2):
                    if h < H1:
                        act.wait_ge(sem("at_nm"), h + 1)
                        if h >= 2:
                            act.wait_ge(sem("at_T"), h - 1)
                        for t in range(NT):
                            c = slice(0, P) if t == 0 else slice(P, 384)
                            ins = act.activation(p2[:, h % 2, c], p1[:, h % 2, c], ACT.Exp, bias=nmx[:, h % 2, t:t + 1],
                                                 accum_out=rsum[:, t, h:h + 1])
                        ins.then_inc(sem("at_exp"), 1)
                    if h >= 2:
                        g = h - 2
                        act.wait_ge(sem("at_T"), g + 1)
                        if g >= 2:
                            act.wait_ge(sem("at_pv"), g - 1)
                        act.activation(pT1[:, g % 2, :], bank[2 + g % 2][:, 0:384], ACT.Copy).then_inc(sem("at_pT"), 1)
                    products(3)
                    if h == H1:
                        act.wait_ge(sem("c_centred"), 1)
                        act.activation(ysq[:], y[:], ACT.Square).then_inc(sem("c_sq"), 1)
                for t in range(NT):
                    act.wait_ge(sem("a_y"), t + 1)
                    act.activation(xs[:, t, 0:DC], yA[:, t, :], ACT.Square, accum_out=yst[:, t:t + 1]).then_inc(sem("a_ss"), 1)
                act.wait_ge(sem("c_scaled"), 1)
                for c in range(CT):
                    ins = act.activation(y[:, c, :], y[:, c, :], ACT.Silu, bias=chan[:, 2, c:c + 1], scale=chan[:, 1, c:c + 1])
                step(ins)
                act.activation(ysq[:], y[:], ACT.Square).then_inc(sem("c_sq"), 1)
                for t in range(NT):
                    act.wait_ge(sem("a_T"), t + 1)
                    act.activation(xThi[:, CT:KD, t * P:(t + 1) * P], bank[t][:].rearrange("p (k c) -> p k c", k=4),
                                   ACT.Copy).then_inc(sem("a_hi"), 1)
                act.wait_ge(sem("c_scaled"), 2)
                for c in range(CT):
                    ins = act.activation(xThi[:, c, :], y[:, c, :], ACT.Copy, scale=chan[:, 3, c:c + 1])
                ins.then_inc(sem("c_hi"), 1)
                split(last_group("mix_out") + SPLIT)

            def mixer2():
                s = first["gdn"]
                split(s + 1 + SPLIT)
                act.wait_ge(sem("g_z"), 1)
                act.activation(a_log[:], a_log[:], ACT.Exp)
                step(act.activation(eab[:], eab[:], ACT.Exp))
                act.activation(eab[:], eab[:], ACT.Ln, bias=1.0).then_inc(sem("g_ln"), 1)
                for b in range(2):
                    split(s + 2 * b + 1 + SPLIT)
                    act.wait_ge(w_used, s + 2 * b + 2)
                    for t in range(NT):
                        ins = act.activation(sg[:, t, b * 512:(b + 1) * 512], bank[2 * b + t][:], ACT.Silu)
                    ins.then_inc(sem("g_gate"), 1)
                    split(s + 2 * b + 2 + SPLIT)
                s += 4
                for b in range(6):
                    split(s + 2 * b + 1 + SPLIT)
                    if b == 5:
                        act.wait_ge(sem("g_ss"), 4)
                        step(act.activation(lkq[:].rearrange("p t h -> p (t h)"), bank[6][:, 0:4 * H2], ACT.Ln, bias=eps_col[:, 0:1]))
                        act.activation(lkq[:], lkq[:], ACT.Copy, scale=-0.5).then_inc(sem("g_lkq"), 1)
                        act.wait_ge(sem("g_vec"), 1)
                        act.activation(vec[:, CKS:CQS + 1, :, :], vec[:, ROWA:ROWQ + 1, :, :], ACT.Exp)
                        act.activation(vec[:, CVN:BETA + 1, :, :], vec[:, CVN:BETA + 1, :, :], ACT.Exp).then_inc(sem("g_vexp"), 1)
                        for g in range(HG):
                            act.wait_ge(sem("g_kn"), g + 1)
                            act.activation(knat[:, 4 * g:4 * g + 4, :].rearrange("p h c -> p (h c)"), bank[4 + g][:], ACT.Copy)\
                                .then_inc(sem("g_knat"), 1)
                    act.wait_ge(w_used, s + 2 * b + 2)
                    if b:
                        act.wait_ge(sem("g_conv"), 3 * W4 * b)
                        act.wait_ge(sem("pool_sum"), W4 * b)
                    for i in range(2):
                        ins = act.activation(u4[:, 2 * i:2 * i + 2, PAD4:], bank[2 * (b % 2) + i][:].rearrange("p (c t) -> p c t", c=2),
                                             ACT.Copy)
                    ins.then_inc(sem("g_u"), 1)
                    if b == 0:
                        act.wait_ge(sem("g_cum"), 1)
                        act.activation(vec[:, G_:GL + 1, :, :].rearrange("p v t h -> p (v t h)"), bank[7][:, 64:64 + 4 * H2], ACT.Copy)\
                        .then_inc(sem("g_cum_in"), 1)
                    split(s + 2 * b + 2 + SPLIT)
                    act.wait_ge(sem("g_conv"), 3 * W4 * (b + 1))
                    act.wait_ge(sem("pool_sum"), W4 * (b + 1))
                    dst = qkT[:, 4 * b:4 * b + 4, :] if b < 4 else vT[:, 4 * (b - 4):4 * (b - 4) + 4, :]
                    ins = act.activation(dst, y4[:], ACT.Silu)
                    if b < 4:
                        step(ins)
                        if b:
                            act.wait_ge(sem("g_ss"), b)
                        act.activation(sq4[:], dst, ACT.Square).then_inc(sem("g_sq"), 1)
                    else:
                        ins.then_inc(sem("g_v"), 1)
                for q in range(UNITS):
                    t, g = q // HG, q % HG
                    for i in range(2):
                        act.wait_ge(sem("g_decm"), 2 * q + i + 1)
                        for h in range(4):
                            ins = act.activation(DEC[i][:, h, :], DEC[i][:, h, :], ACT.Exp,
                                                 bias=vec[:, COL, t, 4 * g + h:4 * g + h + 1])
                        ins.then_inc(sem("g_dec"), 1)
                for l in range(7):
                    if l:
                        for q in range(UNITS):
                            act.wait_ge(sem("i_Y"), UNITS * (l - 1) + q + 1)
                            act.activation(Y[q], bank[q][:, 0:256], ACT.Copy).then_inc(sem("i_Y_in"), 1)
                    if l < 6:
                        for q in range(UNITS):
                            act.wait_ge(sem("i_TT"), UNITS * l + q + 1)
                            act.activation((U[q] if l else T[q]).rearrange("p h c -> p (h c)"), bank[4 + q][:], ACT.Copy)\
                                .then_inc(sem("i_U"), 1)

                def head_squares(t):
                    if t:
                        act.wait_ge(sem("g_oss"), t)
                        act.wait_ge(sem("r_o1"), HG)
                    else:
                        act.wait_ge(sem("r_o_in"), HG)
                    act.activation(bv[:, 0, :], o2[:, t, :], ACT.Square).then_inc(sem("g_osq"), 1)
                for t in range(NT):
                    for g in range(HG):
                        n = HG * t + g
                        act.wait_ge(sem("r_vn"), n + 1)
                        act.activation(vn[:].rearrange("p h c -> p (h c)"), bank[1][:], ACT.Copy).then_inc(sem("r_vn_in"), 1)
                        if t == 0:
                            act.wait_ge(sem("r_o"), n + 1)
                            act.activation(o2[:, 0, g * 512:(g + 1) * 512], bank[2][:], ACT.Copy).then_inc(sem("r_o_in"), 1)
                            act.wait_ge(sem("r_S"), g + 1)
                            act.activation(S[:, 4 * g:4 * g + 4, :].rearrange("p h c -> p (h c)"), bank[3][:], ACT.Copy)\
                                .then_inc(sem("r_S_in"), 1)
                    head_squares(t)
                for t in range(NT):
                    turn_hi("gdn", t)
                split(last_group("gdn_out") + SPLIT)

            def embed(i, m_before, n):
                norm(n, m_before, f"ple_g{i}")
                m = WIDE.index(f"ple_g{i}")
                split(last_group(f"ple_g{i}") + SPLIT)

                def gate(t):
                    wait_wide(act, m, t)
                    for h in range(2):
                        ins = act.activation(gate_s[:, t, h * 512:(h + 1) * 512], out_bank(t, h)[:], ACT.Sigmoid)
                    ins.then_inc(sem("gate_s"), 1)
                return gate

            def mixer3(gate):
                s = first["kv"]

                def evacuate(b, dst):
                    for t in range(NT):
                        ins = act.activation(dst[:, t, (b % 2) * 512:(b % 2 + 1) * 512], bank[2 * (b % 2 if b < 4 else 0) + t][:],
                                             ACT.Copy)
                    ins.then_inc(sem("s_kqv"), 1)

                def squares(i):
                    for t in range(NT):
                        if 2 * i + t:
                            act.wait_ge(sem("s_kss"), 2 * i + t)
                        act.wait_ge(sem("s_kqv"), 2 * i + 2)
                        act.activation(sq_s[:], kn[:, t, :], ACT.Square).then_inc(sem("s_sq"), 1)

                def turned_heads(i, dst):
                    for t in range(NT):
                        for b in range(2):
                            act.wait_ge(sem("s_kT"), 4 * i + 2 * t + b + 1)
                            act.activation(dst[:, 4 * b:4 * b + 4, t * P:(t + 1) * P],
                                           bank[4 + b][:].rearrange("p (k c) -> p k c", k=4), ACT.Copy).then_inc(sem("s_kT_in"), 1)

                def exp_abs(heads):
                    for h in heads:
                        act.wait_ge(sem("sb_z"), h + 1)
                        act.activation(sab[:, h, :], z_bank(h)[:, 0:384], ACT.Abs).then_inc(sem("sb_abs"), 1)
                    for h in heads:
                        act.wait_ge(sem("sb_abs"), h + 1)
                        act.activation(sab[:, h, :], sab[:, h, :], ACT.Exp, scale=-1.0).then_inc(sem("sb_exp"), 1)

                def ln(heads):
                    for h in heads:
                        act.wait_ge(sem("sb_exp"), h + 1)
                        act.activation(sab[:, h, :], sab[:, h, :], ACT.Ln, bias=1.0).then_inc(sem("sb_ln"), 1)

                def weights(heads):
                    for h in heads:
                        act.wait_ge(sem("sb_sfx"), h + 1)
                        act.activation(sab[:, h, :], z_bank(h)[:, 0:384], ACT.Exp).then_inc(sem("sb_w"), 1)

                norm(7, WIDE.index("ple_g0"), "kv", before=gate)
                split(s + 1 + SPLIT)
                act.wait_ge(w_used, s + 2)
                evacuate(0, kn)
                split(s + 2 + SPLIT)
                norm(8, WIDE.index("ple_g0"), None, xThi2)
                split(s + 3 + SPLIT)
                act.wait_ge(w_used, s + 4)
                evacuate(1, kn)
                split(s + 4 + SPLIT)
                squares(0)
                split(s + 5 + SPLIT)
                act.wait_ge(w_used, s + 6)
                act.wait_ge(sem("s_rows"), 2)
                evacuate(2, kn)
                split(s + 7 + SPLIT)
                act.wait_ge(w_used, s + 8)
                evacuate(3, kn)
                turned_heads(0, skT)
                split(s + 8 + SPLIT)
                squares(1)
                split(s + 9 + SPLIT)
                act.wait_ge(w_used, s + 10)
                evacuate(4, vs)
                split(s + 10 + SPLIT)
                turned_heads(1, sqT)
                exp_abs(range(6))
                ln(range(6))
                split(s + 11 + SPLIT)
                act.wait_ge(w_used, s + 12)
                evacuate(5, vs)
                split(s + 12 + SPLIT)
                exp_abs((6, 7))
                weights(range(6))
                ln((6, 7))
                weights((6, 7))
                for pair in range(H2 // 2):
                    act.wait_ge(sem("sb_pv"), 2 * pair + 2)
                    act.activation(xs[:, :, pair * 256:(pair + 1) * 256].rearrange("p t (h c) -> p h t c", h=2),
                                   z_bank(2 * pair)[:].rearrange("p (h t c) -> p h t c", h=2, t=2), ACT.Copy)\
                        .then_inc(sem("sb_o_in"), 1)
                for t in range(NT):
                    turn_hi("sb", t)
                split(last_group("sb_out") + SPLIT)

            norm(0, None, "up0")
            ffn(0)
            split(last_group("down0") + SPLIT)
            norm(1, 0, "mix")
            mixer1()
            norm(2, 1, "up1")
            ffn(1)
            split(last_group("down1") + SPLIT)
            norm(4, 2, "gdn", before=lambda t: norm_sum(FINAL, t, sem("x_ready"), 2 * 2 + t + 1))
            mixer2()
            norm(5, 3, "up2")
            ffn(2)
            split(last_group("down2") + SPLIT)
            gate = embed(0, 4, 6)
            mixer3(gate)
            norm(9, 6, "up3")
            ffn(3)
            split(last_group("down3") + SPLIT)
            gate = embed(1, 7, 10)
            for t in range(NT):
                gate(t)

        def y4_free(b):
            return (sem("g_sq"), b) if b <= 4 else (sem("g_v"), b - 4)

        @block.gpsimd
        def _(pool):
            steps = [0]

            def step(ins):
                steps[0] += 1
                ins.then_inc(sem("pool_step"), 1)
                pool.wait_ge(sem("pool_step"), steps[0])

            def select(ap, cmp, fill, base, pattern, by_partition):
                return pool.affine_select(out=ap, in_=ap, compare_op=cmp, fill=fill, base=base, pattern=pattern,
                                          channel_multiplier=by_partition)

            sums, added = [0], []

            def taps(prod, dst, src, n, weight, bias=None):
                def product(k):
                    q = len(added)
                    if q >= 3:
                        pool.wait_ge(sem("pool_sum"), added[q - 3])
                    pool.tensor_tensor(prod[:, q % 3, :], src(k), weight(k).broadcast_to([P, SEQ]), ALU.mult)\
                        .then_inc(sem("pool_prod"), 1)
                    added.append(base + k + 1)

                base = sums[0]
                if bias is None:
                    ins = pool.tensor_tensor(dst, src(0), weight(0).broadcast_to([P, SEQ]), ALU.mult)
                else:
                    ins = pool.tensor_scalar(dst, src(0), weight(0), bias, ALU.mult, ALU.add)
                ins.then_inc(sem("pool_sum"), 1)
                product(1)
                for k in range(1, n):
                    q = len(added)
                    if k + 1 < n:
                        product(k + 1)
                    pool.wait_ge(sem("pool_prod"), q)
                    pool.wait_ge(sem("pool_sum"), base + k)
                    pool.tensor_tensor(dst, dst, prod[:, (q - 1) % 3, :], ALU.add).then_inc(sem("pool_sum"), 1)
                sums[0] += n

            pool.memset(half[:], -0.5)
            pool.memset(eps_col[:], EPS)
            pool.memset(mean_of[:], 1.0 / DC)
            pool.memset(ones[:], 1.0)
            pool.memset(upto[:], 1.0)
            step(pool.memset(ident[:], 0.0))
            select(ident[:], ALU.not_equal, 1.0, 0, [[-1, P]], 1)
            select(upto[:], ALU.is_ge, 0.0, 0, [[1, P]], -1).then_inc(sem("consts"), 1)

            def root(dst, mean, sums, width, names, value):
                pool.wait_ge(sem(names[0]), value)
                step(pool.tensor_scalar(mean, sums, 1.0 / width, EPS, ALU.mult, ALU.add))
                pool.tensor_tensor(dst, mean, half[:, 0:sums.shape[-1]], ALU.pow).then_inc(sem(names[1]), 1)

            def norm(n, tiles=range(NT)):
                for t in tiles:
                    c = slice(2 * n + t, 2 * n + t + 1)
                    root(rstd[:, c], meansq[:, c], sumsq[:, c], D, ("norm_ss", "norm_rstd"), nth(n, t))

            def mixer1():
                def out_roots():
                    for t in range(NT):
                        root(yrs[:, t:t + 1], yms[:, t:t + 1], yst[:, t:t + 1], DC, ("a_ss", "a_rs"), t + 1)

                norm(1)
                pool.wait_ge(w_used, first["mix"])
                pool.memset(u[:, :, 0:PAD], 0.0).then_inc(sem("m_zero"), 1)
                pool.memset(qz[:], 0.0).then_inc(sem("m_zero"), 1)
                step(pool.memset(pick[:], 0.0))
                select(pick[:], ALU.not_equal, -1.0, 0, [[-1, H1], [0, P]], 1)
                step(pool.memset(mask1[:], 0.0))
                select(mask1[:, P:SEQ], ALU.is_ge, -BIG, 0, [[-1, P]], 1).then_inc(sem("m_mask"), 1)

                def product(k):
                    if k >= 4:
                        pool.wait_ge(sem("c_conv_p"), k - 3)
                    pool.tensor_tensor(prod[:, k % 3, :, :], u[:, CT - 2:, k:k + SEQ],
                                       tap[:, CT - 2:, k:k + 1].broadcast_to([P, 2, SEQ]), ALU.mult).then_inc(sem("c_prod_p"), 1)
                pool.wait_ge(sem("m_u"), 1)
                for k in range(1, TAPS):
                    if k % 4 == 2 and k + 1 < TAPS:
                        product(k + 1)
                    if k % 4 == 3:
                        pool.wait_ge(sem("c_prod_p"), (k + 1) // 4)
                    else:
                        pool.wait_ge(sem("c_prod_a"), k + 1 - (k + 1) // 4)
                    if k > 1:
                        pool.wait_ge(sem("c_conv_p"), k - 1)
                    pool.tensor_tensor(y[:, CT - 2:, :], y[:, CT - 2:, :], prod[:, k % 3, :, :], ALU.add)\
                        .then_inc(sem("c_conv_p"), 1)
                for i in range(2):
                    pool.wait_ge(sem("c_eps"), i + 1)
                    pool.tensor_tensor(stat_r[:, i, :], stat[:, i, :], half[:, 0:NT], ALU.pow).then_inc(sem("c_root"), 1)
                    if i == 0:
                        out_roots()

            def mixer2():
                for t in range(NT):
                    norm(FINAL, (t,))
                    norm(FINAL + 1, (t,))
                pool.wait_ge(w_used, first["gdn"])
                pool.memset(u4[:, :, 0:PAD4], 0.0).then_inc(sem("g_zero"), 1)
                pool.memset(maskT[:], 0.0)
                step(pool.memset(lvl[:], 0.0))
                select(maskT[:], ALU.is_ge, -BIG, 0, [[1, P]], -1)
                for l in range(7):
                    b = 2 ** l
                    v = lvl[:, l, :].rearrange("p (i j) -> p i j", j=2 * b)[:, :, b:2 * b]
                    step(pool.memset(v, 1.0))
                    step(select(v, ALU.is_ge, 0.0, 0, [[-2 * b, 64 // b], [0, b]], 1))
                    ins = select(v, ALU.is_ge, 0.0, b - 1, [[2 * b, 64 // b], [0, b]], -1)
                ins.then_inc(sem("g_masks"), 1)
                pool.wait_ge(sem("g_zero"), 1)

                def diagonal(n):
                    q, i = n // 2, n % 2
                    t, g = q // HG, q % HG
                    pool.tensor_tensor(DG[i][:], ident[:].unsqueeze(1).broadcast_to([P, 4, P]),
                                       vec[:, ROWA + i, t, 4 * g:4 * g + 4].unsqueeze(2).broadcast_to([P, 4, P]),
                                       ALU.mult).then_inc(sem("g_dg"), 1)
                for b in range(6):
                    if b == 5:
                        pool.wait_ge(sem("g_vec"), 1)
                        pool.wait_ge(sem("g_ss"), 4)
                        diagonal(0)
                        diagonal(1)
                    pool.wait_ge(sem("g_u"), b + 1)
                    if b:
                        pool.wait_ge(*y4_free(b))
                    taps(prod4, y4[:, 3, :], lambda k: u4[:, 3, k:k + SEQ], W4, lambda k: tap4[:, 4 * b + 3, k:k + 1])
                for n in range(2, 2 * UNITS):
                    pool.wait_ge(sem("g_row"), n - 1)
                    diagonal(n)
                for l in range(7):
                    for q in range(HG, UNITS):
                        if l == 0:
                            pool.wait_ge(sem("g_AQ"), 2 * q + 1)
                        elif l == 1:
                            pool.wait_ge(sem("i_one"), q + 1)
                        else:
                            pool.wait_ge(sem("i_Y"), UNITS * (l - 2) + q + 1)
                        pool.tensor_tensor(Lm[q], A_[q], lvl[:, l:l + 1, :].broadcast_to([P, 4, P]), ALU.mult)\
                            .then_inc(sem("i_L1"), 1)
                for t in range(NT):
                    root(ors[:, t, :], oms[:, t, :], oss[:, t, :], P, ("g_oss", "g_ors"), t + 1)

            def mixer3():
                norm(7)
                pool.wait_ge(w_used, first["kv"])
                pool.memset(smask[:], 1.0)
                pool.memset(sbig[:], 0.0)
                pool.memset(neg_one[:], -1.0)
                step(pool.memset(neg_tri[:], -1.0))
                for c in (0, 2 * P):
                    select(smask[:, c:c + P], ALU.is_ge, 0.0, -1, [[1, P]], -1)
                select(sbig[:], ALU.is_ge, -BIG, -1, [[1, P]], -1)
                select(neg_tri[:], ALU.is_ge, 0.0, 0, [[-1, P]], 1).then_inc(sem("s_masks"), 1)
                for i in range(2):
                    for t in range(NT):
                        root(krs[:, i, t, :], kms[:, i, t, :], kss[:, i, t, :], P, ("s_kss", "s_krs"), 2 * i + t + 1)

            norm(0)
            mixer1()
            norm(2)
            mixer2()
            norm(5)
            norm(6)
            mixer3()
            norm(9)
            norm(10)

        @block.vector
        def _(dve):
            split_to = [0]
            steps = [0]

            def step(ins):
                steps[0] += 1
                ins.then_inc(sem("dve_step"), 1)
                dve.wait_ge(sem("dve_step"), steps[0])

            def split(n):
                while split_to[0] < min(n, NSLOT):
                    w = split_to[0]
                    dve.wait_ge(w_hi, w + 1)
                    dve.tensor_tensor(wlo[w % SPLIT][:], raw[w % RAW][:], whi[w % SPLIT][:].bitcast(F32),
                                      ALU.subtract).then_inc(w_lo, 1)
                    split_to[0] += 1

            def norm_scale(n, t):
                if n == 8:
                    dve.wait_ge(sem("turn_T"), 4 * turn("n7") + 2 * t + 2)
                else:
                    dve.wait_ge(sem("norm_rstd"), nth(n, t))
                c = 2 * (7 if n == 8 else n) + t
                dve.wait_ge(sem(f"gain_in{n % 2}"), 16 * (n // 2 + 1))
                dst = X if n == FINAL else xs
                dve.scalar_tensor_tensor(out=dst[:, t, :], in0=X[:, t, :], scalar=rstd[:, c:c + 1],
                                         in1=gain[n % 2][:], op0=ALU.mult, op1=ALU.mult)\
                   .then_inc(sem("final_x" if n == FINAL else "turn_in"), 1)

            def turn_lo(name, t, hi=None, lo=None):
                hi, lo = hi or xThi, lo or xTlo
                for b in range(2):
                    dve.wait_ge(sem("turn_hi"), 4 * turn(name) + 2 * t + b + 1)
                    part = (slice(None), slice(4 * b, 4 * b + 4), slice(t * P, (t + 1) * P))
                    dve.tensor_tensor(lo[part], bank[4 + b][:].rearrange("p (k c) -> p k c", k=4),
                                      hi[part].bitcast(F32), ALU.subtract).then_inc(sem("turn_lo"), 1)

            def norm(n, follows, hi=None, lo=None, before=None):
                for t in range(NT):
                    if t and n in (4, 7):
                        split(first[follows] + 2)
                    if before:
                        before(t)
                    if t and follows:
                        split(first[follows] + 2)
                    norm_scale(n, t)
                    if t == 0 and follows:
                        split(first[follows] + 1)
                    turn_lo(f"n{n}", t, hi, lo)

            def residual(name, scale):
                m = WIDE.index(name)

                def add(t):
                    wait_wide(dve, m, t)
                    for h in range(2):
                        ins = dve.scalar_tensor_tensor(
                            out=X[:, t, h * 512:(h + 1) * 512], in0=out_bank(t, h)[:], scalar=scale,
                            in1=X[:, t, h * 512:(h + 1) * 512], op0=ALU.mult, op1=ALU.add)
                    ins.then_inc(sem("x_ready"), 1)
                split(last_group(name) + SPLIT)
                return add

            def ffn(f):
                def hidden_lo(j):
                    dve.wait_ge(sem("ffn_hi"), NBLK * f + j + 1)
                    dve.tensor_tensor(hTlo[:, 2 * j:2 * j + 2, :], bank[4 + j % 2][:].rearrange("p (k c) -> p k c", k=2),
                                      hThi[:, 2 * j:2 * j + 2, :].bitcast(F32), ALU.subtract).then_inc(sem("ffn_lo"), 1)

                for j in range(NBLK):
                    s = up_slot(f, j)
                    if f >= 2 and j == BESIDE - 2:
                        dve.wait_ge(sem("p_hi"), f - 1)
                        dve.tensor_tensor(pTlo[:].rearrange("p k t -> p (k t)"), bank[6][:],
                                          pThi[:].rearrange("p k t -> p (k t)").bitcast(F32), ALU.subtract).then_inc(sem("p_lo"), 1)
                    if f >= 2 and j == BESIDE:
                        split(first[f"ple_p{f - 2}"] + SPLIT)
                        hidden_lo(j - 1)
                    split(s + (0 if j == 0 else 1) + SPLIT)
                    for t in range(NT):
                        if t:
                            split(s + 1 + SPLIT)
                        dve.wait_ge(sem("ffn_silu"), 2 * (NBLK * f + j) + t + 1)
                        if f or j >= 2:
                            dve.wait_ge(sem("ffn_T"), NBLK * f + j - 1)
                        dve.tensor_tensor(hnat[:, j % 2, t, :], silu[:, j % 2, t, :],
                                          bank[2 * (j % 2) + t][:, 256:512], ALU.mult).then_inc(sem("ffn_h"), 1)
                    split(s + 2 + SPLIT)
                    if j and not (f >= 2 and j == BESIDE):
                        hidden_lo(j - 1)
                    if f == 0 and j == 4:
                        setup()
                split(first[f"down{f}"] + SPLIT)
                hidden_lo(NBLK - 1)

            def setup():
                dve.wait_ge(sem("setup_T"), 1)
                dve.tensor_copy(chan[:].rearrange("p v c -> p (v c)"), bank[7][:, 0:4 * CT])
                dve.tensor_copy(tap[:].rearrange("p c k -> p (c k)"), bank[7][:, 16:16 + CT * TAPS])
                dve.tensor_copy(tap4[:].rearrange("p c k -> p (c k)"), bank[7][:, 160:160 + QKV * W4]).then_inc(sem("m_tap"), 1)
                dve.wait_ge(sem("narrow_hi"), 1)
                dve.tensor_tensor(narrow_lo[:], narrow[:], narrow_hi[:].bitcast(F32), ALU.subtract).then_inc(sem("narrow_lo"), 1)

            def mixer1():
                s = first["mix"]
                taps = [0]

                def convolve(n):
                    for k in range(taps[0], min(taps[0] + n, TAPS)):
                        for c in range(CT - 2):
                            src = u[:, c, k:k + SEQ]
                            if k == 0:
                                ins = dve.tensor_scalar(y[:, c, :], src, tap[:, c, k:k + 1], chan[:, 0, c:c + 1], ALU.mult, ALU.add)
                            else:
                                dve.wait_ge(sem("c_conv_d"), 2 * (k - 1) + c + 1)
                                ins = dve.scalar_tensor_tensor(out=y[:, c, :], in0=src, scalar=tap[:, c, k:k + 1],
                                                               in1=y[:, c, :], op0=ALU.mult, op1=ALU.add)
                            ins.then_inc(sem("c_conv_d"), 1)
                    taps[0] = min(taps[0] + n, TAPS)

                def add_eps(i, src):
                    dve.wait_ge(sem("c_sum"), i + 2)
                    dve.tensor_scalar(stat[:, i, :], src, EPS, None, ALU.add).then_inc(sem("c_eps"), 1)

                def scale_y(i, row):
                    dve.wait_ge(sem("c_row"), i + 1)
                    if i:
                        dve.wait_ge(sem("c_sq"), 2)
                    dve.tensor_tensor(y[:], y[:], row.unsqueeze(1).broadcast_to([P, CT, SEQ]), ALU.mult)\
                       .then_inc(sem("c_scaled"), 1)

                split(s + 5 + SPLIT)
                dve.wait_ge(sem("m_sig"), 1)
                dve.wait_ge(sem("m_zero"), 1)
                for i in range(2):
                    ins = dve.tensor_tensor(u[:, 2 * i:2 * i + 2, PAD:], bank[2 + i][:].rearrange("p (c t) -> p c t", c=2),
                                            gs[:, 2 * i:2 * i + 2, :], ALU.mult)
                ins.then_inc(sem("m_u"), 1)
                dve.wait_ge(sem("m_fl"), 1)
                step(dve.tensor_tensor(zf[:], bank[6][:, 0:NT * H1].rearrange("p (t h) -> p t h", t=NT),
                                       forget_b[:].unsqueeze(1).broadcast_to([P, NT, H1]), ALU.add))
                dve.scalar_tensor_tensor(out=zfe[:], in0=zf[:], scalar=-1.0, in1=zf[:], op0=ALU.mult, op1=ALU.min)\
                   .then_inc(sem("m_z"), 1)
                dve.wait_ge(sem("m_u"), 1)
                split(s + 6 + SPLIT)
                convolve(2)
                dve.wait_ge(sem("m_ln"), 1)
                dve.scalar_tensor_tensor(out=lf[:], in0=zf[:], scalar=0.0, in1=zfe[:], op0=ALU.min, op1=ALU.subtract)\
                   .then_inc(sem("m_lf"), 1)
                for i in range(4):
                    convolve((3, 4, 4, 1)[i])
                    split(s + 7 + i + SPLIT)
                dve.wait_ge(sem("m_mask"), 1)
                for h in range(H1):
                    convolve(min(h, 3))
                    dve.wait_ge(sem("at_S"), h + 1)
                    if h >= 2:
                        dve.wait_ge(sem("at_exp"), h - 1)
                    dve.scalar_tensor_tensor(out=p1[:, h % 2, 0:P], in0=bank[h % 2][:, 0:P], scalar=cum[:, 0, h:h + 1],
                                             in1=mask1[:, P:SEQ], op0=ALU.add, op1=ALU.add)
                    step(dve.scalar_tensor_tensor(out=p1[:, h % 2, P:384], in0=bank[h % 2][:, P:384],
                                                  scalar=cum[:, 1, h:h + 1], in1=mask1[:], op0=ALU.add, op1=ALU.add))
                    dve.tensor_reduce(mx[:, h % 2, 0:1], p1[:, h % 2, 0:P], AX_X, ALU.max)
                    step(dve.tensor_reduce(mx[:, h % 2, 1:2], p1[:, h % 2, P:384], AX_X, ALU.max))
                    dve.tensor_scalar(nmx[:, h % 2, :], mx[:, h % 2, :], -1.0, None, ALU.mult).then_inc(sem("at_nm"), 1)
                    if h == H1 - 3:
                        convolve(TAPS)
                    if h == H1 - 1:
                        dve.wait_ge(sem("c_sum"), 1)
                        dve.tensor_tensor(y[:], y[:], bank[7][:, 0:SEQ].unsqueeze(1).broadcast_to([P, CT, SEQ]), ALU.subtract)\
                           .then_inc(sem("c_centred"), 1)
                add_eps(0, bank[7][:, SEQ:SEQ + NT])
                dve.wait_ge(sem("at_exp"), H1)
                step(dve.reciprocal(rinv[:], rsum[:]))
                dve.wait_ge(sem("at_pv"), H1)
                for t in range(NT):
                    dve.tensor_tensor(yA[:, t, :].rearrange("p (h c) -> p h c", h=H1),
                                      bank[4 + t][:].rearrange("p (h c) -> p h c", h=H1),
                                      rinv[:, t, :].unsqueeze(2).broadcast_to([P, H1, D1]), ALU.mult).then_inc(sem("a_y"), 1)
                scale_y(0, bank[6][:, 0:SEQ])
                for t in range(NT):
                    dve.wait_ge(sem("a_rs"), t + 1)
                    dve.scalar_tensor_tensor(out=yA[:, t, :], in0=yA[:, t, :], scalar=yrs[:, t:t + 1], in1=attn_gain[:],
                                             op0=ALU.mult, op1=ALU.mult).then_inc(sem("a_in"), 1)
                for t in range(NT):
                    dve.wait_ge(sem("a_hi"), t + 1)
                    dve.tensor_tensor(xTlo[:, CT:KD, t * P:(t + 1) * P], bank[t][:].rearrange("p (k c) -> p k c", k=4),
                                      xThi[:, CT:KD, t * P:(t + 1) * P].bitcast(F32), ALU.subtract).then_inc(sem("a_lo"), 1)
                add_eps(1, bank[4][:, 0:NT])
                scale_y(1, bank[4][:, SEQ:])
                dve.wait_ge(sem("c_hi"), 1)
                for c in range(CT):
                    ins = dve.scalar_tensor_tensor(out=xTlo[:, c, :], in0=y[:, c, :], scalar=chan[:, 3, c:c + 1],
                                                   in1=xThi[:, c, :].bitcast(F32), op0=ALU.mult, op1=ALU.subtract)
                ins.then_inc(sem("c_lo"), 1)

            def by_head(v, t, g):
                return vec[:, v, t, 4 * g:4 * g + 4].unsqueeze(2).broadcast_to([P, 4, P])

            def mixer2():
                s = first["gdn"]
                split(s + 1 + SPLIT)
                dve.wait_ge(sem("g_ab"), 1)
                z7 = bank[7][:, 0:4 * H2].rearrange("p (t h) -> p t h", t=NT)
                dve.tensor_tensor(zab[:, :, 0:H2], z7[:, :, 0:H2], dt_bias[:].unsqueeze(1).broadcast_to([P, NT, H2]), ALU.add)
                step(dve.tensor_copy(zab[:, :, H2:], z7[:, :, H2:]))
                dve.scalar_tensor_tensor(out=eab[:], in0=zab[:], scalar=-1.0, in1=zab[:], op0=ALU.mult, op1=ALU.min)\
                   .then_inc(sem("g_z"), 1)
                dve.wait_ge(sem("g_ln"), 1)
                dve.scalar_tensor_tensor(out=gl[:, :, H2:], in0=zab[:, :, H2:], scalar=0.0, in1=eab[:, :, H2:],
                                         op0=ALU.min, op1=ALU.subtract)
                step(dve.scalar_tensor_tensor(out=gl[:, :, 0:H2], in0=zab[:, :, 0:H2], scalar=0.0, in1=eab[:, :, 0:H2],
                                              op0=ALU.max, op1=ALU.add))
                dve.scalar_tensor_tensor(out=gl[:, :, 0:H2], in0=gl[:, :, 0:H2], scalar=-1.0,
                                         in1=a_log[:].unsqueeze(1).broadcast_to([P, NT, H2]), op0=ALU.mult, op1=ALU.mult)\
                   .then_inc(sem("g_g"), 1)
                for b in range(2):
                    split(s + 2 * b + 1 + SPLIT)
                    dve.wait_ge(sem("g_gate"), b + 1)
                    for t in range(NT):
                        v = sg[:, t, b * 512:(b + 1) * 512].rearrange("p (h c) -> p h c", h=4)
                        dve.tensor_tensor(v, v, head_gain[:, GDNG:GDNG + 1, :].broadcast_to([P, 4, P]), ALU.mult)\
                           .then_inc(sem("g_sg"), 1)
                    split(s + 2 * b + 2 + SPLIT)
                s += 4
                dve.wait_ge(sem("g_zero"), 1)
                for b in range(6):
                    split(s + 2 * b + 1 + SPLIT)
                    if b == 5:
                        dve.wait_ge(sem("g_lkq"), 1)
                        dve.wait_ge(sem("g_cum_in"), 1)
                        lq, lk, lb = lkq[:, :, 0:H2], lkq[:, :, H2:], gl[:, :, H2:]
                        dve.scalar_tensor_tensor(out=vec[:, ROWQ], in0=lq, scalar=-0.5 * math.log(P), in1=vec[:, G_],
                                                 op0=ALU.add, op1=ALU.add)
                        dve.tensor_copy(vec[:, BETA], lb)
                        dve.tensor_tensor(vec[:, TMP], lb, vec[:, G_], ALU.add)
                        step(dve.tensor_tensor(vec[:, COL], lk, vec[:, G_], ALU.subtract))
                        dve.tensor_tensor(vec[:, CVN], vec[:, COL], vec[:, GL], ALU.add)
                        dve.tensor_tensor(vec[:, ROWA], vec[:, TMP], lk, ALU.add).then_inc(sem("g_vec"), 1)
                    dve.wait_ge(sem("g_u"), b + 1)
                    if b:
                        dve.wait_ge(*y4_free(b))
                    for k in range(W4):
                        for c in range(3):
                            w, src = tap4[:, 4 * b + c, k:k + 1], u4[:, c, k:k + SEQ]
                            if k == 0:
                                ins = dve.tensor_scalar(y4[:, c, :], src, w, None, ALU.mult)
                            else:
                                dve.wait_ge(sem("g_conv"), 3 * (W4 * b + k - 1) + c + 1)
                                ins = dve.scalar_tensor_tensor(out=y4[:, c, :], in0=src, scalar=w, in1=y4[:, c, :],
                                                               op0=ALU.mult, op1=ALU.add)
                            ins.then_inc(sem("g_conv"), 1)
                    split(s + 2 * b + 2 + SPLIT)
                dve.wait_ge(sem("g_masks"), 1)

                def masked(n):
                    dve.wait_ge(sem("g_row"), n + 1)
                    if n >= 2:
                        dve.wait_ge(sem("g_AQ"), n - 1)
                    dve.tensor_tensor(DEC[n % 2][:], bank[n % 4][:].rearrange("p (h c) -> p h c", h=4),
                                      maskT[:].unsqueeze(1).broadcast_to([P, 4, P]), ALU.add).then_inc(sem("g_decm"), 1)
                masked(0)
                for n in range(2 * UNITS):
                    if n + 1 < 2 * UNITS:
                        masked(n + 1)
                    dve.wait_ge(sem("g_dec"), n + 1)
                    dve.wait_ge(sem("g_kq"), n + 1)
                    dve.tensor_tensor((QK if n % 2 else A_)[n // 2], bank[4 + n % 4][:].rearrange("p (h c) -> p h c", h=4),
                                      DEC[n % 2][:], ALU.mult).then_inc(sem("g_AQ"), 1)
                dve.wait_ge(sem("g_vexp"), 1)
                for q in range(UNITS):
                    t, g = q // HG, q % HG
                    dve.wait_ge(sem("g_vn"), q + 1)
                    dve.tensor_tensor(bv[:, t, g * 512:(g + 1) * 512].rearrange("p (h c) -> p h c", h=4),
                                      bank[q][:].rearrange("p (h c) -> p h c", h=4), by_head(BETA, t, g), ALU.mult)\
                       .then_inc(sem("g_bv"), 1)

                def level_mask(l):
                    for q in range(HG):
                        if l == 1:
                            dve.wait_ge(sem("i_one"), q + 1)
                        elif l:
                            dve.wait_ge(sem("i_Y"), UNITS * (l - 2) + q + 1)
                        dve.tensor_tensor(Lm[q], A_[q], lvl[:, l:l + 1, :].broadcast_to([P, 4, P]), ALU.mult)\
                           .then_inc(sem("i_L0"), 1)
                level_mask(0)
                for q in range(UNITS):
                    dve.wait_ge(*((sem("i_L0"), q + 1) if q < HG else (sem("i_L1"), q - HG + 1)))
                    if q == 0:
                        dve.wait_ge(sem("g_bv"), UNITS)
                    dve.tensor_tensor(U[q], ident[:].unsqueeze(1).broadcast_to([P, 4, P]), Lm[q], ALU.subtract)\
                       .then_inc(sem("i_one"), 1)
                level_mask(1)
                for l in range(1, 6):
                    b = 2 ** l
                    level_mask(l + 1)
                    for q in range(UNITS):
                        v = T[q].rearrange("p h (i j) -> p (h i) j", j=2 * b)[:, :, 0:b]
                        dve.wait_ge(sem("i_Z"), UNITS * (l - 1) + q + 1)
                        dve.wait_ge(*((sem("i_U"), q + 1) if l == 1 else (sem("i_T"), UNITS * (l - 2) + q + 1)))
                        dve.tensor_tensor(v, v, bank[q][:, 256:512].rearrange("p (n j) -> p n j", j=b), ALU.subtract)\
                           .then_inc(sem("i_T"), 1)
                for q in range(UNITS):
                    dve.wait_ge(sem("i_Z"), UNITS * 5 + q + 1)
                    dve.tensor_tensor(U[q][0:64], U[q][0:64], bank[4 + q][0:64, :].rearrange("p (h c) -> p h c", h=4), ALU.subtract)\
                       .then_inc(sem("i_T"), 1)

                def head_sums(t):
                    dve.wait_ge(sem("g_osq"), t + 1)
                    dve.tensor_reduce(oss[:, t, :], bv[:, 0, :].rearrange("p (h c) -> p h c", h=H2), AX_X, ALU.add)\
                       .then_inc(sem("g_oss"), 1)

                def gated(t):
                    dve.wait_ge(sem("g_ors"), t + 1)
                    v = o2[:, t, :].rearrange("p (h c) -> p h c", h=H2)
                    step(dve.tensor_tensor(v, v, ors[:, t, :].unsqueeze(2).broadcast_to([P, H2, P]), ALU.mult))
                    dve.tensor_tensor(o2[:, t, :], o2[:, t, :], sg[:, t, :], ALU.mult).then_inc(sem("turn_in"), 1)

                dve.wait_ge(sem("g_sg"), 4)
                for t in range(NT):
                    for g in range(HG):
                        n = HG * t + g
                        if t:
                            dve.wait_ge(sem("r_kS"), g + 1)
                            step(dve.tensor_tensor(tq[:], bank[4 + g][:].rearrange("p (h c) -> p h c", h=4), by_head(CKS, t, g), ALU.mult))
                            if g:
                                dve.wait_ge(sem("r_vn"), n)
                            dve.tensor_tensor(r2[:], bv[:, t, g * 512:(g + 1) * 512].rearrange("p (h c) -> p h c", h=4), tq[:],
                                              ALU.subtract).then_inc(sem("r_r"), 1)
                            dve.wait_ge(sem("r_qS"), g + 1)
                            step(dve.tensor_tensor(vne[:], bank[0][:].rearrange("p (h c) -> p h c", h=4), by_head(CQS, t, g), ALU.mult))
                            dve.wait_ge(sem("r_o"), n + 1)
                            dve.tensor_tensor(o2[:, t, g * 512:(g + 1) * 512], bank[2][:], vne[:].rearrange("p h c -> p (h c)"), ALU.add)\
                               .then_inc(sem("r_o1"), 1)
                            if g == 0:
                                head_sums(0)
                        else:
                            dve.wait_ge(sem("r_vn_in"), n + 1)
                            if g:
                                dve.wait_ge(sem("r_S"), g)
                            dve.tensor_tensor(vne[:], vn[:], by_head(CVN, t, g), ALU.mult).then_inc(sem("r_vne"), 1)
                gated(0)
                head_sums(1)
                turn_lo("gdn", 0)
                gated(1)
                turn_lo("gdn", 1)

            def embed(i, n):
                add = residual(f"down{2 + i}", 1.0)
                norm(n, f"ple_g{i}", before=add)
                split(last_group(f"ple_g{i}") + SPLIT)

                def add_gated(t):
                    dve.wait_ge(sem("gate_s"), 2 * i + t + 1)
                    dve.wait_ge(sem("pp_in"), 2 * i + t + 1)
                    step(dve.tensor_tensor(gate_s[:, t, :], gate_s[:, t, :], pp[:, t, :], ALU.mult))
                    dve.tensor_tensor(X[:, t, :], X[:, t, :], gate_s[:, t, :], ALU.add).then_inc(sem("x_ready"), 1)
                return add_gated

            def head_norm(i, t, g_):
                dve.wait_ge(sem("s_krs"), 2 * i + t + 1)
                v = kn[:, t, :].rearrange("p (h c) -> p h c", h=H2)
                w = xs[:, t, :].rearrange("p (h c) -> p h c", h=H2)
                if i:
                    dve.wait_ge(sem("s_kT"), 4)
                else:
                    dve.wait_ge(sem("turn_T"), 4 * turn("n8") + 4)
                step(dve.tensor_tensor(w, v, krs[:, i, t, :].unsqueeze(2).broadcast_to([P, H2, P]), ALU.mult))
                dve.tensor_tensor(w, w, head_gain[:, g_:g_ + 1, :].broadcast_to([P, H2, P]), ALU.mult).then_inc(sem("s_rows"), 1)

            def mixer3(add):
                s = first["kv"]

                def head_sums(i):
                    for t in range(NT):
                        dve.wait_ge(sem("s_sq"), 2 * i + t + 1)
                        dve.tensor_reduce(kss[:, i, t, :], sq_s[:].rearrange("p (h c) -> p h c", h=H2), AX_X, ALU.add)\
                           .then_inc(sem("s_kss"), 1)

                def softplus(heads):
                    for h in heads:
                        dve.wait_ge(sem("sb_ln"), h + 1)
                        step(dve.scalar_tensor_tensor(out=sab[:, h, :], in0=z_bank(h)[:, 0:384], scalar=0.0,
                                                      in1=sab[:, h, :], op0=ALU.max, op1=ALU.add))
                        dve.tensor_tensor(sab[:, h, :], sab[:, h, :], smask[:], ALU.mult).then_inc(sem("sb_sp"), 1)

                norm(7, "kv", before=add)
                split(s + 2 + SPLIT)
                norm(8, None, xThi2, xTlo2)
                split(s + 4 + SPLIT)
                head_sums(0)
                dve.tensor_scalar(head_gain[:, QG, :], head_gain[:, QG, :], P ** -0.5, None, ALU.mult).then_inc(sem("s_qg"), 1)
                for t in range(NT):
                    head_norm(0, t, KG)
                split(s + 8 + SPLIT)
                head_sums(1)
                dve.wait_ge(sem("s_qg"), 1)
                for t in range(NT):
                    head_norm(1, t, QG)
                split(s + 10 + SPLIT)
                dve.wait_ge(sem("s_masks"), 1)
                softplus(range(6))
                split(s + 12 + SPLIT)
                softplus((6, 7))
                for t in range(NT):
                    turn_lo("sb", t)

            norm(0, "up0")
            ffn(0)
            add = residual("down0", 0.5)
            norm(1, "mix", before=add)
            mixer1()
            add = residual("mix_out", 1.0)
            norm(2, "up1", before=add)
            ffn(1)
            add = residual("down1", 0.5)
            def final_norm(t):
                add(t)
                norm_scale(FINAL, t)
            norm(4, "gdn", before=final_norm)
            mixer2()
            add = residual("gdn_out", 1.0)
            norm(5, "up2", before=add)
            ffn(2)
            add = embed(0, 6)
            mixer3(add)
            add = residual("sb_out", 1.0)
            norm(9, "up3", before=add)
            ffn(3)
            add = embed(1, 10)
            for t in range(NT):
                add(t)

        @block.tensor
        def _(pe):
            xT, hT, pT, xT2 = (xThi, xTlo), (hThi, hTlo), (pThi, pTlo), (xThi2, xTlo2)

            def passes(psum, lhs, rhs, start, stop):
                pe.matmul(psum, lhs[0], rhs[0], start=start, stop=False, skip_group_check=True)
                pe.matmul(psum, lhs[0], rhs[1], start=False, stop=False, skip_group_check=True)
                return pe.matmul(psum, lhs[1], rhs[0], start=False, stop=stop, skip_group_check=True)

            def ring(w):
                return whi[w % SPLIT], wlo[w % SPLIT]

            def rows(w, t, src, k0, nk, psums, begins, ends):
                for k in range(nk):
                    for c, psum in enumerate(psums):
                        at = (k * len(psums) + c) * 512
                        ins = passes(psum[:], [x[:, k0 + k, t * P:(t + 1) * P] for x in src],
                                     [x[:, at:at + 512] for x in ring(w)], begins and k == 0, ends and k == nk - 1)
                return ins

            def turn_T(name, t, wait=None):
                pe.wait_ge(*(wait or (sem("turn_in"), turned_in(name, t))))
                for b in range(2):
                    before = 4 * turn(name) + 2 * t + b - 1
                    if before > 0:
                        pe.wait_ge(sem("turn_lo"), before)
                    for k in range(4):
                        ins = pe.transpose(bank[4 + b][:, k * P:(k + 1) * P],
                                           xs[:, t, (4 * b + k) * P:(4 * b + k + 1) * P], ident[:])
                    ins.then_inc(sem("turn_T"), 1)

            def turned(name, t):
                pe.wait_ge(sem("turn_lo"), 4 * turn(name) + 2 * t + 2)

            def wide(name, src, ready=None, middle=None, pairs=None, order=None, k_ready=None):
                s, n = first[name], wide_slots[name]
                order = order or [(i, t) for i in range(n - SPLIT) for t in range(NT)] + \
                    [(i, t) for t in range(NT) for i in range(n - SPLIT, n)]
                for i, t in order:
                    if t == 0:
                        pe.wait_ge(w_lo, s + i + 1)
                        if ready:
                            ready(i)
                    if i == 0 and k_ready:
                        k_ready(t)
                    if (i, t) == (n - 1, NT - 1) and middle:
                        middle()
                    k0 = 2 * (pairs[i] if pairs else i)
                    ins = rows(s + i, t, src, k0, 2, [out_bank(t, 0), out_bank(t, 1)], i == 0, i == n - 1)
                    if t == NT - 1:
                        ins.then_inc(w_used, 1)
                    elif i == n - 1:
                        ins.then_inc(sem("wide_mm0"), 1)

            def block_rows(s, src, banks, k_ready=None, tilewise=False, done0=None, free=None):
                order = [(h, t) for h in range(2) for t in range(NT)]
                if tilewise:
                    order.sort(key=lambda x: x[1])
                seen = set()
                for h, t in order:
                    if h == 0 and k_ready:
                        k_ready(t)
                    if h not in seen:
                        pe.wait_ge(w_lo, s + h + 1)
                        seen.add(h)
                    if h == 0 and free:
                        free(t)
                    ins = rows(s + h, t, src, 4 * h, 4, [banks[t]], h == 0, h == 1)
                    if h == 1 and t == 0 and done0:
                        ins.then_inc(sem(done0), 1)
                    if t == NT - 1:
                        ins.then_inc(w_used, 1)

            def block_cols(s, src, banks, k_ready=None):
                tiles = [slice(0, SEQ)] if k_ready is None else [slice(t * P, (t + 1) * P) for t in range(NT)]
                for t, tok in enumerate(tiles):
                    for h in range(2):
                        if h == 0 and k_ready:
                            k_ready(t)
                        if t == 0:
                            pe.wait_ge(w_lo, s + h + 1)
                        for k in range(4):
                            for c in range(4):
                                at = k * 512 + c * P
                                off = (c % 2) * SEQ
                                ins = passes(banks[c // 2][:, off + tok.start:off + tok.stop],
                                             [x[:, at:at + P] for x in ring(s + h)],
                                             [x[:, 4 * h + k, tok] for x in src],
                                             t == 0 and h == 0 and k == 0 and c % 2 == 0, h == 1 and k == 3)
                        if t == len(tiles) - 1:
                            ins.then_inc(w_used, 1)

            def narrow_rows(psum, c0, n, src):
                for t in range(NT):
                    for k in range(KD):
                        ins = passes(psum[:, t * n:(t + 1) * n], [x[:, k, t * P:(t + 1) * P] for x in src],
                                     [x[:, k, c0:c0 + n] for x in (narrow_hi, narrow_lo)], t == 0 and k == 0, k == KD - 1)
                return ins

            def tile_ready(name):
                def ready(t):
                    if t:
                        turn_T(name, t)
                    turned(name, t)
                return ready

            def ffn(f):
                def hidden_T(j):
                    pe.wait_ge(sem("ffn_h"), 2 * (NBLK * f + j) + 2)
                    if j >= 2:
                        pe.wait_ge(sem("ffn_lo"), NBLK * f + j - 1)
                    for k in range(2):
                        for t in range(NT):
                            ins = pe.transpose(bank[4 + j % 2][:, k * SEQ + t * P:k * SEQ + (t + 1) * P],
                                               hnat[:, j % 2, t, k * P:(k + 1) * P], ident[:])
                    ins.then_inc(sem("ffn_T"), 1)

                name = turn_of_up[f]
                for j in range(NBLK):
                    if f >= 2 and j == BESIDE:
                        ple_product(f - 2, lambda: hidden_T(j - 1))
                    block_rows(up_slot(f, j), xT, [bank[2 * (j % 2) + t] for t in range(NT)],
                               k_ready=tile_ready(name) if j == 0 else None, tilewise=j == 0, done0="ffn_mm0",
                               free=(lambda t: pe.wait_ge(sem("ffn_h"), 2 * (NBLK * f + j - 2) + t + 1)) if j >= 2 else None)
                    if j and not (f >= 2 and j == BESIDE):
                        hidden_T(j - 1)
                    if f >= 2 and j == BESIDE - 3:
                        p_turn(f - 2)
                    if f == 0 and j == 2:
                        setup()

                def ready(i):
                    if i == 1:
                        hidden_T(NBLK - 1)
                    if i == 0:
                        if f == 0:
                            pe.wait_ge(sem("m_tap"), 1)
                        pe.wait_ge(sem("ffn_h"), 2 * (NBLK * f + NBLK - 2) + 2)
                    pe.wait_ge(sem("ffn_lo"), NBLK * f + i + 1)
                return ready

            def setup():
                pe.wait_ge(sem("consts_in"), 16 * N_LOADS)
                pe.transpose(bank[7][:, 0:4 * CT], row_chan[:], ident[0:4 * CT, 0:4 * CT])
                for c in range(CT):
                    pe.transpose(bank[7][:, 16 + c * TAPS:16 + (c + 1) * TAPS], row_tap[:, c * P:(c + 1) * P],
                                 ident[0:TAPS, 0:TAPS])
                for c in range(QKV):
                    ins = pe.transpose(bank[7][:, 160 + c * W4:160 + (c + 1) * W4], row_tap4[:, c * P:(c + 1) * P],
                                       ident[0:W4, 0:W4])
                ins.then_inc(sem("setup_T"), 1)

            def mixer1():
                s = first["mix"]
                block_rows(s, xT, [bank[0], bank[1]], k_ready=tile_ready("n1"), tilewise=True)
                pe.wait_ge(sem("x_ready"), 2)
                block_cols(s + 2, xT, [bank[2], bank[3]])
                pe.wait_ge(sem("narrow_lo"), 1)
                narrow_rows(bank[6], 0, H1, xT).then_inc(sem("m_fl"), 1)
                pe.wait_ge(sem("m_v"), 1)
                block_cols(s + 4, xT, [bank[0], bank[1]])
                block_cols(s + 6, xT, [bank[4], bank[5]])
                pe.wait_ge(sem("m_u"), 1)
                pe.wait_ge(sem("m_lf"), 1)
                pe.matmul(bank[6][:, 32:32 + H1], upto[:], lf[:, 0, :], start=True, stop=True)
                pe.matmul(bank[6][:, 32 + H1:32 + 2 * H1], ones[:], lf[:, 0, :], start=True, stop=False)
                pe.matmul(bank[6][:, 32 + H1:32 + 2 * H1], upto[:], lf[:, 1, :], start=False, stop=True).then_inc(sem("m_cum"), 1)
                block_cols(s + 8, xT, [bank[0], bank[1]])
                pe.wait_ge(sem("m_cum_in"), 1)
                for t in range(NT):
                    ins = pe.transpose(bank[6][0:H1, 128 + t * P:128 + (t + 1) * P], cum[:, t, :], ident[:])
                ins.then_inc(sem("m_cumT"), 1)

                def layer_norm(i):
                    if i == 0:
                        pe.wait_ge(sem("c_conv_d"), 2 * TAPS)
                        pe.wait_ge(sem("c_conv_p"), TAPS - 1)
                        for c in range(CT):
                            ins = pe.matmul(bank[7][:, 0:SEQ], mean_of[:], y[:, c, :], start=c == 0, stop=c == CT - 1)
                        ins.then_inc(sem("c_sum"), 1)
                    elif i in (1, 3):
                        pe.wait_ge(sem("c_sq"), 1 + i // 2)
                        for t in range(NT):
                            dst = bank[7][:, SEQ + t:SEQ + t + 1] if i == 1 else bank[4][:, t:t + 1]
                            for c in range(CT):
                                ins = pe.matmul(dst, ysq[:, c, t * P:(t + 1) * P], mean_of[:, 0:1], start=c == 0, stop=c == CT - 1)
                        ins.then_inc(sem("c_sum"), 1)
                    else:
                        pe.wait_ge(sem("c_root"), i // 2)
                        for t in range(NT):
                            dst = bank[6][:, t * P:(t + 1) * P] if i == 2 else bank[4][:, SEQ + t * P:SEQ + (t + 1) * P]
                            ins = pe.matmul(dst, stat_r[:, i // 2 - 1, t:t + 1].broadcast_to([P, P]), ident[:], start=True, stop=True)
                        ins.then_inc(sem("c_row"), 1)

                pe.wait_ge(sem("m_mask"), 1)
                pe.wait_ge(sem("m_q"), 1)
                pe.wait_ge(sem("m_k"), 1)
                pe.wait_ge(sem("m_cumT_in"), 1)
                for i in range(H1 + 3):
                    if i < H1:
                        h = i
                        if h >= 2:
                            pe.wait_ge(sem("at_nm"), h - 1)
                        S_ = bank[h % 2]
                        for t in range(NT):
                            c = slice(0, P) if t == 0 else slice(P, 384)
                            n = P * (t + 1)
                            pe.matmul(S_[:, c], qz[:, h, t * P:(t + 1) * P], kT[:, h // 2, 0:n], start=t == 0, stop=False,
                                      skip_group_check=True)
                            ins = pe.matmul(S_[:, c], pick[:, h, :], cumT[:, 0:n], start=False, stop=True, skip_group_check=True)
                        ins.then_inc(sem("at_S"), 1)
                    if 2 <= i <= H1 + 1:
                        h = i - 2
                        pe.wait_ge(sem("at_exp"), h + 1)
                        if h >= 2:
                            pe.wait_ge(sem("at_pT"), h - 1)
                        for c in range(3):
                            ins = pe.transpose(bank[2 + h % 2][:, c * P:(c + 1) * P], p2[:, h % 2, c * P:(c + 1) * P], ident[:])
                        ins.then_inc(sem("at_T"), 1)
                    if i >= 3:
                        h = i - 3
                        pe.wait_ge(sem("at_pT"), h + 1)
                        o = slice(h * D1, (h + 1) * D1)
                        pe.matmul(bank[4][:, o], pT1[:, h % 2, 0:P], v1[:, 0, o], start=True, stop=True)
                        pe.matmul(bank[5][:, o], pT1[:, h % 2, P:2 * P], v1[:, 0, o], start=True, stop=False)
                        pe.matmul(bank[5][:, o], pT1[:, h % 2, 2 * P:], v1[:, 1, o], start=False, stop=True).then_inc(sem("at_pv"), 1)
                    if i == H1 - 1:
                        layer_norm(0)
                    if i == H1 + 1:
                        layer_norm(1)
                layer_norm(2)
                for t in range(NT):
                    pe.wait_ge(sem("a_in"), t + 1)
                    for k in range(4):
                        ins = pe.transpose(bank[t][:, k * P:(k + 1) * P], yA[:, t, k * P:(k + 1) * P], ident[:])
                    ins.then_inc(sem("a_T"), 1)

                def ready(i):
                    if i == 0:
                        pe.wait_ge(sem("a_lo"), NT)
                        pe.wait_ge(sem("c_scaled"), 1)
                        layer_norm(3)
                    if i == 1:
                        layer_norm(4)
                    if i == 2:
                        pe.wait_ge(sem("c_lo"), 1)
                return ready

            def mixer2():
                s = first["gdn"]

                def squares(b):
                    pe.wait_ge(sem("g_sq"), b + 1)
                    for c in range(4):
                        for t in range(NT):
                            col = t * 2 * H2 + 4 * b + c
                            ins = pe.matmul(bank[6][:, col:col + 1], sq4[:, c, t * P:(t + 1) * P], ones[:, 0:1], start=True, stop=True)
                    ins.then_inc(sem("g_ss"), 1)
                for b in range(2):
                    block_rows(s + 2 * b, xT, [bank[2 * b], bank[2 * b + 1]], k_ready=tile_ready("n4") if b == 0 else None,
                               tilewise=b == 0)
                    if b == 0:
                        narrow_rows(bank[7], H1, 2 * H2, xT).then_inc(sem("g_ab"), 1)
                pe.wait_ge(sem("g_g"), 1)
                for t in range(NT):
                    pe.matmul(bank[7][:, 64 + t * H2:64 + (t + 1) * H2], upto[:], gl[:, t, 0:H2], start=True, stop=True)
                    ins = pe.matmul(bank[7][:, 80 + t * H2:80 + (t + 1) * H2], ones[:], gl[:, t, 0:H2], start=True, stop=True)
                ins.then_inc(sem("g_cum"), 1)
                s += 4
                for b in range(6):
                    pe.wait_ge(*((sem("g_gate"), b + 1) if b < 2 else (sem("g_u"), b - 1)))
                    block_cols(s + 2 * b, xT, [bank[2 * (b % 2)], bank[2 * (b % 2) + 1]])
                    if 1 <= b <= 4:
                        squares(b - 1)
                    if b == 4:
                        for g in range(HG):
                            for h in range(4):
                                ins = pe.transpose(bank[4 + g][:, h * P:(h + 1) * P], qkT[:, H2 + 4 * g + h, 0:P], ident[:])
                            ins.then_inc(sem("g_kn"), 1)
                pe.wait_ge(sem("g_knat"), HG)
                pe.wait_ge(sem("g_u"), 6)
                for n in range(2 * UNITS):
                    q, i = n // 2, n % 2
                    t, g = q // HG, q % HG
                    tok = slice(t * P, (t + 1) * P)
                    pe.wait_ge(sem("g_dg"), n + 1)
                    if n >= 4:
                        pe.wait_ge(sem("g_AQ"), n - 3)
                    pe.matmul(bank[n % 4][:], ones[:], DG[i][:].rearrange("p h c -> p (h c)"), start=True, stop=True)\
                      .then_inc(sem("g_row"), 1)
                    off = H2 if i == 0 else 0
                    for h in range(4):
                        ins = pe.matmul(bank[4 + n % 4][:, h * P:(h + 1) * P], qkT[:, H2 + 4 * g + h, tok],
                                        qkT[:, off + 4 * g + h, tok], start=True, stop=True)
                    ins.then_inc(sem("g_kq"), 1)
                pe.wait_ge(sem("g_v"), 2)
                for q in range(UNITS):
                    t, g = q // HG, q % HG
                    pe.wait_ge(sem("g_decm"), UNITS + q + 1)
                    for h in range(4):
                        ins = pe.transpose(bank[q][:, h * P:(h + 1) * P], vT[:, 4 * g + h, t * P:(t + 1) * P], ident[:])
                    ins.then_inc(sem("g_vn"), 1)
                pe.wait_ge(sem("g_AQ"), 2 * UNITS)

                def transposed(l, src):
                    for q in range(UNITS):
                        pe.wait_ge(*((sem("i_one"), q + 1) if l == 0 else (sem("i_T"), UNITS * (l - 1) + q + 1)))
                        for h in range(4):
                            ins = pe.transpose(bank[4 + q][:, h * P:(h + 1) * P], src[q][:, h, :], ident[:])
                        ins.then_inc(sem("i_TT"), 1)
                transposed(0, U)
                for l in range(1, 7):
                    b = 2 ** l
                    for q in range(UNITS):
                        n = UNITS * (l - 1) + q
                        pe.wait_ge(*((sem("i_L0"), HG * l + q + 1) if q < HG else (sem("i_L1"), HG * l + q - HG + 1)))
                        pe.wait_ge(*((sem("i_U"), q + 1) if l == 1 else (sem("i_T"), n + 1 - UNITS)))
                        for h in range(4):
                            ins = pe.matmul(bank[q][:, h * 64:(h + 1) * 64].rearrange("p (i j) -> p i j", j=b),
                                            Lm[q][:, h, :], T[q][:, h, :].rearrange("p (i j) -> p i j", j=2 * b)[:, :, 0:b],
                                            start=True, stop=True)
                        ins.then_inc(sem("i_Y"), 1)
                    for q in range(UNITS):
                        n = UNITS * (l - 1) + q
                        pe.wait_ge(sem("i_Y_in"), n + 1)
                        if l > 1:
                            pe.wait_ge(sem("i_U"), UNITS * (l - 1) + q + 1)
                        for h in range(4):
                            y_, z_ = Y[q][:, h * 64:(h + 1) * 64], bank[q][:, 256 + h * 64:256 + (h + 1) * 64]
                            if l < 6:
                                ins = pe.matmul(z_, U[q][:, h, :], y_, start=True, stop=True)
                            else:
                                ins = pe.matmul(bank[4 + q][0:64, h * P:(h + 1) * P], y_, U[q][:, h, :], start=True, stop=True)
                        ins.then_inc(sem("i_Z"), 1)
                    if l < 6:
                        transposed(l, T)
                pe.wait_ge(sem("i_T"), UNITS * 6)
                for t in range(NT):
                    tok = slice(t * P, (t + 1) * P)
                    if t:
                        pe.wait_ge(sem("r_S_in"), HG)
                    for g in range(HG):
                        n = HG * t + g
                        cols = lambda h: slice((4 * g + h) * P, (4 * g + h + 1) * P)
                        if t:
                            for h in range(4):
                                ins = pe.matmul(bank[4 + g][:, h * P:(h + 1) * P], qkT[:, H2 + 4 * g + h, tok], S[:, 4 * g + h, :],
                                                start=True, stop=True)
                            ins.then_inc(sem("r_kS"), 1)
                            if g:
                                pe.wait_ge(sem("r_o1"), g)
                            for h in range(4):
                                ins = pe.matmul(bank[0][:, h * P:(h + 1) * P], qkT[:, 4 * g + h, tok], S[:, 4 * g + h, :],
                                                start=True, stop=True)
                            ins.then_inc(sem("r_qS"), 1)
                            pe.wait_ge(sem("r_r"), g + 1)
                        if n:
                            pe.wait_ge(sem("r_vn_in"), n)
                        for h in range(4):
                            ins = pe.matmul(bank[1][:, h * P:(h + 1) * P], U[n][:, h, :], r2[:, h, :] if t else bv[:, 0, cols(h)],
                                            start=True, stop=True)
                        ins.then_inc(sem("r_vn"), 1)
                        pe.wait_ge(sem("r_vn_in"), n + 1)
                        if n:
                            pe.wait_ge(*((sem("r_o1"), g) if t and g else (sem("r_o_in"), n)))
                        for h in range(4):
                            ins = pe.matmul(bank[2][:, h * P:(h + 1) * P], QK[n][:, h, :], vn[:, h, :], start=True, stop=True)
                        ins.then_inc(sem("r_o"), 1)
                        if t == 0:
                            pe.wait_ge(sem("r_vne"), g + 1)
                            if g:
                                pe.wait_ge(sem("r_S_in"), g)
                            for h in range(4):
                                ins = pe.matmul(bank[3][:, h * P:(h + 1) * P], knat[:, 4 * g + h, :], vne[:, h, :],
                                                start=True, stop=True)
                            ins.then_inc(sem("r_S"), 1)

            def gdn_ready(t):
                turn_T("gdn", t)
                turned("gdn", t)

            def p_turn(i):
                pe.wait_ge(sem("p_in"), 32 * (i + 1))
                for k in range(2):
                    for t in range(NT):
                        ins = pe.transpose(bank[6][:, k * SEQ + t * P:k * SEQ + (t + 1) * P], p_in[:, t, k * P:(k + 1) * P], ident[:])
                ins.then_inc(sem("p_T"), 1)

            def ple_product(i, between):
                s = first[f"ple_p{i}"]
                pe.wait_ge(sem("p_lo"), i + 1)
                pe.wait_ge(w_lo, s + 1)
                for t in range(NT):
                    if t:
                        between()
                        pe.wait_ge(sem("pp_in"), 2 * i + 1)
                    ins = rows(s, t, pT, 0, 2, [bank[6], bank[7]], True, True)
                    ins.then_inc(sem("pp_mm0") if t == 0 else w_used, 1)

            GATE_ORDER = [(0, 0), (1, 0), (0, 1), (2, 0), (3, 0), (1, 1), (2, 1), (3, 1)]

            def mixer3():
                s = first["kv"]

                def head_turn(i):
                    for t in range(NT):
                        pe.wait_ge(sem("s_rows"), 2 * i + t + 1)
                        for b in range(2):
                            if i == 0 and t == 0:
                                pe.wait_ge(sem("turn_lo"), 4 * turn("n8") + 4)
                            if 4 * i + 2 * t + b - 1 > 0:
                                pe.wait_ge(sem("s_kT_in"), 4 * i + 2 * t + b - 1)
                            for k in range(4):
                                ins = pe.transpose(bank[4 + b][:, k * P:(k + 1) * P], xs[:, t, (4 * b + k) * P:(4 * b + k + 1) * P],
                                                   ident[:])
                            ins.then_inc(sem("s_kT"), 1)

                def scores(heads):
                    for h in heads:
                        z = z_bank(h)
                        pe.matmul(z[:, 0:SEQ], skT[:, h, 0:P], sqT[:, h, :], start=True, stop=False, skip_group_check=True)
                        pe.matmul(z[:, SEQ:384], skT[:, h, P:], sqT[:, h, P:], start=False, stop=False, skip_group_check=True)\
                          .then_inc(sem("sb_z"), 1)

                def suffix(h):
                    z, sp_ = z_bank(h), sab[:, h, :]
                    pe.wait_ge(sem("sb_sp"), h + 1)
                    pe.matmul(z[:, 0:SEQ], neg_tri[:], sp_[:, 0:SEQ], start=False, stop=False, skip_group_check=True)
                    pe.matmul(z[:, P:SEQ], neg_one[:], sp_[:, SEQ:], start=False, stop=True, skip_group_check=True)
                    pe.matmul(z[:, SEQ:384], neg_tri[:], sp_[:, SEQ:], start=False, stop=False, skip_group_check=True)
                    pe.matmul(z[:, 0:P], ident[:], sbig[:], start=False, stop=True, skip_group_check=True)
                    pe.matmul(z[:, SEQ:384], ident[:], sbig[:], start=False, stop=True, skip_group_check=True)\
                      .then_inc(sem("sb_sfx"), 1)

                def output(h):
                    pe.wait_ge(sem("sb_w"), h + 1 + (h % 2 == 0))
                    o, c = z_bank(h - h % 2), (h % 2) * SEQ
                    v = [vs[:, t, h * P:(h + 1) * P] for t in range(NT)]
                    pe.matmul(o[:, c:c + P], sab[:, h, 0:P], v[0], start=True, stop=True)
                    pe.matmul(o[:, c + P:c + SEQ], sab[:, h, P:SEQ], v[0], start=True, stop=False)
                    pe.matmul(o[:, c + P:c + SEQ], sab[:, h, SEQ:], v[1], start=False, stop=True).then_inc(sem("sb_pv"), 1)

                block_rows(s, xT, [bank[0], bank[1]], k_ready=tile_ready("n7"), tilewise=True)
                block_rows(s + 2, xT, [bank[2], bank[3]])
                for t in range(NT):
                    turn_T("n8", t)
                pe.wait_ge(sem("s_kqv"), 1)
                pe.wait_ge(sem("turn_lo"), 4 * turn("n8") + 4)
                block_rows(s + 4, xT2, [bank[0], bank[1]])
                pe.wait_ge(sem("s_kqv"), 2)
                block_rows(s + 6, xT2, [bank[2], bank[3]])
                head_turn(0)
                pe.wait_ge(sem("s_kqv"), 3)
                block_rows(s + 8, xT, [bank[0], bank[1]])
                head_turn(1)
                pe.wait_ge(sem("s_kT_in"), 8)
                pe.wait_ge(sem("s_kqv"), 4)
                scores(range(6))
                pe.wait_ge(sem("s_kqv"), 5)
                block_rows(s + 10, xT, [bank[0], bank[1]])
                pe.wait_ge(sem("s_kqv"), 6)
                scores((6, 7))
                pe.wait_ge(sem("s_masks"), 1)
                for i in range(H2 + 2):
                    if i < H2:
                        suffix(i)
                    if i >= 2:
                        output(i - 2)
                for t in range(NT):
                    turn_T("sb", t, (sem("sb_o_in"), 4))

                def ready(i):
                    if i == 0:
                        for t in range(NT):
                            turned("sb", t)
                return ready

            def next_turn(name):
                return lambda: turn_T(name, 0)

            pe.wait_ge(sem("consts"), 1)
            turn_T("n0", 0)
            wide("down0", hT, ffn(0), next_turn("n1"))
            wide("mix_out", xT, mixer1(), next_turn("n2"), MIX_PAIRS)
            wide("down1", hT, ffn(1), next_turn("n4"))
            mixer2()
            wide("gdn_out", xT, None, next_turn("n5"), order=GATE_ORDER, k_ready=gdn_ready)
            wide("down2", hT, ffn(2), next_turn("n6"))
            wide("ple_g0", xT, None, next_turn("n7"), order=GATE_ORDER, k_ready=tile_ready("n6"))
            wide("sb_out", xT, mixer3(), next_turn("n9"))
            wide("down3", hT, ffn(3), next_turn("n10"))
            wide("ple_g1", xT, order=GATE_ORDER, k_ready=tile_ready("n10"))
_INS = ["x", "ffn1_norm", "ffn1_w13", "ffn1_w2", "mix_norm", "w_in", "conv_w", "conv_b", "conv_ln_g", "conv_ln_b",
    "forget_b", "out_norm_conv", "out_norm_attn", "w_out", "ffn2_norm", "ffn2_w13", "ffn2_w2", "final_norm",
    "p_2", "ln_mix_2", "ln_ffn_2", "ln_ple_2", "gdn_w_in_2", "gdn_conv_2", "gdn_a_log_2", "gdn_dt_bias_2",
    "gdn_norm_2", "gdn_w_out_2", "kv_norm_2", "w_kv_2", "k_norm_2", "sb_w_q_2", "sb_q_norm_2", "sb_w_out_2",
    "ffn_w_in_2", "ffn_w_out_2", "ple_w_proj_2", "ple_w_gate_2"]
def kernel(**inputs):
    import numpy as _np
    import concourse.bacc as _bacc
    from concourse import mybir as _mybir
    from concourse.bass_utils import run_bass_kernel_spmd as _run
    nc = _bacc.Bacc("TRN2", target_bir_lowering=False, num_devices=1)
    arrays, args = {}, {}
    for name in _INS:
        v = _np.ascontiguousarray(inputs[name])
        arrays[f"in_{name}_dram"] = v
        args[name] = nc.dram_tensor(f"in_{name}_dram", v.shape, _mybir.dt.from_np(v.dtype), kind="ExternalInput").ap()
    out = nc.dram_tensor("out_0_dram", (1, 256, 1024), _mybir.dt.float32, kind="ExternalOutput").ap()
    build_program(nc, args, out)
    r = _run(nc, [arrays], core_ids=[0])
    return r.results[0]["out_0_dram"]
```
